# Optimizing a Trainium2 kernel written in Bass

```python
import jax, jax.numpy as jnp
from jax import lax
import numpy as np

D_MODEL = 2048
BATCH = 1
SEQ = 512
DEPTH = 2
DEC_BATCH = 1
DEC_SEQ = 32
PAST_LEN = 256

CHUNK = 64
N_MIXERS = 2
N_HEADS = 16
HEAD_DIM = D_MODEL // N_HEADS
N_ATTN = (DEPTH + 1) // 2
N_HGRN = DEPTH // 2
Q_BLOCK = 128
SUB_CHUNK = 16
N_PROJ = 4
EPS = 1e-6
LB_FLOOR = 1e-30

kernel_name = 'stickbreak_hgrn2_streaming_step'

def rms_norm(x, w):
    xf = x.astype(jnp.float32)
    y = xf * lax.rsqrt(jnp.mean(xf * xf, axis=-1, keepdims=True) + EPS)
    return (y * w.astype(jnp.float32)).astype(x.dtype)

def stick_breaking_block(q, k, v, q_pos, k_pos):
    z = jnp.einsum('bqhd,bkhd->bhqk', q, k).astype(jnp.float32) * (HEAD_DIM ** -0.5)
    earlier = k_pos[None, :] < q_pos[:, None]
    log_one_minus = jnp.where(earlier, jax.nn.log_sigmoid(-z), 0.0)
    between = lax.cumsum(log_one_minus, axis=3, reverse=True) - log_one_minus
    w = jnp.where(earlier, jnp.exp(jnp.where(earlier, jax.nn.log_sigmoid(z) + between, 0.0)), 0.0)
    return jnp.einsum('bhqk,bkhd->bqhd', w.astype(v.dtype), v)

def stick_breaking(q, k, v, q_offset):
    tq = q.shape[1]
    outs = []
    for start in range(0, tq, Q_BLOCK):
        end = min(start + Q_BLOCK, tq)
        kend = q_offset + end
        outs.append(stick_breaking_block(q[:, start:end], k[:, :kend], v[:, :kend],
                                         jnp.arange(q_offset + start, q_offset + end), jnp.arange(kend)))
    return jnp.concatenate(outs, axis=1)

def hgrn2_chunk(S, inp):
    q, k, v, g = inp
    bn, h, c, dk = q.shape
    n = c // SUB_CHUNK
    b = jnp.cumsum(g, axis=2)
    o = jnp.einsum('bhtk,bhkv->bhtv', q * jnp.exp(b), S)
    qs = q.reshape(bn, h, n, SUB_CHUNK, dk)
    ks = k.reshape(bn, h, n, SUB_CHUNK, dk)
    bs = b.reshape(bn, h, n, SUB_CHUNK, dk)
    b_ref = jnp.concatenate([jnp.zeros_like(bs[:, :, :1, 0]), bs[:, :, :-1, -1]], axis=2)
    q_rel = qs * jnp.exp(jnp.minimum(bs - b_ref[:, :, :, None], 0.0))
    k_rel = ks[:, :, None] * jnp.exp(jnp.minimum(b_ref[:, :, :, None, None] - bs[:, :, None], 0.0))
    sub = jnp.arange(n)
    off_mask = (sub[None, :] < sub[:, None])[:, None, :, None]
    off = jnp.einsum('bhaik,bhacjk->bhaicj', q_rel, k_rel) * off_mask
    pos = jnp.arange(SUB_CHUNK)
    tri = pos[:, None] >= pos[None, :]
    decay = jnp.exp(jnp.minimum(bs[:, :, :, :, None] - bs[:, :, :, None, :], 0.0))
    diag = jnp.einsum('bhaik,bhajk,bhaijk->bhaij', qs, ks, decay) * tri
    scores = off + jnp.einsum('bhaij,ac->bhaicj', diag, jnp.eye(n, dtype=diag.dtype))
    o = o + jnp.einsum('bhts,bhsv->bhtv', scores.reshape(bn, h, c, c), v)
    b_last = b[:, :, -1]
    S_new = jnp.exp(b_last)[..., None] * S + jnp.einsum('bhsk,bhsv->bhkv', k * jnp.exp(jnp.minimum(b_last[:, :, None] - b, 0.0)), v)
    return S_new, o

def hgrn2(q, k, v, logf, S0):
    bn, t = q.shape[:2]
    nc = -(-t // CHUNK)
    pad = nc * CHUNK - t

    def prep(a):
        a = jnp.pad(a.astype(jnp.float32), ((0, 0), (0, pad), (0, 0), (0, 0)))
        return a.reshape(bn, nc, CHUNK, N_HEADS, HEAD_DIM).transpose(1, 0, 3, 2, 4)

    S, o = lax.scan(hgrn2_chunk, S0.astype(jnp.float32), (prep(q), prep(k), prep(v), prep(logf)))
    o = o.transpose(1, 0, 3, 2, 4).reshape(bn, nc * CHUNK, N_HEADS, HEAD_DIM)[:, :t]
    return o, S

def attn_mixer(h, w_in, q_w, k_w, past_k, past_v):
    bn, t = h.shape[:2]
    qa, ka, va, g = jnp.split(h @ w_in, N_PROJ, axis=-1)
    q = rms_norm(qa.reshape(bn, t, N_HEADS, HEAD_DIM), q_w)
    k = rms_norm(ka.reshape(bn, t, N_HEADS, HEAD_DIM), k_w)
    v = va.reshape(bn, t, N_HEADS, HEAD_DIM)
    if past_k is None:
        kk, vv, off = k, v, 0
    else:
        kk = jnp.concatenate([past_k.astype(k.dtype), k], axis=1)
        vv = jnp.concatenate([past_v.astype(v.dtype), v], axis=1)
        off = past_k.shape[1]
    o = stick_breaking(q, kk, vv, off).reshape(bn, t, D_MODEL)
    return o * jax.nn.silu(g), k, v

def hgrn_mixer(h, w_in, lb, out_w, S0):
    bn, t = h.shape[:2]
    qa, fa, ia, g = jnp.split(h @ w_in, N_PROJ, axis=-1)
    f32 = fa.astype(jnp.float32)
    logf = jnp.logaddexp(jnp.log(jnp.maximum(lb, LB_FLOOR)), jnp.log1p(-lb) + jax.nn.log_sigmoid(f32))
    logf = jnp.minimum(logf, 0.0)
    kk = (1.0 - lb) * jax.nn.sigmoid(-f32)
    heads = lambda a: a.reshape(bn, t, N_HEADS, HEAD_DIM)
    o, S = hgrn2(heads(jax.nn.silu(qa)), heads(kk), heads(ia), heads(logf), S0)
    o = rms_norm(o, out_w).reshape(bn, t, D_MODEL).astype(h.dtype)
    return o * jax.nn.silu(g), S

def setup_inputs(seed: int = 0) -> dict:
    key = jax.random.key(seed)
    ks = jax.random.split(key, 13)
    nrm = jax.random.normal
    scale = D_MODEL ** -0.5
    return {
        'x_prompt': nrm(ks[0], (BATCH, SEQ, D_MODEL), jnp.float32),
        'x_sample': nrm(ks[1], (DEC_BATCH, DEC_SEQ, D_MODEL), jnp.float32),
        'cache_k': nrm(ks[2], (N_ATTN, DEC_BATCH, PAST_LEN, N_HEADS, HEAD_DIM), jnp.float32),
        'cache_v': nrm(ks[3], (N_ATTN, DEC_BATCH, PAST_LEN, N_HEADS, HEAD_DIM), jnp.float32),
        'state_hgrn': 0.5 * nrm(ks[4], (N_HGRN, DEC_BATCH, N_HEADS, HEAD_DIM, HEAD_DIM), jnp.float32),
        'norm_w': 1.0 + 0.02 * nrm(ks[5], (DEPTH, D_MODEL), jnp.float32),
        'w_in': scale * nrm(ks[6], (DEPTH, D_MODEL, N_PROJ * D_MODEL), jnp.float32),
        'w_out': scale * nrm(ks[7], (DEPTH, D_MODEL, D_MODEL), jnp.float32),
        'q_norm_w': 1.0 + 0.02 * nrm(ks[8], (N_ATTN, HEAD_DIM), jnp.float32),
        'k_norm_w': 1.0 + 0.02 * nrm(ks[9], (N_ATTN, HEAD_DIM), jnp.float32),
        'hgrn_norm_w': 1.0 + 0.02 * nrm(ks[10], (N_HGRN, HEAD_DIM), jnp.float32),
        'hgrn_lb': 0.5 * nrm(ks[11], (N_HGRN, D_MODEL), jnp.float32),
    }

def reference(x_prompt, x_sample, cache_k, cache_v, state_hgrn, norm_w, w_in, w_out,
              q_norm_w, k_norm_w, hgrn_norm_w, hgrn_lb):
    lb_sm = jax.nn.softmax(hgrn_lb.astype(jnp.float32), axis=0)
    lbs = jnp.clip(jnp.cumsum(lb_sm, axis=0) - lb_sm[0], 0.0, 1.0 - 1e-6)
    xp, xs = x_prompt, x_sample
    kp, vp, sp, ksm, vsm, ssm = [], [], [], [], [], []
    for layer in range(DEPTH):
        j = layer // N_MIXERS
        hp = rms_norm(xp, norm_w[layer])
        hs = rms_norm(xs, norm_w[layer])
        if layer % N_MIXERS == 0:
            op, k1, v1 = attn_mixer(hp, w_in[layer], q_norm_w[j], k_norm_w[j], None, None)
            osm, k2, v2 = attn_mixer(hs, w_in[layer], q_norm_w[j], k_norm_w[j], cache_k[j], cache_v[j])
            kp.append(k1); vp.append(v1); ksm.append(k2); vsm.append(v2)
        else:
            s0 = jnp.zeros((xp.shape[0], N_HEADS, HEAD_DIM, HEAD_DIM), jnp.float32)
            op, s1 = hgrn_mixer(hp, w_in[layer], lbs[j], hgrn_norm_w[j], s0)
            osm, s2 = hgrn_mixer(hs, w_in[layer], lbs[j], hgrn_norm_w[j], state_hgrn[j])
            sp.append(s1); ssm.append(s2)
        xp = xp + op @ w_out[layer]
        xs = xs + osm @ w_out[layer]
    return (xp, xs, jnp.stack(kp), jnp.stack(vp), jnp.stack(sp), jnp.stack(ksm), jnp.stack(vsm), jnp.stack(ssm))


_drawn_inputs = setup_inputs


def setup_inputs(seed=0):
    import zlib

    import numpy as np

    out = dict(_drawn_inputs(seed))
    spreads = {}
    factors = {'state_hgrn': 3.916, 'q_norm_w': 22.056, 'hgrn_norm_w': 5.002}
    for name, (base, spread) in spreads.items():
        noise = np.random.default_rng([zlib.crc32(name.encode()), seed]).standard_normal(out[name].shape)
        drawn = base * np.exp(spread * noise) if base else spread * noise
        out[name] = __import__('jax').numpy.asarray(drawn.astype(out[name].dtype))
    for name, factor in factors.items():
        out[name] = (out[name] * factor).astype(out[name].dtype)
    return out
```

```python
from contextlib import ExitStack

import concourse.bass as bass
from concourse import mybir

F32 = mybir.dt.float32
F32R = mybir.dt.float32r
BF16 = mybir.dt.bfloat16
I32 = mybir.dt.int32
ALU = mybir.AluOpType
ACT = mybir.ActivationFunctionType

P = 128
D = 2048
KT = D // P
H = 16
SEQ, SAMPLE, PAST = 512, 32, 256
T = SEQ + SAMPLE
HT = T // 2
NB = SEQ // P
LAST = T - P
SROW = P - SAMPLE
EPS = 1e-6
MASKED = -1e30
LB_FLOOR = 1e-30
LB_TOP = 1.0 - 1e-6
TWO60 = float(2.0 ** 60)
LN_TWO60 = 41.58883083359672

KH = KT // 2
RING = 4
AHEAD = 3
HEAD_HALVES = 8
IN_HALVES = H * HEAD_HALVES
OUT_HALVES = KT * 2
LAYER_HALVES = IN_HALVES + OUT_HALVES
ALL_HALVES = 2 * LAYER_HALVES
LAYER_TILES = LAYER_HALVES // 2

Z_COL = [0, 512, 896, 1152]
Z_LEN = [512, 384, 256, 128]
Z_PAST0, Z_PAST1, Z_NEW = 1280, 1312, 1344
Z_ALL = 1376
LEVELS = [64, 32, 16, 8, 4, 2, 1]
MASK_COL = {m: 64 * i for i, m in enumerate(LEVELS)}


class Chain:

    def __init__(self, eng, sem):
        self.eng, self.sem, self.base, self.n = eng, sem, 0, 0

    def done(self, ins):
        ins.then_inc(self.sem, 1)
        self.n += 1
        return self.n

    def wait(self, mark=None):
        self.eng.wait_ge(self.sem, self.base + (self.n if mark is None else mark))

    def enter(self, i, first, per):
        self.outer, self.first, self.per = self.base + self.n, first, per
        self.base, self.n = i * per + self.outer, 0

    def leave(self, times):
        assert self.n == self.per, (self.n, self.per)
        self.base, self.n = self.outer + self.per * times, 0


def encoder_step(nc, x_prompt, x_sample, cache_k, cache_v, state_hgrn, norm_w, w_in, w_out, q_norm_w, k_norm_w,
                 hgrn_norm_w, hgrn_lb, y_prompt, y_sample, k_prompt, v_prompt, s_prompt, k_sample, v_sample,
                 s_sample):
    x_residual = nc.dram_tensor("x_residual", (KT, P, T), F32, kind="Internal").ap()

    with ExitStack() as ctx:
        def sb(name, shape, dt=F32):
            return ctx.enter_context(nc.sbuf_tensor(name, shape, dt))

        def sem(name):
            return ctx.enter_context(nc.semaphore(name))

        act_hi = sb("act_hi", [P, KT, T], F32R)
        act_lo = sb("act_lo", [P, KT, T], F32R)
        full = sb("full", [P, KT, T])
        w_raw = sb("w_raw", [P, RING, KH, P])
        w_hi = sb("w_hi", [P, RING, KH, P], F32R)
        w_lo = sb("w_lo", [P, RING, KH, P], F32R)
        Y = sb("Y", [P, 4, T])
        rstd_x = sb("rstd_x", [P, T])
        ident = sb("ident", [P, P])
        ident_b = sb("ident_b", [P, P], BF16)
        neg_tri = sb("neg_tri", [P, P])
        ones = sb("ones", [P, P])
        neg_ones = sb("neg_ones", [P, P])
        hide = sb("hide", [P, P], BF16)
        hide_last = sb("hide_last", [P, SAMPLE], BF16)
        level_mask = sb("level_mask", [P, 64 * len(LEVELS)])
        run_on = sb("run_on", [P, T])
        vec_rows = sb("vec_rows", [51, P])
        vecs = sb("vecs", [P, 51])
        small = sb("small", [P, 8, KT])
        eps = sb("eps", [P, 1])
        one_c = sb("one_c", [P, 1])
        WORK = 10000
        work = sb("work", [P, WORK])

        psum = ctx.enter_context(nc.psum_tensor("psum", [P, 8, 512], F32))
        acc = [psum[:, 0:2, 0:HT], psum[:, 2:4, 0:HT]]
        M = [psum[:, 4 + i, :] for i in range(4)]
        M01 = psum[:, 4:6, :]

        NORM = [vecs[:, 0:KT], vecs[:, KT:2 * KT]]
        LB_RAW = vecs[:, 32:48]
        WQ, WK, WO = vecs[:, 48:49], vecs[:, 49:50], vecs[:, 50:51]
        LB, ONE_LB, LOG_A, LOG_BA = small[:, 0], small[:, 1], small[:, 2], small[:, 3]
        LB_E, LB_T, LB_R, LB_Q = small[:, 4], small[:, 5], small[:, 6], small[:, 7]
        WQS = small[:, 7, 1:2]

        class Carve:
            def __init__(self):
                self.at = 0

            def __call__(self, n):
                v = work[:, self.at:self.at + n]
                self.at += n
                assert self.at <= WORK, self.at
                return v

        c = Carve()
        qk_sq = c(2 * T).rearrange("p (b t) -> p b t", b=2)
        qn, kn = c(T), c(T)
        gate = g_tmp = c(T)
        za = c(Z_ALL)
        sp = c(Z_ALL)
        v_nat = c(5 * P).rearrange("p (b d) -> p b d", b=5)
        k_nat = c(5 * P).rearrange("p (b d) -> p b d", b=5)
        past_kT = c(PAST)
        past_k = c(PAST).rearrange("p (b d) -> p b d", b=2)
        past_v = c(PAST).rearrange("p (b d) -> p b d", b=2)
        c = Carve()
        r_tmp = c(2 * T).rearrange("p (b t) -> p b t", b=2)
        lse = c(T)
        cum = c(T)
        qs, kk, qe, kd = c(T), c(T), c(T), c(T)
        eb = c(T)
        gate_r = g_tmp_r = c(T)
        dl = [c(T) for _ in range(1)]
        xl = [c(T) for _ in range(2)]
        A = c(SEQ + SAMPLE)
        v_nat_r = c(5 * P).rearrange("p (b d) -> p b d", b=5)
        kd_nat = c(5 * P).rearrange("p (b d) -> p b d", b=5)
        S = c(6 * P).rearrange("p (b d) -> p b d", b=6)
        o_cp, o_sq = r_tmp[:, 0], r_tmp[:, 1]
        c = Carve()
        x_old = [c(T) for _ in range(2)]
        x_new = [c(T) for _ in range(2)]
        x_sq = c(T)
        sq_sum = c(T)
        y_nat = [c(5 * P).rearrange("p (b d) -> p b d", b=5) for _ in range(2)]
        x_tmp = [c(T) for _ in range(2)]
        x_nat_s = c(D)[0:SAMPLE]
        x_nat = full[:, :, :].rearrange("p a b -> p (a b)")

        x_loaded = sem("x_loaded"); vec_loaded = sem("vec_loaded")
        consts_ready = sem("consts_ready"); pool_chain = sem("pool_chain")
        act_chain = sem("act_chain"); dve_chain = sem("dve_chain")
        raw_loaded = [sem(f"raw_loaded{i}") for i in range(RING)]
        hi_ready = sem("hi_ready"); lo_ready = sem("lo_ready"); half_done = sem("half_done")
        evacuated = sem("evacuated")
        vecs_turned = sem("vecs_turned"); vecs_ready = sem("vecs_ready")
        x_turned = sem("x_turned"); x_copied = sem("x_copied"); x_scaled = sem("x_scaled")
        x_squared = sem("x_squared"); x_summed = sem("x_summed"); x_stored = [sem("x_stored0"), sem("x_stored1")]
        x_old_loaded = [sem("x_old_loaded0"), sem("x_old_loaded1")]
        rms_summed = sem("rms_summed"); rstd_ready = sem("rstd_ready")
        act_hi_ready = sem("act_hi_ready"); act_lo_ready = sem("act_lo_ready")
        full_ready = sem("full_ready")
        qk_squared = sem("qk_squared"); stage_a = sem("att_sums_and_turns"); qk_rstd = sem("qk_rstd")
        v_copied = sem("v_copied"); past_copied = sem("past_copied")
        qk_normed = sem("qk_normed"); stage_b = sem("att_scores"); k_copied = sem("k_copied")
        soft_log = sem("soft_log"); sp_ready = sem("sp_ready"); stage_c = sem("att_cumulated")
        k_last_copied = sem("k_last_copied"); weights_ready = sem("weights_ready"); stage_d = sem("att_mixed")
        gate_ls = sem("gate_ls"); gate_log = sem("gate_log"); gate_sig = sem("gate_sig"); gate_ready = sem("gate_ready")
        o_ready = sem("o_ready")
        past_k_loaded = sem("past_k_loaded"); past_v_loaded = sem("past_v_loaded")
        v_stored = sem("v_stored"); k_stored = sem("k_stored")
        r_log = sem("r_log"); r_ls = sem("r_ls"); r_lse = sem("r_lse"); r_kx = sem("r_kx"); r_cum = sem("r_cum")
        r_sig = sem("r_sig"); r_kexp = sem("r_kexp"); r_qk = sem("r_qk"); r_eb = sem("r_eb")
        r_kdx = sem("r_kdx"); r_kde = sem("r_kde"); r_kd = sem("r_kd")
        r_vT = sem("r_v_turned"); r_v = sem("r_v_copied"); r_kdT = sem("r_kd_turned"); r_kdn = sem("r_kd_copied")
        r_diff = sem("r_diff"); r_dexp = sem("r_dexp"); r_x = sem("r_x"); r_lev = sem("r_level_scores")
        r_put = sem("r_scores_put")
        r_diag_put = sem("r_diag_put")
        r_upd = sem("r_update"); r_state = sem("r_state")
        r_gls = sem("r_gate_ls"); r_glog = sem("r_gate_log"); r_gsig = sem("r_gate_sig"); r_gate = sem("r_gate")
        r_out = sem("r_out"); r_ocp = sem("r_out_copied"); r_ssq = sem("r_out_sum"); r_orstd = sem("r_out_rstd")
        s_loaded = sem("s_loaded"); s_stored = sem("s_stored")
        y_turned = sem("y_turned"); y_copied = sem("y_copied"); y_stored = [sem("y_stored0"), sem("y_stored1")]

        NL = len(LEVELS)

        def added(l, n):
            return n + (l * LAYER_TILES + 4 * H + 1)

        block = ctx.enter_context(nc.Block())

        w_in_v = [w_in[l].rearrange("(kh kt p) c -> kh p kt c", p=P, kt=KH) for l in range(2)]
        w_out_v = [w_out[l].rearrange("(kh kt p) c -> kh p kt c", p=P, kt=KH) for l in range(2)]
        k_prompt_v = k_prompt[0, 0].rearrange("(b p) h d -> p b h d", p=P)
        v_prompt_v = v_prompt[0, 0].rearrange("(b p) h d -> p b h d", p=P)
        past_k_v = cache_k[0, 0].rearrange("(b p) h d -> p b h d", p=P)
        past_v_v = cache_v[0, 0].rearrange("(b p) h d -> p b h d", p=P)
        y_prompt_v = y_prompt[0].rearrange("(b p) c -> p b c", p=P)

        @block.sync
        def _(sp_eng):
            xp = x_prompt[0].rearrange("(b p) c -> b p c", p=P)
            sp_eng.dma_start(vec_rows[0:32, :], norm_w.rearrange("l (k p) -> (l k) p", p=P)).then_inc(vec_loaded, 16)
            sp_eng.dma_start(vec_rows[32:48, :], hgrn_lb.rearrange("l (k p) -> (l k) p", p=P)).then_inc(vec_loaded, 16)
            sp_eng.dma_start(vec_rows[48:49, :], q_norm_w).then_inc(vec_loaded, 16)
            sp_eng.dma_start(vec_rows[49:50, :], k_norm_w).then_inc(vec_loaded, 16)
            sp_eng.dma_start(vec_rows[50:51, :], hgrn_norm_w).then_inc(vec_loaded, 16)
            for b in range(NB):
                sp_eng.dma_start(x_nat[:, b * D:(b + 1) * D], xp[b]).then_inc(x_loaded, 16)
            sp_eng.dma_start(x_nat_s, x_sample[0]).then_inc(x_loaded, 16)

            def half(g, slot, src):
                if not (isinstance(g, int) and g < RING):
                    sp_eng.wait_ge(lo_ready, g - RING + 1)
                sp_eng.dma_start(w_raw[:, slot], src).then_inc(raw_loaded[slot], 16)

            def in_halves(l, h):
                for u in range(HEAD_HALVES):
                    g = h * HEAD_HALVES + (l * LAYER_HALVES + u)
                    half(g, u % RING, w_in_v[l][u % 2][:, :, bass.ds(h * P + (u // 2) * D, P)])

            for l in range(2):
                in_halves(l, 0)
                with sp_eng.Fori(1, H) as h:
                    in_halves(l, h)
                if l == 1:
                    pass
                out0 = l * LAYER_HALVES + IN_HALVES

                def out_pair(i, first, last):
                    for u in range(4):
                        half(i * 4 + (out0 + u), u, w_out_v[l][u % 2][:, :, bass.ds(i * (2 * P) + (u // 2) * P, P)])
                    for par in range(2):
                        if first:
                            if par == 0:
                                sp_eng.wait_ge(o_ready, (l + 1) * H)
                            n = (KT // 2) * (l + 1) * 16
                            sp_eng.wait_ge(x_stored[0], n)
                            sp_eng.wait_ge(x_stored[1], n)
                        else:
                            sp_eng.wait_ge(evacuated, added(l, i * 2 + (par - 2)))
                        sp_eng.dma_start(x_old[par], x_residual[bass.ds(i * 2 + par, 1)].rearrange("a p t -> (a p) t")
                                         ).then_inc(x_old_loaded[par], 16)
                out_pair(0, True, False)
                with sp_eng.Fori(1, KT // 2) as i:
                    out_pair(i, False, False)
            sp_eng.wait_ge(v_stored, 32 * H)
            sp_eng.wait_ge(k_stored, 32 * H)
            sp_eng.wait_ge(s_stored, 32 * H)
            for par in range(2):
                sp_eng.wait_ge(y_stored[par], 32 * (KT // 2))
                sp_eng.wait_ge(x_stored[par], 16 * KT)

        @block.gpsimd
        def _(pool):
            ch = Chain(pool, pool_chain)
            ch.done(pool.memset(ones[:], 1.0))
            ch.done(pool.memset(neg_ones[:], -1.0))
            ch.done(pool.memset(ident[:], 0.0))
            ch.done(pool.memset(hide[:], 0.0))
            ch.done(pool.memset(hide_last[:], 0.0))
            ch.done(pool.memset(level_mask[:], 1.0))
            ch.done(pool.memset(run_on[:], 1.0))
            ch.done(pool.memset(eps[:], EPS))
            ch.done(pool.memset(one_c[:], 1.0))
            ch.done(pool.memset(sq_sum, 0.0))
            ch.wait()
            ch.done(pool.memset(run_on[:, 0:T:P], 0.0))
            ch.done(pool.affine_select(out=ident[:], in_=ident[:], pattern=[[-1, P]], base=0, channel_multiplier=1,
                                       compare_op=ALU.not_equal, fill=1.0))
            ch.done(pool.affine_select(out=neg_tri[:], in_=neg_ones[:], pattern=[[-1, P]], base=0,
                                       channel_multiplier=1, compare_op=ALU.is_ge, fill=0.0))
            ch.done(pool.affine_select(out=hide[:], in_=hide[:], pattern=[[1, P]], base=0, channel_multiplier=-1,
                                       compare_op=ALU.is_gt, fill=MASKED))
            ch.done(pool.affine_select(out=hide_last[:], in_=hide_last[:], pattern=[[0, SAMPLE]], base=-SROW,
                                       channel_multiplier=1, compare_op=ALU.is_ge, fill=MASKED))
            ch.wait()
            ch.done(pool.affine_select(out=hide_last[:], in_=hide_last[:], pattern=[[1, SAMPLE]], base=SROW,
                                       channel_multiplier=-1, compare_op=ALU.is_gt, fill=MASKED))
            for m in LEVELS:
                v = level_mask[:, MASK_COL[m]:MASK_COL[m] + 64].rearrange("p (b j) -> p b j", j=m)
                ch.done(pool.affine_select(out=v, in_=v, pattern=[[-2 * m, 64 // m], [0, m]], base=0,
                                           channel_multiplier=1, compare_op=ALU.is_ge, fill=0.0))
                ch.wait()
                ch.done(pool.affine_select(out=v, in_=v, pattern=[[2 * m, 64 // m], [0, m]], base=m - 1,
                                           channel_multiplier=-1, compare_op=ALU.is_ge, fill=0.0))
                ch.wait()
            pool.tensor_copy(ident_b[:], ident[:]).then_inc(consts_ready, 1)

            def add_squares(n):
                pool.wait_ge(x_squared, n + 1)
                if not (isinstance(n, int) and n == 0):
                    pool.wait_ge(x_summed, n)
                pool.tensor_tensor(sq_sum, sq_sum, x_sq, ALU.add).then_inc(x_summed, 1)

            for n in range(KT):
                add_squares(n)
            pool.wait_ge(o_ready, H)
            pool.memset(sq_sum, 0.0).then_inc(pool_chain, 1)
            ch.n += 1
            ch.wait()
            with pool.Fori(0, KT) as i:
                add_squares(i + KT)

        @block.tensor
        def _(pe):
            def turn(out, in_, n=P, **kw):
                return pe.matmul(out, in_, ident[0:n, 0:n], is_transpose=True, start=True, stop=True, **kw)

            def half(g, slot, t, par, kh, wait_act=None):
                pe.wait_ge(lo_ready, g + 1)
                if kh == 0 and not (isinstance(t, int) and t < 2):
                    pe.wait_ge(evacuated, t - 1)
                for kt in range(KH):
                    k = kh * KH + kt
                    if wait_act is not None:
                        pe.wait_ge(act_lo_ready, wait_act + k + 1)
                    for n, (w, a) in enumerate(((w_hi, act_hi), (w_hi, act_lo), (w_lo, act_hi))):
                        for j in range(2):
                            mm = pe.matmul(acc[par][:, j, :], w[:, slot, kt, :], a[:, k, j * HT:(j + 1) * HT],
                                           start=(k == 0 and n == 0), stop=(k == KT - 1 and n == 2))
                mm.then_inc(half_done, 1)

            def in_half(l, h, u, wait_act=None):
                half(h * HEAD_HALVES + (l * LAYER_HALVES + u), u % RING, h * 4 + (l * LAYER_TILES + u // 2),
                     (u // 2) % 2, u % 2, wait_act)

            def att_sums_and_turns(h):
                pe.wait_ge(qk_squared, h + 1)
                pe.wait_ge(evacuated, h * 4 + 3)
                pe.wait_ge(past_k_loaded, (h + 1) * 16)
                if not (isinstance(h, int) and h == 0):
                    pe.wait_ge(o_ready, h)
                for b in range(2):
                    pe.matmul(M[b], ones[:], qk_sq[:, b, 0:SEQ], start=True, stop=True)
                for b in range(2):
                    pe.matmul(M[2][:, b * SAMPLE:(b + 1) * SAMPLE], ones[:], qk_sq[:, b, SEQ:T], start=True, stop=True)
                turn(M[2][:, 64:192], Y[:, 2, LAST:T])
                for b in range(2):
                    turn(M[2][:, 192 + b * P:192 + (b + 1) * P], past_k[:, b, :])
                for b in range(NB):
                    mm = turn(M[3][:, b * P:(b + 1) * P], Y[:, 2, b * P:(b + 1) * P])
                mm.then_inc(stage_a, 1)

            def att_scores(h):
                pe.wait_ge(qk_normed, h + 1)
                pe.wait_ge(v_copied, h + 1)
                pe.wait_ge(past_copied, h + 1)
                for b in range(NB):
                    out = M[b] if b < 3 else M[2]
                    at = 256 if b == 3 else 0
                    pe.matmul(out[:, at:at + Z_LEN[b]], kn[:, b * P:(b + 1) * P], qn[:, b * P:SEQ],
                              start=(b < 3), stop=False, skip_group_check=True)
                    pe.matmul(out[:, at:at + P], ident_b[:], hide[:], start=False, stop=True, skip_group_check=True)
                for b in range(2):
                    pe.matmul(M[2][:, 384 + b * SAMPLE:384 + (b + 1) * SAMPLE], past_kT[:, b * P:(b + 1) * P],
                              qn[:, SEQ:T], start=False, stop=True, skip_group_check=True)
                pe.matmul(M[2][:, 448:480], kn[:, LAST:T], qn[:, SEQ:T], start=False, stop=False,
                          skip_group_check=True)
                pe.matmul(M[2][:, 448:480], ident_b[:], hide_last[:], start=False, stop=True, skip_group_check=True)
                for b in range(NB):
                    mm = turn(M[3][:, b * P:(b + 1) * P], kn[:, b * P:(b + 1) * P])
                mm.then_inc(stage_b, 1)

            def att_cumulated(h):
                pe.wait_ge(sp_ready, h + 1)
                pe.wait_ge(k_copied, h + 1)
                turn(M[3][:, 0:P], kn[:, LAST:T])
                for b in range(NB):
                    out = M[b] if b < 3 else M[2]
                    at = 256 if b == 3 else 0
                    pe.matmul(out[:, at:at + Z_LEN[b]], neg_tri[:], sp[:, Z_COL[b]:Z_COL[b] + Z_LEN[b]],
                              start=False, stop=True, skip_group_check=True)
                    for later in range(b + 1, NB):
                        pe.matmul(out[:, at + (later - b) * P:at + Z_LEN[b]], neg_ones[:],
                                  sp[:, Z_COL[later]:Z_COL[later] + Z_LEN[later]], start=False, stop=True,
                                  skip_group_check=True)
                cols = [Z_PAST0, Z_PAST1, Z_NEW]
                for b in range(3):
                    for later in range(b, 3):
                        mm = pe.matmul(M[2][:, 384 + b * SAMPLE:384 + (b + 1) * SAMPLE],
                                       neg_tri[:] if later == b else neg_ones[:],
                                       sp[:, cols[later]:cols[later] + SAMPLE], start=False, stop=True,
                                       skip_group_check=True)
                mm.then_inc(stage_c, 1)

            def att_mixed(h):
                pe.wait_ge(weights_ready, h + 1)
                pe.wait_ge(k_last_copied, h + 1)
                pe.wait_ge(past_v_loaded, (h + 1) * 16)
                for b in range(NB):
                    pe.matmul(M[3][:, b * P:SEQ], v_nat[:, b, :], za[:, Z_COL[b]:Z_COL[b] + Z_LEN[b]],
                              start=(b == 0), stop=(b == NB - 1), skip_group_check=True)
                out = M[1][:, 384:384 + SAMPLE]
                pe.matmul(out, past_v[:, 0, :], za[:, Z_PAST0:Z_PAST0 + SAMPLE], start=True, stop=False)
                pe.matmul(out, past_v[:, 1, :], za[:, Z_PAST1:Z_PAST1 + SAMPLE], start=False, stop=False)
                pe.matmul(out, v_nat[:, 4, :], za[:, Z_NEW:Z_NEW + SAMPLE], start=False, stop=True).then_inc(stage_d, 1)

            def rec_turn_v(h):
                pe.wait_ge(evacuated, h * 4 + (LAYER_TILES + 3))
                if not (isinstance(h, int) and h == 0):
                    pe.wait_ge(r_ocp, h)
                for b in range(NB):
                    turn(M[3][:, b * P:(b + 1) * P], Y[:, 2, b * P:(b + 1) * P])
                turn(M[2][:, 0:P], Y[:, 2, LAST:T]).then_inc(r_vT, 1)

            def rec_level(h, i, bank):
                m = LEVELS[i]
                pe.wait_ge(r_x, h * NL + (i + 1))
                x = xl[i % 2]
                for b in range(NB):
                    rhs = x[:, b * P:(b + 1) * P].rearrange("p (b j) -> p b j", j=2 * m)[:, :, m:2 * m]
                    mm = pe.matmul(M[bank][:, b * 64:(b + 1) * 64], x[:, b * P:(b + 1) * P], rhs,
                                   start=True, stop=True)
                if m <= SAMPLE // 2:
                    rhs = x[:, SEQ:T].rearrange("p (b j) -> p b j", j=2 * m)[:, :, m:2 * m]
                    mm = pe.matmul(M[bank][:, 256:256 + SAMPLE // 2], x[:, LAST:T], rhs, start=True, stop=True)
                mm.then_inc(r_lev, 1)

            def rec_stage(h, u):
                if u == 1:
                    pe.wait_ge(r_qk, h + 1)
                    if not (isinstance(h, int) and h == 0):
                        pe.wait_ge(r_orstd, h)
                    for b in range(NB):
                        pe.matmul(M[0][:, b * P:(b + 1) * P], kk[:, b * P:(b + 1) * P], qs[:, b * P:(b + 1) * P],
                                  start=True, stop=True)
                    pe.wait_ge(r_v, h + 1)
                    pe.matmul(M[2][:, P:P + SAMPLE], kk[:, LAST:T], qs[:, SEQ:T], start=True, stop=True)
                    pe.wait_ge(r_kd, h + 1)
                    for b in range(NB):
                        turn(M[3][:, b * P:(b + 1) * P], kd[:, b * P:(b + 1) * P])
                    turn(M[2][:, 0:P], kd[:, LAST:T]).then_inc(r_kdT, 1)
                    rec_level(h, 0, 1)
                elif u == 2:
                    pe.wait_ge(r_diag_put, h + 1)
                    rec_level(h, 1, 0)
                    pe.wait_ge(r_kdn, h + 1)
                    for b in range(NB):
                        pe.matmul(M[3][:, b * P:(b + 1) * P], kd_nat[:, b, :], v_nat_r[:, b, :], start=True, stop=True)
                    pe.matmul(M[2][:, 0:P], kd_nat[SROW:P, 4, :], v_nat_r[SROW:P, 4, :], start=True, stop=True
                              ).then_inc(r_upd, 1)
                elif u == 3:
                    pe.wait_ge(r_put, h * NL + 1)
                    rec_level(h, 2, 1)
                    pe.wait_ge(r_put, h * NL + 2)
                    rec_level(h, 3, 0)
                elif u == 4:
                    pe.wait_ge(r_put, h * NL + 3)
                    rec_level(h, 4, 1)
                    pe.wait_ge(r_put, h * NL + 4)
                    rec_level(h, 5, 0)
                elif u == 5:
                    pe.wait_ge(r_put, h * NL + 5)
                    rec_level(h, 6, 1)
                elif u == 6:
                    pe.wait_ge(r_put, h * NL + 7)
                    pe.wait_ge(r_state, h + 1)
                    for b in range(NB):
                        out = M[3][:, b * P:(b + 1) * P]
                        pe.matmul(out, v_nat_r[:, b, :], A[:, b * P:(b + 1) * P], start=True, stop=(b == 0))
                        if b:
                            pe.matmul(out, S[:, b, :], qe[:, b * P:(b + 1) * P], start=False, stop=True)
                    out = M[2][:, 0:SAMPLE]
                    pe.matmul(out, v_nat_r[:, 4, :], A[:, SEQ:T], start=True, stop=False)
                    pe.matmul(out, S[:, 0, :], qe[:, SEQ:T], start=False, stop=True).then_inc(r_out, 1)
                elif u == 7:
                    pe.wait_ge(r_ocp, h + 1)
                    pe.matmul(M[0], ones[:], o_sq[:, 0:SEQ], start=True, stop=True)
                    pe.matmul(M[1][:, 0:SAMPLE], ones[:], o_sq[:, SEQ:T], start=True, stop=True).then_inc(r_ssq, 1)

            def mixer_stage(l, h, u):
                if l == 0:
                    if u == 1:
                        att_scores(h)
                    elif u == 3:
                        att_cumulated(h)
                    elif u == 5:
                        att_mixed(h)
                else:
                    rec_stage(h, u)

            def first_stage(l, h):
                if l == 0:
                    att_sums_and_turns(h)
                else:
                    rec_turn_v(h)

            pe.wait_ge(consts_ready, 1)
            pe.wait_ge(vec_loaded, 16 * 5)
            turn(M[0][:, 0:51], vec_rows[:, :], n=51).then_inc(vecs_turned, 1)
            pe.wait_ge(vecs_ready, 1)
            pe.wait_ge(x_loaded, 16 * 5)
            for k in range(KT):
                if k >= 2:
                    pe.wait_ge(x_scaled, k - 1)
                    pe.wait_ge(x_copied, k - 1)
                for b in range(NB):
                    turn(psum[:, 4 + 2 * (k % 2), b * P:(b + 1) * P], x_nat[:, b * D + k * P:b * D + (k + 1) * P])
                turn(psum[:, 5 + 2 * (k % 2), 0:SAMPLE], x_nat_s[:, k * P:(k + 1) * P], n=SAMPLE).then_inc(x_turned, 1)

            def rms_sum(l):
                pe.wait_ge(x_summed, (l + 1) * KT)
                pe.matmul(M[0], ones[:], sq_sum[:, 0:SEQ], start=True, stop=True)
                pe.matmul(M[1][:, 0:SAMPLE], ones[:], sq_sum[:, SEQ:T], start=True, stop=True).then_inc(rms_summed, 1)

            for l in range(2):
                for u in range(HEAD_HALVES):
                    in_half(l, 0, u, 2 * l * KT if u < 2 else None)
                    if u == 0:
                        if l == 0:
                            pe.wait_ge(x_copied, KT)
                            pe.wait_ge(x_scaled, KT)
                        rms_sum(l)
                first_stage(l, 0)
                with pe.Fori(0, H - 1) as h:
                    for u in range(HEAD_HALVES):
                        in_half(l, h + 1, u)
                        mixer_stage(l, h, u)
                    first_stage(l, h + 1)
                for u in range(HEAD_HALVES):
                    mixer_stage(l, H - 1, u)

                def out_pair(l, i, first=False):
                    for par in range(2):
                        for kh in range(2):
                            u = 2 * par + kh
                            half(i * 4 + (l * LAYER_HALVES + IN_HALVES + u), u, i * 2 + (l * LAYER_TILES + 4 * H + par),
                                 par, kh, (2 * l + 1) * KT if first and par == 0 else None)
                            if l == 1 and kh == 0 and not (first and par == 0):
                                turn_y(i * 2 + (par - 1), 1 - par)

                def turn_y(n, par):
                    pe.wait_ge(evacuated, added(1, n))
                    if not (isinstance(n, int) and n == 0):
                        pe.wait_ge(y_copied, n)
                    for b in range(NB):
                        turn(M[0][:, b * P:(b + 1) * P], x_new[par][:, b * P:(b + 1) * P])
                    turn(M[1][:, 0:P], x_new[par][:, LAST:T]).then_inc(y_turned, 1)

                out_pair(l, 0, True)
                with pe.Fori(1, KT // 2) as i:
                    out_pair(l, i)
                if l == 1:
                    turn_y(KT - 1, 1)

        @block.scalar
        def _(act):
            ch = Chain(act, act_chain)
            nc.scalar.preload_act_table_set("natural_log_exp_and_others")

            def func(out, in_, f, **kw):
                return nc.scalar.activation(out, in_, f, **kw)

            def hi(g, slot):
                if not (isinstance(g, int) and g < RING):
                    act.wait_ge(half_done, g - RING + 1)
                act.wait_ge(raw_loaded[slot], raw_count(g, slot))
                func(w_hi[:, slot], w_raw[:, slot], ACT.Copy).then_inc(hi_ready, 1)

            def raw_count(g, slot):
                if isinstance(g, int):
                    return 16 * (g // RING + 1)
                return (g - slot) * 4 + 16

            def split_ahead(l, h, u):
                g = h * HEAD_HALVES + (l * LAYER_HALVES + u + AHEAD)
                hi(g, (u + AHEAD) % RING)

            def act_split(base, wait):
                for k in range(KT):
                    if wait is not None and k == 0:
                        act.wait_ge(*wait)
                    func(act_hi[:, k, :], full[:, k, :], ACT.Copy).then_inc(act_hi_ready, 1)

            def att_square(h):
                act.wait_ge(evacuated, h * 4 + 2)
                if not (isinstance(h, int) and h == 0):
                    act.wait_ge(qk_normed, h)
                func(qk_sq, Y[:, 0:2, :], ACT.Square).then_inc(qk_squared, 1)

            def att_load_past_k(h):
                act.dma_start(past_k, past_k_v[:, :, bass.ds(h, 1), :].rearrange("p b h d -> p b (h d)")).then_inc(past_k_loaded, 16)

            def att_load_past_v(h):
                act.dma_start(past_v, past_v_v[:, :, bass.ds(h, 1), :].rearrange("p b h d -> p b (h d)")).then_inc(past_v_loaded, 16)

            def att_act(h, u):
                if u == 0:
                    act.wait_ge(stage_a, h + 1)
                    ch.done(func(qk_sq[:, :, 0:SEQ], M01, ACT.Ln, scale=1.0 / P, bias=eps[:]))
                    ch.done(func(qk_sq[:, :, SEQ:T], M[2][:, 0:2 * SAMPLE].rearrange("p (b t) -> p b t", b=2), ACT.Ln,
                                 scale=1.0 / P, bias=eps[:]))
                    func(past_kT, M[2][:, 192:448], ACT.Copy).then_inc(past_copied, 1)
                    ch.wait()
                    func(qk_sq, qk_sq, ACT.Exp, scale=-0.5).then_inc(qk_rstd, 1)
                    act.wait_ge(evacuated, h * 4 + 4)
                    ch.done(func(g_tmp, Y[:, 3, :], ACT.Abs))
                    ch.wait()
                    ch.done(func(g_tmp, g_tmp, ACT.Exp, scale=-1.0))
                    ch.wait()
                    func(g_tmp, g_tmp, ACT.Ln, bias=one_c[:]).then_inc(gate_log, 1)
                elif u == 1:
                    act.wait_ge(gate_ls, h + 1)
                    func(g_tmp, g_tmp, ACT.Exp).then_inc(gate_sig, 1)
                elif u == 2:
                    act.wait_ge(stage_b, h + 1)
                    ch.done(func(za[:, 0:512], M[0], ACT.Abs))
                    ch.done(func(za[:, 512:896], M[1][:, 0:384], ACT.Abs))
                    ch.done(func(za[:, 896:Z_ALL], M[2][:, 0:480], ACT.Abs))
                    if not (isinstance(h, int) and h == 0):
                        act.wait_ge(k_stored, h * 32)
                    func(k_nat[:, 0:NB, :], M[3].rearrange("p (b d) -> p b d", b=NB), ACT.Copy).then_inc(k_copied, 1)
                    ch.wait()
                    ch.done(func(za, za, ACT.Exp, scale=-1.0))
                    ch.wait()
                    func(za, za, ACT.Ln, bias=one_c[:]).then_inc(soft_log, 1)
                elif u == 3:
                    act.wait_ge(v_copied, h + 1)
                    act.dma_start(v_prompt_v[:, :, bass.ds(h, 1), :].rearrange("p b h d -> p b (h d)"), v_nat[:, 0:NB, :]).then_inc(v_stored, 16)
                    act.dma_start(v_sample[0, 0][:, bass.ds(h, 1), :].rearrange("p h d -> p (h d)"), v_nat[SROW:P, 4, :]).then_inc(v_stored, 16)
                elif u == 4:
                    act.wait_ge(stage_c, h + 1)
                    ch.done(func(za[:, 0:512], M[0], ACT.Exp))
                    ch.done(func(za[:, 512:896], M[1][:, 0:384], ACT.Exp))
                    func(za[:, 896:Z_ALL], M[2][:, 0:480], ACT.Exp).then_inc(weights_ready, 1)
                    func(k_nat[:, 4, :], M[3][:, 0:P], ACT.Copy).then_inc(k_last_copied, 1)
                elif u == 5:
                    act.wait_ge(k_copied, h + 1)
                    act.wait_ge(k_last_copied, h + 1)
                    act.dma_start(k_prompt_v[:, :, bass.ds(h, 1), :].rearrange("p b h d -> p b (h d)"), k_nat[:, 0:NB, :]).then_inc(k_stored, 16)
                    act.dma_start(k_sample[0, 0][:, bass.ds(h, 1), :].rearrange("p h d -> p (h d)"), k_nat[SROW:P, 4, :]).then_inc(k_stored, 16)

            def att_next(h, u):
                if u == 2:
                    act.wait_ge(stage_a, h)
                    att_load_past_k(h)
                elif u == 5:
                    att_square(h)
                elif u == 6:
                    act.wait_ge(stage_d, h)
                    att_load_past_v(h)

            def rec_next(h, u):
                if u == 5:
                    act.wait_ge(evacuated, h * 4 + (LAYER_TILES + 2))
                    if not (isinstance(h, int) and h == 0):
                        act.wait_ge(o_ready, h + (H - 1))
                    ch.done(func(r_tmp, Y[:, 0:2, :], ACT.Abs))
                    ch.wait()
                    ch.done(func(r_tmp, r_tmp, ACT.Exp, scale=-1.0))
                    ch.wait()
                    func(r_tmp, r_tmp, ACT.Ln, bias=one_c[:]).then_inc(r_log, 1)
                elif u == 6:
                    act.wait_ge(r_ls, h + 1)
                    ch.done(func(lse, r_tmp[:, 1], ACT.Abs, bias=LOG_BA[:, bass.ds(h, 1)]))
                    ch.wait()
                    ch.done(func(lse, lse, ACT.Exp, scale=-1.0))
                    ch.wait()
                    func(lse, lse, ACT.Ln, bias=one_c[:]).then_inc(r_lse, 1)
                    func(r_tmp[:, 0], r_tmp[:, 0], ACT.Exp).then_inc(r_sig, 1)
                elif u == 7:
                    act.wait_ge(r_kx, h + 1)
                    func(kk, kk, ACT.Exp).then_inc(r_kexp, 1)

            def level_exp(h, i):
                n = T if LEVELS[i] <= SAMPLE // 2 else SEQ
                act.wait_ge(r_diff, h * NL + (i + 1))
                func(dl[0][:, 0:n], dl[0][:, 0:n], ACT.Exp).then_inc(r_dexp, 1)

            def rec_act(h, u):
                if u == 0:
                    act.wait_ge(r_cum, h + 1)
                    func(eb, cum, ACT.Exp).then_inc(r_eb, 1)
                    act.wait_ge(r_kdx, h + 1)
                    func(kd, kd, ACT.Exp).then_inc(r_kde, 1)
                    act.wait_ge(r_vT, h + 1)
                    ch.done(func(v_nat_r[:, 0:NB, :], M[3].rearrange("p (b d) -> p b d", b=NB), ACT.Copy))
                    func(v_nat_r[:, 4, :], M[2][:, 0:P], ACT.Copy).then_inc(r_v, 1)
                    level_exp(h, 0)
                elif u == 1:
                    level_exp(h, 1)
                    act.wait_ge(evacuated, h * 4 + (LAYER_TILES + 4))
                    ch.done(func(g_tmp_r, Y[:, 3, :], ACT.Abs))
                    ch.wait()
                    ch.done(func(g_tmp_r, g_tmp_r, ACT.Exp, scale=-1.0))
                    ch.wait()
                    func(g_tmp_r, g_tmp_r, ACT.Ln, bias=one_c[:]).then_inc(r_glog, 1)
                elif u == 2:
                    act.wait_ge(r_kdT, h + 1)
                    ch.done(func(kd_nat[:, 0:NB, :], M[3].rearrange("p (b d) -> p b d", b=NB), ACT.Copy))
                    act.wait_ge(r_diag_put, h + 1)
                    func(kd_nat[:, 4, :], M[2][:, 0:P], ACT.Copy).then_inc(r_kdn, 1)
                    level_exp(h, 2)
                    level_exp(h, 3)
                elif u == 3:
                    level_exp(h, 4)
                    act.wait_ge(r_gls, h + 1)
                    func(g_tmp_r, g_tmp_r, ACT.Exp).then_inc(r_gsig, 1)
                    level_exp(h, 5)
                elif u == 4:
                    level_exp(h, 6)
                elif u == 5:
                    act.wait_ge(r_state, h + 1)
                    act.dma_start(s_prompt[0, 0][bass.ds(h, 1)].rearrange("h a b -> (h a) b"), S[:, NB, :]).then_inc(s_stored, 16)
                    act.dma_start(s_sample[0, 0][bass.ds(h, 1)].rearrange("h a b -> (h a) b"), S[:, 5, :]).then_inc(s_stored, 16)
                elif u == 7:
                    act.wait_ge(r_out, h + 1)
                    if not (isinstance(h, int) and h == H - 1):
                        act.wait_ge(r_qk, h + 2)
                    ch.done(func(o_cp[:, 0:SEQ], M[3], ACT.Copy))
                    ch.done(func(o_cp[:, SEQ:T], M[2][:, 0:SAMPLE], ACT.Copy))
                    ch.wait()
                    func(o_sq, o_cp, ACT.Square).then_inc(r_ocp, 1)

            def rec_norm(h):
                act.wait_ge(r_ssq, h + 1)
                ch.done(func(o_sq[:, 0:SEQ], M[0], ACT.Ln, scale=1.0 / P, bias=eps[:]))
                ch.done(func(o_sq[:, SEQ:T], M[1][:, 0:SAMPLE], ACT.Ln, scale=1.0 / P, bias=eps[:]))
                ch.wait()
                func(o_sq, o_sq, ACT.Exp, scale=-0.5).then_inc(r_orstd, 1)

            def load_state(h):
                act.dma_start(S[:, 0, :], state_hgrn[0, 0][bass.ds(h, 1)].rearrange("h a b -> (h a) b")).then_inc(s_loaded, 16)

            act.wait_ge(consts_ready, 1)
            act.wait_ge(vecs_ready, 1)
            ch.done(func(LB_E, LB_T, ACT.Exp))
            act.wait_ge(vecs_ready, 2)
            ch.done(func(LOG_A, LB_R, ACT.Ln))
            ch.done(func(LOG_BA, ONE_LB, ACT.Ln))
            for k in range(KT):
                act.wait_ge(x_turned, k + 1)
                if k >= 2:
                    act.wait_ge(x_stored[k % 2], 16 * (k // 2))
                src = psum[:, 4 + 2 * (k % 2), :]
                ch.done(func(x_new[k % 2][:, 0:SEQ], src, ACT.Copy))
                func(x_new[k % 2][:, SEQ:T], psum[:, 5 + 2 * (k % 2), 0:SAMPLE], ACT.Copy).then_inc(x_copied, 1)
                act.wait_ge(x_copied, k + 1)
                ch.wait()
                if k >= 1:
                    act.wait_ge(x_summed, k)
                func(x_sq, x_new[k % 2], ACT.Square).then_inc(x_squared, 1)
                act.dma_start(x_residual[k], x_new[k % 2]).then_inc(x_stored[k % 2], 16)
                act.wait_ge(x_scaled, k + 1)
                func(act_hi[:, k, :], x_tmp[k % 2], ACT.Copy).then_inc(act_hi_ready, 1)
            for g in range(AHEAD):
                hi(g, g)

            def rms(l):
                act.wait_ge(rms_summed, l + 1)
                for par in range(2):
                    act.wait_ge(x_stored[par], 16 * (KT // 2) * (l + 1))
                if l:
                    act.wait_ge(evacuated, LAYER_TILES)
                ch.done(func(rstd_x[:, 0:SEQ], M[0], ACT.Ln, scale=1.0 / D, bias=eps[:]))
                ch.done(func(rstd_x[:, SEQ:T], M[1][:, 0:SAMPLE], ACT.Ln, scale=1.0 / D, bias=eps[:]))
                ch.wait()
                func(rstd_x[:], rstd_x[:], ACT.Exp, scale=-0.5).then_inc(rstd_ready, 1)

            for l in range(2):
                if l == 1:
                    act.wait_ge(half_done, LAYER_HALVES)
                    act_split(2 * KT, (full_ready, KT))
                for u in range(HEAD_HALVES):
                    split_ahead(l, 0, u)
                    if u == 0:
                        rms(l)
                        if l == 0:
                            att_load_past_k(0)
                            att_load_past_v(0)
                        else:
                            load_state(0)
                    if u >= 5:
                        (att_square(0) if u == 5 else None) if l == 0 else rec_next(0, u)
                with act.Fori(0, H - 1) as h:
                    ch.enter(h, 0, 10 if l == 0 else 12)
                    for u in range(HEAD_HALVES):
                        split_ahead(l, h + 1, u)
                        if l == 0:
                            att_act(h, u)
                            att_next(h + 1, u)
                        else:
                            rec_act(h, u) if u != 7 else None
                            rec_next(h + 1, u)
                            if u == 7:
                                rec_act(h, 7)
                                rec_norm(h)
                                act.wait_ge(r_out, h + 1)
                                load_state(h + 1)
                    ch.leave(H - 1)
                for u in range(HEAD_HALVES):
                    att_act(H - 1, u) if l == 0 else rec_act(H - 1, u)
                if l == 1:
                    rec_norm(H - 1)
                act.wait_ge(half_done, l * LAYER_HALVES + IN_HALVES)
                act_split((2 * l + 1) * KT, (o_ready, (l + 1) * H))

                def out_pair(l, i, last=False):
                    for par in range(2):
                        n = i * 2 + par
                        for kh in range(2):
                            u = 2 * par + kh
                            if last and l == 1 and u + AHEAD >= 4:
                                continue
                            hi(i * 4 + (l * LAYER_HALVES + IN_HALVES + u + AHEAD), (u + AHEAD) % RING)
                        act.wait_ge(evacuated, added(l, n))
                        if l == 0:
                            func(full[:, bass.ds(n, 1), :].rearrange("p a t -> p (a t)"), x_new[par], ACT.Copy,
                                 scale=NORM[1][:, bass.ds(n, 1)]).then_inc(full_ready, 1)
                            act.wait_ge(x_summed, n + KT)
                            func(x_sq, x_new[par], ACT.Square).then_inc(x_squared, 1)
                            act.dma_start(x_residual[bass.ds(n, 1)].rearrange("a p t -> (a p) t"), x_new[par]
                                          ).then_inc(x_stored[par], 16)
                        else:
                            act.wait_ge(y_turned, n + 1)
                            if not (isinstance(i, int) and i == 0):
                                act.wait_ge(y_stored[par], i * 32)
                            ch.done(func(y_nat[par][:, 0:NB, :], M[0].rearrange("p (b d) -> p b d", b=NB), ACT.Copy))
                            func(y_nat[par][:, 4, :], M[1][:, 0:P], ACT.Copy).then_inc(y_copied, 1)
                            ch.wait()
                            act.wait_ge(y_copied, n + 1)
                            act.dma_start(y_prompt_v[:, :, bass.ds(n * P, P)], y_nat[par][:, 0:NB, :]).then_inc(y_stored[par], 16)
                            act.dma_start(y_sample[0][:, bass.ds(n * P, P)], y_nat[par][SROW:P, 4, :]).then_inc(y_stored[par], 16)

                with act.Fori(0, KT // 2 - 1) as i:
                    ch.enter(i, 0, 0 if l == 0 else 2)
                    out_pair(l, i)
                    ch.leave(KT // 2 - 1)
                out_pair(l, KT // 2 - 1, last=True)

        @block.vector
        def _(dve):
            ch = Chain(dve, dve_chain)

            def lo(g, slot):
                dve.wait_ge(hi_ready, g + 1)
                dve.tensor_tensor(w_lo[:, slot], w_raw[:, slot], w_hi[:, slot].bitcast(F32), ALU.subtract
                                  ).then_inc(lo_ready, 1)

            def split_ahead(l, h, u):
                lo(h * HEAD_HALVES + (l * LAYER_HALVES + u + AHEAD), (u + AHEAD) % RING)

            def act_split(base):
                for k in range(KT):
                    dve.wait_ge(act_hi_ready, base + k + 1)
                    dve.tensor_tensor(act_lo[:, k, :], full[:, k, :], act_hi[:, k, :].bitcast(F32), ALU.subtract
                                      ).then_inc(act_lo_ready, 1)

            def evacuate(l, h, j):
                dve.wait_ge(half_done, h * HEAD_HALVES + (l * LAYER_HALVES + 2 * j + 2))
                if l == 0 and j < 2 and not (isinstance(h, int) and h == 0):
                    dve.wait_ge(qk_normed, h)
                dve.tensor_tensor(Y[:, j, :].rearrange("p (a t) -> p a t", a=2), acc[j % 2],
                                  rstd_x[:].rearrange("p (a t) -> p a t", a=2), ALU.mult).then_inc(evacuated, 1)

            def att_dve(h, u):
                if u == 0:
                    dve.wait_ge(stage_a, h + 1)
                    if not (isinstance(h, int) and h == 0):
                        dve.wait_ge(v_stored, h * 32)
                    ch.done(dve.tensor_copy(v_nat[:, 0:NB, :], M[3].rearrange("p (b d) -> p b d", b=NB)))
                    dve.wait_ge(past_copied, h + 1)
                    dve.tensor_copy(v_nat[:, 4, :], M[2][:, 64:192]).then_inc(v_copied, 1)
                    dve.wait_ge(qk_rstd, h + 1)
                    ch.done(dve.scalar_tensor_tensor(out=qn, in0=Y[:, 0, :], scalar=WQS, in1=qk_sq[:, 0, :],
                                                     op0=ALU.mult, op1=ALU.mult))
                    dve.scalar_tensor_tensor(out=kn, in0=Y[:, 1, :], scalar=WK, in1=qk_sq[:, 1, :],
                                             op0=ALU.mult, op1=ALU.mult).then_inc(qk_normed, 1)
                elif u == 1:
                    dve.wait_ge(gate_log, h + 1)
                    dve.scalar_tensor_tensor(out=g_tmp, in0=Y[:, 3, :], scalar=0.0, in1=g_tmp,
                                             op0=ALU.min, op1=ALU.subtract).then_inc(gate_ls, 1)
                elif u == 2:
                    dve.wait_ge(gate_sig, h + 1)
                    dve.tensor_tensor(gate, Y[:, 3, :], g_tmp, ALU.mult).then_inc(gate_ready, 1)
                elif u == 3:
                    dve.wait_ge(soft_log, h + 1)
                    for k, (at, src) in enumerate(((0, M[0]), (512, M[1][:, 0:384]), (896, M[2][:, 0:480]))):
                        n = src.shape[-1]
                        ins = dve.scalar_tensor_tensor(out=sp[:, at:at + n], in0=src, scalar=0.0,
                                                       in1=za[:, at:at + n], op0=ALU.max, op1=ALU.add)
                        ins.then_inc(sp_ready, 1) if k == 2 else ch.done(ins)
                elif u == 6:
                    dve.wait_ge(stage_d, h + 1)
                    dve.wait_ge(gate_ready, h + 1)
                    out = full[:, bass.ds(h, 1), :].rearrange("p a t -> p (a t)")
                    ch.done(dve.tensor_tensor(full[:, bass.ds(h, 1), 0:SEQ].rearrange("p a t -> p (a t)"), M[3],
                                              gate[:, 0:SEQ], ALU.mult))
                    dve.tensor_tensor(full[:, bass.ds(h, 1), SEQ:T].rearrange("p a t -> p (a t)"),
                                      M[1][:, 384:384 + SAMPLE], gate[:, SEQ:T], ALU.mult).then_inc(o_ready, 1)

            def rec_next(h, u):
                if u == 6:
                    dve.wait_ge(r_log, h + 1)
                    dve.scalar_tensor_tensor(out=r_tmp, in0=Y[:, 0:2, :], scalar=0.0, in1=r_tmp,
                                             op0=ALU.min, op1=ALU.subtract).then_inc(r_ls, 1)
                elif u == 7:
                    if not (isinstance(h, int) and h == 0):
                        dve.wait_ge(r_lev, h * NL)
                    dve.wait_ge(r_ls, h + 1)
                    dve.tensor_tensor(kk, r_tmp[:, 1], Y[:, 1, :], ALU.subtract).then_inc(r_kx, 1)
                    dve.wait_ge(r_lse, h + 1)
                    ch.done(dve.tensor_scalar(cum, r_tmp[:, 1], LOG_BA[:, bass.ds(h, 1)], 0.0, ALU.add, ALU.max))
                    ch.wait()
                    ch.done(dve.tensor_tensor(cum, cum, lse, ALU.add))
                    ch.wait()
                    ch.done(dve.tensor_scalar(lse, cum, LOG_A[:, bass.ds(h, 1)], 0.0, ALU.add, ALU.min))
                    dve.wait_ge(r_sig, h + 1)
                    ch.done(dve.tensor_tensor(qs, Y[:, 0, :], r_tmp[:, 0], ALU.mult))
                    ch.wait()
                    dve.tensor_tensor_scan(cum, run_on[:], lse, 0.0, ALU.mult, ALU.add).then_inc(r_cum, 1)
                    dve.wait_ge(r_kexp, h + 1)
                    dve.tensor_scalar(kk, kk, ONE_LB[:, bass.ds(h, 1)], None, ALU.mult).then_inc(r_qk, 1)

            def level(h, i, part):
                m = LEVELS[i]
                n = T if m <= SAMPLE // 2 else SEQ

                def cut(v):
                    v = v[:, 0:n].rearrange("p (b j) -> p b j", j=2 * m)
                    return v[:, :, 0:m], v[:, :, m:2 * m]
                d1, d2 = cut(dl[0])
                c1, c2 = cut(cum)
                x1, x2 = cut(xl[i % 2])
                r = cum[:, 0:n].rearrange("p (b j) -> p b j", j=2 * m)[:, :, m - 1:m].broadcast_to([P, n // (2 * m), m])
                if part == 0:
                    if i:
                        dve.wait_ge(r_x, h * NL + i)
                    ch.done(dve.tensor_tensor(d1, r, c1, ALU.subtract))
                    dve.tensor_tensor(d2, c2, r, ALU.subtract).then_inc(r_diff, 1)
                else:
                    dve.wait_ge(r_dexp, h * NL + (i + 1))
                    if i >= 2:
                        dve.wait_ge(r_lev, h * NL + (i - 1))
                    ch.done(dve.tensor_tensor(x1, cut(kk)[0], d1, ALU.mult))
                    dve.tensor_tensor(x2, cut(qs)[1], d2, ALU.mult).then_inc(r_x, 1)

            def put(h, i, bank):
                m = LEVELS[i]
                dve.wait_ge(consts_ready, 1)
                if i:
                    dve.wait_ge(r_put, h * NL + i)
                dve.wait_ge(r_lev, h * NL + (i + 1))
                msk = level_mask[:, MASK_COL[m]:MASK_COL[m] + 64].bitcast(I32).rearrange("p (b j) -> p b j", j=m)
                for b in range(NB):
                    dst = A[:, b * P:(b + 1) * P].rearrange("p (b j) -> p b j", j=2 * m)[:, :, m:2 * m]
                    src = M[bank][:, b * 64:(b + 1) * 64].rearrange("p (b j) -> p b j", j=m)
                    ins = dve.copy_predicated(dst, msk, src)
                    if b < NB - 1 or m <= SAMPLE // 2:
                        ch.done(ins)
                if m <= SAMPLE // 2:
                    dst = A[:, SEQ:T].rearrange("p (b j) -> p b j", j=2 * m)[:, :, m:2 * m]
                    src = M[bank][:, 256:256 + SAMPLE // 2].rearrange("p (b j) -> p b j", j=m)
                    nb = SAMPLE // 2 // m
                    ins = dve.copy_predicated(dst, msk[:, 64 // m - nb:64 // m, :], src)
                ins.then_inc(r_put, 1)

            def rec_dve(h, u):
                if u == 0:
                    dve.wait_ge(r_cum, h + 1)
                    dve.wait_ge(r_qk, h + 1)
                    for b in range(5):
                        n = P if b < NB else SAMPLE
                        v = cum[:, b * P:b * P + n]
                        ins = dve.tensor_tensor(kd[:, b * P:b * P + n], v[:, n - 1:n].broadcast_to([P, n]), v, ALU.subtract)
                        ins.then_inc(r_kdx, 1) if b == NB else ch.done(ins)
                    level(h, 0, 0)
                    dve.wait_ge(r_kde, h + 1)
                    dve.tensor_tensor(kd, kd, kk, ALU.mult).then_inc(r_kd, 1)
                    level(h, 0, 1)
                    dve.wait_ge(r_eb, h + 1)
                    ch.done(dve.tensor_tensor(qe, qs, eb, ALU.mult))
                elif u == 1:
                    level(h, 1, 0)
                    level(h, 1, 1)
                elif u == 2:
                    dve.wait_ge(r_kdT, h + 1)
                    ch.done(dve.tensor_tensor(A[:, 0:SEQ].rearrange("p (b t) -> p b t", b=NB),
                                              M[0].rearrange("p (b t) -> p b t", b=NB),
                                              ident[:].unsqueeze(1).broadcast_to([P, NB, P]), ALU.mult))
                    dve.tensor_tensor(A[:, SEQ:T], M[2][:, P:P + SAMPLE], ident[:, SROW:P], ALU.mult
                                      ).then_inc(r_diag_put, 1)
                    dve.wait_ge(r_glog, h + 1)
                    dve.scalar_tensor_tensor(out=g_tmp_r, in0=Y[:, 3, :], scalar=0.0, in1=g_tmp_r,
                                             op0=ALU.min, op1=ALU.subtract).then_inc(r_gls, 1)
                    dve.wait_ge(r_diag_put, h + 1)
                    level(h, 2, 0)
                    put(h, 0, 1)
                    level(h, 2, 1)
                    level(h, 3, 0)
                elif u == 3:
                    put(h, 1, 0)
                    level(h, 3, 1)
                    level(h, 4, 0)
                    dve.wait_ge(r_upd, h + 1)
                    if not (isinstance(h, int) and h == 0):
                        dve.wait_ge(s_stored, h * 32)
                    dve.wait_ge(s_loaded, h * 16 + 16)
                    ch.done(dve.tensor_copy(S[:, 1, :], M[3][:, 0:P]))
                    ch.done(dve.scalar_tensor_tensor(out=S[:, 5, :], in0=S[:, 0, :], scalar=eb[:, T - 1:T],
                                                     in1=M[2][:, 0:P], op0=ALU.mult, op1=ALU.add))
                    for b in range(1, NB):
                        ch.wait()
                        ins = dve.scalar_tensor_tensor(out=S[:, b + 1, :], in0=S[:, b, :],
                                                       scalar=eb[:, (b + 1) * P - 1:(b + 1) * P],
                                                       in1=M[3][:, b * P:(b + 1) * P], op0=ALU.mult, op1=ALU.add)
                        ins.then_inc(r_state, 1) if b == NB - 1 else ch.done(ins)
                    dve.wait_ge(r_gsig, h + 1)
                    dve.tensor_tensor(gate_r, Y[:, 3, :], g_tmp_r, ALU.mult).then_inc(r_gate, 1)
                    level(h, 4, 1)
                    level(h, 5, 0)
                elif u == 4:
                    put(h, 2, 1)
                    put(h, 3, 0)
                    level(h, 5, 1)
                    level(h, 6, 0)
                elif u == 5:
                    put(h, 4, 1)
                    put(h, 5, 0)
                    level(h, 6, 1)
                elif u == 6:
                    put(h, 6, 1)

            def rec_gate(h):
                dve.wait_ge(r_orstd, h + 1)
                dve.wait_ge(r_gate, h + 1)
                ch.done(dve.scalar_tensor_tensor(out=o_cp, in0=o_cp, scalar=WO, in1=o_sq, op0=ALU.mult, op1=ALU.mult))
                ch.wait()
                dve.tensor_tensor(full[:, bass.ds(h, 1), :].rearrange("p a t -> p (a t)"), o_cp, gate_r, ALU.mult
                                  ).then_inc(o_ready, 1)

            dve.wait_ge(vecs_turned, 1)
            ch.done(dve.tensor_copy(vecs[:], M[0][:, 0:51]))
            ch.wait()
            ch.done(dve.tensor_scalar(WQS, WQ, float(P) ** -0.5, None, ALU.mult))
            dve.tensor_tensor(LB_T, LB_RAW, LB_RAW, ALU.subtract).then_inc(vecs_ready, 1)
            dve.wait_ge(act_chain, 1)
            ch.done(dve.reciprocal(LB_R, LB_E))
            ch.wait()
            ch.done(dve.tensor_tensor(LB_T, LB_E, LB_R, ALU.mult))
            ch.wait()
            ch.done(dve.tensor_tensor(LB, LB_T, LB_T, ALU.subtract))
            ch.wait()
            ch.done(dve.tensor_scalar(LB, LB, 0.0, LB_TOP, ALU.max, ALU.min))
            ch.wait()
            ch.done(dve.tensor_scalar(ONE_LB, LB, -1.0, 1.0, ALU.mult, ALU.add))
            ch.wait()
            dve.tensor_scalar(LB_R, LB, LB_FLOOR, TWO60, ALU.max, ALU.mult).then_inc(vecs_ready, 1)
            dve.wait_ge(act_chain, 3)
            ch.done(dve.tensor_scalar(LOG_A, LOG_A, -LN_TWO60, None, ALU.add))
            ch.wait()
            ch.done(dve.tensor_tensor(LOG_BA, LOG_BA, LOG_A, ALU.subtract))
            for k in range(KT):
                dve.wait_ge(x_turned, k + 1)
                if k >= 2:
                    dve.wait_ge(act_lo_ready, k - 1)
                dve.wait_ge(x_copied, k + 1)
                ch.done(dve.tensor_scalar(x_tmp[k % 2][:, 0:SEQ], psum[:, 4 + 2 * (k % 2), :], NORM[0][:, k:k + 1], None, ALU.mult))
                dve.tensor_scalar(x_tmp[k % 2][:, SEQ:T], psum[:, 5 + 2 * (k % 2), 0:SAMPLE], NORM[0][:, k:k + 1], None,
                                  ALU.mult).then_inc(x_scaled, 1)
                dve.wait_ge(act_hi_ready, k + 1)
                dve.wait_ge(x_scaled, k + 1)
                dve.tensor_tensor(act_lo[:, k, :], x_tmp[k % 2], act_hi[:, k, :].bitcast(F32), ALU.subtract
                                  ).then_inc(act_lo_ready, 1)
            for g in range(AHEAD):
                lo(g, g)

            for l in range(2):
                if l == 1:
                    act_split(2 * KT)
                for u in range(HEAD_HALVES):
                    split_ahead(l, 0, u)
                    if u == 0:
                        dve.wait_ge(rstd_ready, l + 1)
                    if u in (2, 4, 6):
                        evacuate(l, 0, u // 2 - 1)
                    if l == 1:
                        rec_next(0, u)
                with dve.Fori(0, H - 1) as h:
                    ch.enter(h, 0, 5 if l == 0 else 55)
                    for u in range(HEAD_HALVES):
                        split_ahead(l, h + 1, u)
                        if u == 0:
                            evacuate(l, h, 3)
                            if l == 1:
                                pass
                        elif u % 2 == 0:
                            evacuate(l, h + 1, u // 2 - 1)
                        if l == 0:
                            att_dve(h, u)
                        else:
                            rec_dve(h, u)
                            rec_next(h + 1, u)
                            if u == 7:
                                rec_gate(h)
                    ch.leave(H - 1)
                evacuate(l, H - 1, 3)
                for u in range(HEAD_HALVES):
                    att_dve(H - 1, u) if l == 0 else rec_dve(H - 1, u)
                if l == 1:
                    rec_gate(H - 1)
                act_split((2 * l + 1) * KT)

                def out_pair(l, i, last=False):
                    for par in range(2):
                        for kh in range(2):
                            u = 2 * par + kh
                            if last and l == 1 and u + AHEAD >= 4:
                                continue
                            lo(i * 4 + (l * LAYER_HALVES + IN_HALVES + u + AHEAD), (u + AHEAD) % RING)
                        dve.wait_ge(half_done, i * 4 + (l * LAYER_HALVES + IN_HALVES + 2 * par + 2))
                        dve.wait_ge(x_old_loaded[par], i * 16 + (16 * (KT // 2) * l + 16))
                        if not (isinstance(i, int) and i == 0):
                            if l == 0:
                                dve.wait_ge(x_stored[par], i * 16 + 16 * (KT // 2))
                                dve.wait_ge(x_squared, i * 2 + (KT + par - 1))
                                dve.wait_ge(full_ready, i * 2 + (par - 1))
                            else:
                                dve.wait_ge(y_turned, i * 2 + (par - 1))
                        dve.tensor_tensor(x_new[par].rearrange("p (a t) -> p a t", a=2), acc[par],
                                          x_old[par].rearrange("p (a t) -> p a t", a=2), ALU.add).then_inc(evacuated, 1)

                out_pair(l, 0)
                with dve.Fori(1, KT // 2 - 1) as i:
                    out_pair(l, i)
                out_pair(l, KT // 2 - 1, last=True)


_INS = ["x_prompt", "x_sample", "cache_k", "cache_v", "state_hgrn", "norm_w", "w_in", "w_out", "q_norm_w",
        "k_norm_w", "hgrn_norm_w", "hgrn_lb"]
_OUTS = [(1, SEQ, D), (1, SAMPLE, D), (1, 1, SEQ, H, P), (1, 1, SEQ, H, P), (1, 1, H, P, P),
         (1, 1, SAMPLE, H, P), (1, 1, SAMPLE, H, P), (1, 1, H, P, P)]


def kernel(**inputs):
    import numpy as _np
    import concourse.bacc as _bacc
    from concourse.bass_utils import run_bass_kernel_spmd as _run

    nc = _bacc.Bacc("TRN2", target_bir_lowering=False, num_devices=1)
    arrays, args = {}, []
    for name in _INS:
        a = _np.ascontiguousarray(inputs[name])
        arrays[f"in_{name}"] = a
        args.append(nc.dram_tensor(f"in_{name}", a.shape, F32, kind="ExternalInput").ap())
    for i, shape in enumerate(_OUTS):
        args.append(nc.dram_tensor(f"out_{i}", shape, F32, kind="ExternalOutput").ap())
    encoder_step(nc, *args)
    r = _run(nc, [arrays], core_ids=[0])
    return tuple(r.results[0][f"out_{i}"] for i in range(len(_OUTS)))
```

```python
from contextlib import ExitStack

import concourse.bass as bass
from concourse import mybir

F32 = mybir.dt.float32
F32R = mybir.dt.float32r
BF16 = mybir.dt.bfloat16
I32 = mybir.dt.int32
ALU = mybir.AluOpType
ACT = mybir.ActivationFunctionType

P = 128
D = 2048
KT = D // P
H = 16
SEQ, SAMPLE, PAST = 512, 32, 256
T = SEQ + SAMPLE
HT = T // 2
NB = SEQ // P
LAST = T - P
SROW = P - SAMPLE
EPS = 1e-6
MASKED = -1e30
LB_FLOOR = 1e-30
LB_TOP = 1.0 - 1e-6
TWO60 = float(2.0 ** 60)
LN_TWO60 = 41.58883083359672

KH = KT // 2
RING = 4
AHEAD = 3
HEAD_HALVES = 8
IN_HALVES = H * HEAD_HALVES
OUT_HALVES = KT * 2
LAYER_HALVES = IN_HALVES + OUT_HALVES
ALL_HALVES = 2 * LAYER_HALVES
LAYER_TILES = LAYER_HALVES // 2

Z_COL = [0, 512, 896, 1152]
Z_LEN = [512, 384, 256, 128]
Z_PAST0, Z_PAST1, Z_NEW = 1280, 1312, 1344
Z_ALL = 1376
LEVELS = [64, 32, 16, 8, 4, 2, 1]
MASK_COL = {m: 64 * i for i, m in enumerate(LEVELS)}
X_CHUNKS = [0, 2, 4, 8, 12, KT]
LAST_SPLIT = [{-1: range(0, 4), 0: [], 1: range(4, 12), 2: [], 3: [], 4: range(12, 15), 5: [], 6: []},
              {-1: range(0, 3), 0: range(3, 6), 1: range(6, 8), 2: range(8, 10), 3: range(10, 12), 4: range(12, 15),
               5: [], 6: []}]
LAST_FILL = [{-1: range(0, 4), 0: [], 1: [4, 5, 6], 2: [7, 8], 3: [9, 10], 4: [11, 12], 5: [13], 6: [14]},
             {-1: range(0, 3), 0: [3, 4], 1: [5, 6], 2: [7, 8], 3: [9], 4: [10, 11], 5: [12], 6: [13, 14]}]


class Chain:

    def __init__(self, eng, sem):
        self.eng, self.sem, self.base, self.n = eng, sem, 0, 0

    def done(self, ins):
        ins.then_inc(self.sem, 1)
        self.n += 1
        return self.n

    def wait(self, mark=None):
        self.eng.wait_ge(self.sem, self.base + (self.n if mark is None else mark))

    def enter(self, i, first, per):
        self.outer, self.first, self.per = self.base + self.n, first, per
        self.base, self.n = i * per + self.outer, 0

    def leave(self, times):
        assert self.n == self.per, (self.n, self.per)
        self.base, self.n = self.outer + self.per * times, 0


def encoder_step(nc, x_prompt, x_sample, cache_k, cache_v, state_hgrn, norm_w, w_in, w_out, q_norm_w, k_norm_w,
                 hgrn_norm_w, hgrn_lb, y_prompt, y_sample, k_prompt, v_prompt, s_prompt, k_sample, v_sample,
                 s_sample):
    x_residual = nc.dram_tensor("x_residual", (KT, P, T), F32, kind="Internal").ap()

    with ExitStack() as ctx:
        def sb(name, shape, dt=F32):
            return ctx.enter_context(nc.sbuf_tensor(name, shape, dt))

        def sem(name):
            return ctx.enter_context(nc.semaphore(name))

        act_hi = sb("act_hi", [P, KT, T], F32R)
        act_lo = sb("act_lo", [P, KT, T], F32R)
        full = sb("full", [P, KT, T])
        w_raw = sb("w_raw", [P, RING, KH, P])
        w_hi = sb("w_hi", [P, RING, KH, P], F32R)
        w_lo = sb("w_lo", [P, RING, KH, P], F32R)
        Y = sb("Y", [P, 4, T])
        rstd_x = sb("rstd_x", [P, T])
        ident = sb("ident", [P, P])
        ident_b = sb("ident_b", [P, P], BF16)
        neg_tri = sb("neg_tri", [P, P], F32R)
        neg_ones = sb("neg_ones", [P, P], F32R)
        ones_r = sb("ones_r", [P, P], F32R)
        ones = ones_r[:].bitcast(F32)
        hide = sb("hide", [P, P], BF16)
        hide_last = sb("hide_last", [P, SAMPLE], BF16)
        level_mask = sb("level_mask", [P, 64 * len(LEVELS)])
        run_on = sb("run_on", [P, T])
        vecs = sb("vecs", [P, 51])
        small = sb("small", [P, 8, KT])
        eps = sb("eps", [P, 1])
        one_c = sb("one_c", [P, 1])
        WORK = 10208
        work_at = -(-nc.sbuf_base // 32) * 32
        work = ctx.enter_context(nc.sbuf_tensor("work", [P, WORK], F32))

        def work_r(name, at, n):
            return nc.alloc_sbuf_tensor_at(name, [P, n], F32R, offset=work_at + 4 * at)[:]

        psum = ctx.enter_context(nc.psum_tensor("psum", [P, 8, 512], F32))
        acc = [psum[:, 0:2, 0:HT], psum[:, 2:4, 0:HT]]
        M = [psum[:, 4 + i, :] for i in range(4)]
        M01 = psum[:, 4:6, :]

        NORM = [vecs[:, 0:KT], vecs[:, KT:2 * KT]]
        LB_RAW = vecs[:, 32:48]
        WQ, WK, WO = vecs[:, 48:49], vecs[:, 49:50], vecs[:, 50:51]
        LB, ONE_LB, LOG_A, LOG_BA = small[:, 0], small[:, 1], small[:, 2], small[:, 3]
        LB_E, LB_T, LB_R, LB_Q = small[:, 4], small[:, 5], small[:, 6], small[:, 7]
        WQS = small[:, 7, 1:2]

        class Carve:
            def __init__(self):
                self.at = 0

            def __call__(self, n):
                v = work[:, self.at:self.at + n]
                self.at += n
                assert self.at <= WORK, self.at
                return v

        c = Carve()
        qk_sq = c(2 * T).rearrange("p (b t) -> p b t", b=2)
        qkn = c(2 * T).rearrange("p (b t) -> p b t", b=2)
        qn, kn = qkn[:, 0], qkn[:, 1]
        gate = g_tmp = c(T)
        za = c(Z_ALL)
        v_nat = c(5 * P).rearrange("p (b d) -> p b d", b=5)
        k_nat = c(5 * P).rearrange("p (b d) -> p b d", b=5)
        past_kT = c(PAST)
        past_k = c(PAST).rearrange("p (b d) -> p b d", b=2)
        past_v = c(PAST).rearrange("p (b d) -> p b d", b=2)
        sp_hi = work_r("sp_hi", c.at, Z_ALL)
        sp_lo = work_r("sp_lo", c.at + Z_ALL, Z_ALL)
        qk_hi = work_r("qk_hi", c.at, 2 * T).rearrange("p (b t) -> p b t", b=2)
        qk_lo = work_r("qk_lo", c.at + 2 * T, 2 * T).rearrange("p (b t) -> p b t", b=2)
        v_hi, v_lo = [work_r(n, c.at + 2 * Z_ALL + i * 3 * P, 3 * P).rearrange("p (b d) -> p b d", b=3)
                      for i, n in enumerate(("v_hi", "v_lo"))]
        assert c.at + 2 * Z_ALL + 6 * P <= WORK
        c = Carve()
        r_tmp = c(2 * T).rearrange("p (b t) -> p b t", b=2)
        lse = c(T)
        cum = c(T)
        qs, kk, qe, kd = c(T), c(T), c(T), c(T)
        eb = c(T)
        gate_r = g_tmp_r = c(T)
        dl = [c(T) for _ in range(2)]
        xl = [c(T) for _ in range(2)]
        A = c(SEQ + SAMPLE)
        v_nat_r = c(5 * P).rearrange("p (b d) -> p b d", b=5)
        kd_nat = c(5 * P).rearrange("p (b d) -> p b d", b=5)
        S = c(6 * P).rearrange("p (b d) -> p b d", b=6)
        o_cp, o_sq = xl
        o_hi, o_lo = [work_r(n, (4 * 2 + 2 + i) * T, T) for i, n in enumerate(("o_hi", "o_lo"))]
        c = Carve()
        x_old = [c(T) for _ in range(2)]
        x_new = [c(T) for _ in range(2)]
        x_sq = c(T)
        sq_sum = c(T)
        y_nat = [c(5 * P).rearrange("p (b d) -> p b d", b=5) for _ in range(2)]
        x_more = [work[:, c.at - 2 * T + i * T:c.at - T + i * T] for i in range(2)]
        x_tmp = [c(T) for _ in range(2)]
        x_sq_b = c(T)
        x_nat_s = c(D)[0:SAMPLE]
        vec_rows = c(P)[0:51]
        tri_f = c(P)
        neg_f = c(P)
        ones_f = c(P)
        x_in = x_old + x_new + x_more
        XB = len(x_in)
        x_nat = full[:, :, :].rearrange("p a b -> p (a b)")[:, 0:NB * D].rearrange("p (b c) -> p b c", b=NB)

        x_loaded = [sem(f"x_loaded{i}") for i in range(len(X_CHUNKS) - 1)]; x_s_loaded = sem("x_s_loaded"); x_s_copied = sem("x_s_copied")
        x_in_stored = [sem(f"x_in_stored{i}") for i in range(XB)]
        ident_ready = sem("ident_ready"); start_sq = sem("start_sq"); r_diag = sem("r_diag"); soft = sem("softplus"); sp_hi_ready = sem("sp_hi_ready"); qk_hi_ready = sem("qk_hi_ready"); qk_lo_ready = sem("qk_lo_ready"); qkn_hi_ready = sem("qkn_hi_ready"); qkn_lo_ready = sem("qkn_lo_ready"); v_hi_ready = sem("v_hi_ready"); v_lo_ready = sem("v_lo_ready"); w_att = sem("att_weights"); att_hi_ready = sem("att_weights_hi"); vec_loaded = sem("vec_loaded")
        consts_ready = sem("consts_ready"); pool_chain = sem("pool_chain")
        act_chain = sem("act_chain"); dve_chain = sem("dve_chain")
        raw_loaded = [sem(f"raw_loaded{i}") for i in range(RING)]
        hi_ready = sem("hi_ready"); lo_ready = sem("lo_ready"); half_done = sem("half_done")
        evacuated = sem("evacuated")
        vecs_turned = sem("vecs_turned"); vecs_ready = sem("vecs_ready")
        x_turned = sem("x_turned"); x_copied = sem("x_copied"); x_scaled = sem("x_scaled")
        x_squared = sem("x_squared"); x_summed = sem("x_summed"); x_stored = [sem("x_stored0"), sem("x_stored1")]
        x_old_loaded = [sem("x_old_loaded0"), sem("x_old_loaded1")]
        rms_summed = sem("rms_summed"); rstd_ready = sem("rstd_ready")
        act_hi_ready = sem("act_hi_ready"); act_lo_ready = sem("act_lo_ready")
        full_ready = sem("full_ready")
        qk_squared = sem("qk_squared"); stage_a = sem("att_sums_and_turns"); qk_rstd = sem("qk_rstd")
        v_copied = sem("v_copied"); past_copied = sem("past_copied")
        qk_normed = sem("qk_normed"); stage_b = sem("att_scores"); k_copied = sem("k_copied")
        soft_log = sem("soft_log"); sp_ready = sem("sp_ready"); stage_c = sem("att_cumulated")
        k_last_copied = sem("k_last_copied"); weights_ready = sem("weights_ready"); stage_d = sem("att_mixed")
        gate_ls = sem("gate_ls"); gate_log = sem("gate_log"); gate_sig = sem("gate_sig"); gate_ready = sem("gate_ready")
        o_ready = sem("o_ready")
        past_k_loaded = sem("past_k_loaded"); past_v_loaded = sem("past_v_loaded")
        v_stored = sem("v_stored"); k_stored = sem("k_stored")
        r_log = sem("r_log"); r_ls = sem("r_ls"); r_lse = sem("r_lse"); r_kx = sem("r_kx"); r_cum = sem("r_cum")
        r_sig = sem("r_sig"); r_kexp = sem("r_kexp"); r_qk = sem("r_qk"); r_eb = sem("r_eb")
        r_kdx = sem("r_kdx"); r_kde = sem("r_kde"); r_kd = sem("r_kd")
        r_vT = sem("r_v_turned"); r_v = sem("r_v_copied"); r_kdT = sem("r_kd_turned"); r_kdn = sem("r_kd_copied")
        r_diff = sem("r_diff"); r_dexp = sem("r_dexp"); r_x = sem("r_x"); r_lev = sem("r_level_scores")
        r_put = sem("r_scores_put")
        r_diag_put = sem("r_diag_put")
        r_upd = sem("r_update"); r_state = sem("r_state")
        r_gls = sem("r_gate_ls"); r_glog = sem("r_gate_log"); r_gsig = sem("r_gate_sig"); r_gate = sem("r_gate")
        r_out = sem("r_out"); r_ocp = sem("r_out_copied"); r_ohi = sem("r_out_sq_hi"); r_olo = sem("r_out_sq_lo"); r_ssq = sem("r_out_sum"); r_orstd = sem("r_out_rstd")
        s_loaded = sem("s_loaded"); s_stored = sem("s_stored")
        y_turned = sem("y_turned"); y_copied = sem("y_copied"); y_stored = [sem("y_stored0"), sem("y_stored1")]

        NL = len(LEVELS)

        def added(l, n):
            return n + (l * LAYER_TILES + 4 * H + 1)

        def stored_all(l, b):
            return 16 * len(range(b, KT, (XB, 2)[l]))

        block = ctx.enter_context(nc.Block())

        w_in_v = [w_in[l].rearrange("(kh kt p) c -> kh p kt c", p=P, kt=KH) for l in range(2)]
        w_out_v = [w_out[l].rearrange("(kh kt p) c -> kh p kt c", p=P, kt=KH) for l in range(2)]
        k_prompt_v = k_prompt[0, 0].rearrange("(b p) h d -> p b h d", p=P)
        v_prompt_v = v_prompt[0, 0].rearrange("(b p) h d -> p b h d", p=P)
        past_k_v = cache_k[0, 0].rearrange("(b p) h d -> p b h d", p=P)
        past_v_v = cache_v[0, 0].rearrange("(b p) h d -> p b h d", p=P)
        y_prompt_v = y_prompt[0].rearrange("(b p) c -> p b c", p=P)

        @block.sync
        def _(sp_eng):
            xp = x_prompt[0].rearrange("(b p) c -> p b c", p=P)
            def half(g, slot, src):
                if not (isinstance(g, int) and g < RING):
                    sp_eng.wait_ge(lo_ready, g - RING + 1)
                sp_eng.dma_start(w_raw[:, slot], src).then_inc(raw_loaded[slot], 16)

            def in_half(l, h, u):
                half(h * HEAD_HALVES + (l * LAYER_HALVES + u), u % RING,
                     w_in_v[l][u % 2][:, :, bass.ds(h * P + (u // 2) * D, P)])

            def load_x(q):
                cols = slice(X_CHUNKS[q] * P, X_CHUNKS[q + 1] * P)
                sp_eng.dma_start(x_nat[:, :, cols], xp[:, :, cols]).then_inc(x_loaded[q], 16)

            sp_eng.dma_start(vec_rows[0:32, :], norm_w.rearrange("l (k p) -> (l k) p", p=P)).then_inc(vec_loaded, 16)
            sp_eng.dma_start(vec_rows[32:48, :], hgrn_lb.rearrange("l (k p) -> (l k) p", p=P)).then_inc(vec_loaded, 16)
            sp_eng.dma_start(vec_rows[48:49, :], q_norm_w).then_inc(vec_loaded, 16)
            sp_eng.dma_start(vec_rows[49:50, :], k_norm_w).then_inc(vec_loaded, 16)
            sp_eng.dma_start(vec_rows[50:51, :], hgrn_norm_w).then_inc(vec_loaded, 16)
            load_x(0)
            sp_eng.dma_start(x_nat_s, x_sample[0]).then_inc(x_s_loaded, 16)
            for u in range(2):
                in_half(0, 0, u)
                load_x(u + 1)
            load_x(3)
            load_x(4)
            for l in range(2):
                if l == 0:
                    sp_eng.wait_ge(x_copied, 10)
                for u in range(2 if l == 0 else 0, HEAD_HALVES):
                    in_half(l, 0, u)
                with sp_eng.Fori(1, H) as h:
                    for u in range(HEAD_HALVES):
                        in_half(l, h, u)
                out0 = l * LAYER_HALVES + IN_HALVES

                def out_pair(i, first, last):
                    for u in range(4):
                        half(i * 4 + (out0 + u), u, w_out_v[l][u // 2][:, :, bass.ds(i * (2 * P) + (u % 2) * P, P)])
                    for par in range(2):
                        if first:
                            if par == 0:
                                sp_eng.wait_ge(qk_normed if l == 0 else r_qk, H)
                            if par == 0:
                                for b, stored in enumerate((x_in_stored, x_stored)[l]):
                                    sp_eng.wait_ge(stored, stored_all(l, b))
                        else:
                            sp_eng.wait_ge(evacuated, added(l, i * 2 + (par - 2)))
                        sp_eng.dma_start(x_old[par], x_residual[bass.ds(i * 2 + par, 1)].rearrange("a p t -> (a p) t")
                                         ).then_inc(x_old_loaded[par], 16)
                out_pair(0, True, False)
                with sp_eng.Fori(1, KT // 2) as i:
                    out_pair(i, False, False)
            sp_eng.wait_ge(v_stored, 32 * H)
            sp_eng.wait_ge(k_stored, 32 * H)
            sp_eng.wait_ge(s_stored, 32 * H)
            for par in range(2):
                sp_eng.wait_ge(y_stored[par], 32 * (KT // 2))
                sp_eng.wait_ge(x_stored[par], 16 * (KT // 2))

        @block.gpsimd
        def _(pool):
            ch = Chain(pool, pool_chain)
            ch.done(pool.memset(ident[:], 0.0))
            ch.wait()
            pool.affine_select(out=ident[:], in_=ident[:], pattern=[[-1, P]], base=0, channel_multiplier=1,
                               compare_op=ALU.not_equal, fill=1.0).then_inc(ident_ready, 1)
            ch.done(pool.memset(eps[:], EPS))
            ch.done(pool.memset(one_c[:], 1.0))
            ch.done(pool.memset(ones_f, 1.0))
            ch.done(pool.memset(neg_f, -1.0))
            ch.done(pool.memset(hide[:], 0.0))
            ch.done(pool.memset(hide_last[:], 0.0))
            ch.done(pool.memset(level_mask[:], 1.0))
            ch.done(pool.memset(run_on[:], 1.0))
            ch.done(pool.memset(sq_sum, 0.0))
            ch.wait()
            ch.done(pool.memset(run_on[:, 0:T:P], 0.0))
            ch.done(pool.affine_select(out=tri_f, in_=neg_f, pattern=[[-1, P]], base=0,
                                       channel_multiplier=1, compare_op=ALU.is_ge, fill=0.0))
            ch.done(pool.affine_select(out=hide[:], in_=hide[:], pattern=[[1, P]], base=0, channel_multiplier=-1,
                                       compare_op=ALU.is_gt, fill=MASKED))
            ch.done(pool.affine_select(out=hide_last[:], in_=hide_last[:], pattern=[[0, SAMPLE]], base=-SROW,
                                       channel_multiplier=1, compare_op=ALU.is_ge, fill=MASKED))
            ch.wait()
            ch.done(pool.affine_select(out=hide_last[:], in_=hide_last[:], pattern=[[1, SAMPLE]], base=SROW,
                                       channel_multiplier=-1, compare_op=ALU.is_gt, fill=MASKED))
            for m in LEVELS:
                v = level_mask[:, MASK_COL[m]:MASK_COL[m] + 64].rearrange("p (b j) -> p b j", j=m)
                ch.done(pool.affine_select(out=v, in_=v, pattern=[[-2 * m, 64 // m], [0, m]], base=0,
                                           channel_multiplier=1, compare_op=ALU.is_ge, fill=0.0))
                ch.wait()
                ch.done(pool.affine_select(out=v, in_=v, pattern=[[2 * m, 64 // m], [0, m]], base=m - 1,
                                           channel_multiplier=-1, compare_op=ALU.is_ge, fill=0.0))
                ch.wait()
            pool.wait_ge(ident_ready, 1)
            ch.done(pool.tensor_copy(neg_tri[:], tri_f))
            ch.done(pool.tensor_copy(neg_ones[:], neg_f))
            ch.done(pool.tensor_copy(ones_r[:], ones_f))
            pool.tensor_copy(ident_b[:], ident[:]).then_inc(consts_ready, 1)

            def add_squares(n, squares):
                pool.wait_ge(x_squared, n + 1)
                if not (isinstance(n, int) and n == 0):
                    pool.wait_ge(x_summed, n)
                pool.tensor_tensor(sq_sum, sq_sum, squares, ALU.add).then_inc(x_summed, 1)

            for n in range(KT):
                add_squares(n, (x_sq, x_sq_b)[n % 2])
            pool.wait_ge(o_ready, H)
            pool.memset(sq_sum, 0.0).then_inc(pool_chain, 1)
            ch.n += 1
            ch.wait()
            with pool.Fori(0, KT) as i:
                add_squares(i + KT, x_sq)

        @block.tensor
        def _(pe):
            def turn(out, in_, n=P, **kw):
                return pe.matmul(out, in_, ident[0:n, 0:n], is_transpose=True, start=True, stop=True, **kw)

            def part(slot, par, ks, wait_act=None, opens=None):
                for k in ks:
                    if wait_act is not None:
                        pe.wait_ge(act_lo_ready, wait_act + k + 1)
                    for n, (w, a) in enumerate(((w_hi, act_hi), (w_hi, act_lo), (w_lo, act_hi))):
                        for j in range(2):
                            mm = pe.matmul(acc[par][:, j, :], w[:, slot, k % KH, :], a[:, k, j * HT:(j + 1) * HT],
                                           start=(k == 0 and n == 0), stop=(k == KT - 1 and n == 2))
                return mm

            def half_ready(g, t, kh):
                pe.wait_ge(lo_ready, g + 1)
                if kh == 0 and not (isinstance(t, int) and t < 2):
                    pe.wait_ge(evacuated, t - 1)

            def half(g, slot, t, par, kh, wait_act=None):
                half_ready(g, t, kh)
                part(slot, par, range(kh * KH, (kh + 1) * KH), wait_act).then_inc(half_done, 1)

            def in_half(l, h, u, wait_act=None):
                half(h * HEAD_HALVES + (l * LAYER_HALVES + u), u % RING, h * 4 + (l * LAYER_TILES + u // 2),
                     (u // 2) % 2, u % 2, wait_act)

            def att_sums_and_turns(h):
                pe.wait_ge(qk_lo_ready, h + 1)
                pe.wait_ge(evacuated, h * 4 + 3)
                pe.wait_ge(past_k_loaded, (h + 1) * 16)
                if not (isinstance(h, int) and h == 0):
                    pe.wait_ge(o_ready, h)
                for b in range(2):
                    pe.matmul(M[b], ones_r[:], qk_hi[:, b, 0:SEQ], start=True, stop=False)
                    pe.matmul(M[b], ones_r[:], qk_lo[:, b, 0:SEQ], start=False, stop=True)
                out = M[2][:, 0:2 * SAMPLE].rearrange("p (b t) -> p b t", b=2)
                pe.matmul(out, ones_r[:], qk_hi[:, :, SEQ:T], start=True, stop=False)
                pe.matmul(out, ones_r[:], qk_lo[:, :, SEQ:T], start=False, stop=True)
                turn(M[2][:, 64:192], Y[:, 2, LAST:T])
                for b in range(2):
                    turn(M[2][:, 192 + b * P:192 + (b + 1) * P], past_k[:, b, :])
                for b in range(NB):
                    mm = turn(M[3][:, b * P:(b + 1) * P], Y[:, 2, b * P:(b + 1) * P])
                mm.then_inc(stage_a, 1)

            def att_scores(h):
                pe.wait_ge(qkn_lo_ready, h + 1)
                pe.wait_ge(v_copied, h + 1)
                pe.wait_ge(past_copied, h + 1)
                for b in range(3):
                    for n, (k_, q_) in enumerate(((qk_hi, qk_hi), (qk_hi, qk_lo), (qk_lo, qk_hi))):
                        pe.matmul(M[b][:, 0:Z_LEN[b]], k_[:, 1, b * P:(b + 1) * P], q_[:, 0, b * P:SEQ],
                                  start=(n == 0), stop=False, skip_group_check=True)
                pe.matmul(M[2][:, 256:384], kn[:, 3 * P:SEQ], qn[:, 3 * P:SEQ], start=False, stop=False,
                          skip_group_check=True)
                for b in range(2):
                    pe.matmul(M[2][:, 384 + b * SAMPLE:384 + (b + 1) * SAMPLE], past_kT[:, b * P:(b + 1) * P],
                              qn[:, SEQ:T], start=False, stop=True, skip_group_check=True)
                pe.matmul(M[2][:, 448:480], kn[:, LAST:T], qn[:, SEQ:T], start=False, stop=False,
                          skip_group_check=True)
                for out, mask in ((M[0][:, 0:P], hide[:]), (M[1][:, 0:P], hide[:]), (M[2][:, 0:P], hide[:]),
                                  (M[2][:, 256:384], hide[:]), (M[2][:, 448:480], hide_last[:])):
                    pe.matmul(out, ident_b[:], mask, start=False, stop=True, skip_group_check=True)
                for b in range(NB):
                    mm = turn(M[3][:, b * P:(b + 1) * P], kn[:, b * P:(b + 1) * P])
                mm.then_inc(stage_b, 1)

            def att_cumulated(h):
                pe.wait_ge(sp_ready, h + 1)
                pe.wait_ge(k_copied, h + 1)
                turn(M[3][:, 0:P], kn[:, LAST:T])
                for part_ in (sp_hi, sp_lo):
                    for out, at in ((M[0], 0), (M[1][:, 0:384], 512), (M[2][:, 0:480], 896)):
                        pe.matmul(out, neg_tri[:], part_[:, at:at + out.shape[-1]], start=False, stop=True,
                                  skip_group_check=True)
                for part_ in (sp_hi, sp_lo):
                    for b in range(NB):
                        for later in range(b + 1, NB):
                            pe.matmul(M[b][:, (later - b) * P:Z_LEN[b]], neg_ones[:],
                                      part_[:, Z_COL[later]:Z_COL[later] + Z_LEN[later]], start=False, stop=True,
                                      skip_group_check=True)
                    pe.matmul(M[2][:, 384:448], neg_ones[:], part_[:, Z_PAST1:Z_ALL], start=False, stop=True,
                              skip_group_check=True)
                    mm = pe.matmul(M[2][:, 384:416], neg_ones[:], part_[:, Z_NEW:Z_ALL], start=False, stop=True,
                                   skip_group_check=True)
                mm.then_inc(stage_c, 1)

            def att_mixed(h):
                pe.wait_ge(weights_ready, h + 1)
                pe.wait_ge(k_last_copied, h + 1)
                pe.wait_ge(past_v_loaded, (h + 1) * 16)
                pe.wait_ge(v_lo_ready, h + 1)
                for b in range(3):
                    for n, (v_, w_) in enumerate(((v_hi, sp_hi), (v_hi, sp_lo), (v_lo, sp_hi))):
                        pe.matmul(M[3][:, b * P:SEQ], v_[:, b, :], w_[:, Z_COL[b]:Z_COL[b] + Z_LEN[b]],
                                  start=(b == 0 and n == 0), stop=False, skip_group_check=True)
                pe.matmul(M[3][:, 3 * P:SEQ], v_nat[:, 3, :], za[:, Z_COL[3]:Z_COL[3] + P], start=False, stop=True,
                          skip_group_check=True)
                out = M[1][:, 384:384 + SAMPLE]
                pe.matmul(out, past_v[:, 0, :], za[:, Z_PAST0:Z_PAST0 + SAMPLE], start=True, stop=False)
                pe.matmul(out, past_v[:, 1, :], za[:, Z_PAST1:Z_PAST1 + SAMPLE], start=False, stop=False)
                pe.matmul(out, v_nat[:, 4, :], za[:, Z_NEW:Z_NEW + SAMPLE], start=False, stop=True).then_inc(stage_d, 1)

            def rec_turn_v(h):
                pe.wait_ge(evacuated, h * 4 + (LAYER_TILES + 3))
                if not (isinstance(h, int) and h == 0):
                    pe.wait_ge(r_ocp, h)
                for b in range(NB):
                    turn(M[3][:, b * P:(b + 1) * P], Y[:, 2, b * P:(b + 1) * P])
                turn(M[2][:, 0:P], Y[:, 2, LAST:T]).then_inc(r_vT, 1)

            def rec_level(h, i, bank):
                m = LEVELS[i]
                pe.wait_ge(r_x, h * NL + (i + 1))
                x = xl[i % 2]
                for b in range(NB):
                    rhs = x[:, b * P:(b + 1) * P].rearrange("p (b j) -> p b j", j=2 * m)[:, :, m:2 * m]
                    mm = pe.matmul(M[bank][:, b * 64:(b + 1) * 64], x[:, b * P:(b + 1) * P], rhs,
                                   start=True, stop=True)
                if m <= SAMPLE // 2:
                    rhs = x[:, SEQ:T].rearrange("p (b j) -> p b j", j=2 * m)[:, :, m:2 * m]
                    mm = pe.matmul(M[bank][:, 256:256 + SAMPLE // 2], x[:, LAST:T], rhs, start=True, stop=True)
                mm.then_inc(r_lev, 1)

            def rec_stage(h, u):
                if u == 0:
                    pe.wait_ge(r_qk, h + 1)
                    if not (isinstance(h, int) and h == 0):
                        pe.wait_ge(r_orstd, h)
                    for b in range(NB):
                        pe.matmul(M[0][:, b * P:(b + 1) * P], kk[:, b * P:(b + 1) * P], qs[:, b * P:(b + 1) * P],
                                  start=True, stop=True)
                    pe.wait_ge(r_v, h + 1)
                    pe.matmul(M[2][:, P:P + SAMPLE], kk[:, LAST:T], qs[:, SEQ:T], start=True, stop=True
                              ).then_inc(r_diag, 1)
                    rec_level(h, 0, 1)
                elif u == 1:
                    pe.wait_ge(r_kd, h + 1)
                    for b in range(NB):
                        turn(M[3][:, b * P:(b + 1) * P], kd[:, b * P:(b + 1) * P])
                    pe.wait_ge(r_diag_put, h + 1)
                    turn(M[2][:, 0:P], kd[:, LAST:T]).then_inc(r_kdT, 1)
                    rec_level(h, 1, 0)
                elif u == 2:
                    pe.wait_ge(r_kdn, h + 1)
                    for b in range(NB):
                        pe.matmul(M[3][:, b * P:(b + 1) * P], kd_nat[:, b, :], v_nat_r[:, b, :], start=True, stop=True)
                    pe.matmul(M[2][:, 0:P], kd_nat[SROW:P, 4, :], v_nat_r[SROW:P, 4, :], start=True, stop=True
                              ).then_inc(r_upd, 1)
                    pe.wait_ge(r_put, h * NL + 1)
                    rec_level(h, 2, 1)
                elif u == 3:
                    pe.wait_ge(r_put, h * NL + 2)
                    rec_level(h, 3, 0)
                    pe.wait_ge(r_put, h * NL + 3)
                    rec_level(h, 4, 1)
                elif u == 4:
                    pe.wait_ge(r_put, h * NL + 4)
                    rec_level(h, 5, 0)
                    pe.wait_ge(r_put, h * NL + 5)
                    rec_level(h, 6, 1)
                elif u == 5:
                    pe.wait_ge(r_put, h * NL + 7)
                    pe.wait_ge(r_state, h + 1)
                    for b in range(NB):
                        out = M[3][:, b * P:(b + 1) * P]
                        pe.matmul(out, v_nat_r[:, b, :], A[:, b * P:(b + 1) * P], start=True, stop=(b == 0))
                        if b:
                            pe.matmul(out, S[:, b, :], qe[:, b * P:(b + 1) * P], start=False, stop=True)
                    out = M[2][:, 0:SAMPLE]
                    pe.matmul(out, v_nat_r[:, 4, :], A[:, SEQ:T], start=True, stop=False)
                    pe.matmul(out, S[:, 0, :], qe[:, SEQ:T], start=False, stop=True).then_inc(r_out, 1)
                elif u == 6:
                    pe.wait_ge(r_olo, h + 1)
                    pe.matmul(M[0], ones_r[:], o_hi[:, 0:SEQ], start=True, stop=False)
                    pe.matmul(M[0], ones_r[:], o_lo[:, 0:SEQ], start=False, stop=True)
                    pe.matmul(M[1][:, 0:SAMPLE], ones_r[:], o_hi[:, SEQ:T], start=True, stop=False)
                    pe.matmul(M[1][:, 0:SAMPLE], ones_r[:], o_lo[:, SEQ:T], start=False, stop=True).then_inc(r_ssq, 1)

            def mixer_stage(l, h, u):
                if l == 0:
                    if u == 1:
                        att_scores(h)
                    elif u == 4:
                        att_cumulated(h)
                    elif u == 6:
                        att_mixed(h)
                else:
                    rec_stage(h, u)

            def first_stage(l, h):
                if l == 0:
                    att_sums_and_turns(h)
                else:
                    rec_turn_v(h)

            pe.wait_ge(ident_ready, 1)
            pe.wait_ge(vec_loaded, 16 * 5)
            turn(M[0][:, 0:51], vec_rows, n=51).then_inc(vecs_turned, 1)

            def start_turn(k):
                if k in X_CHUNKS:
                    pe.wait_ge(x_loaded[X_CHUNKS.index(k)], 16)
                if k == 1:
                    pe.wait_ge(vecs_ready, 1)
                if k >= 3:
                    pe.wait_ge(x_copied, k - 2)
                    pe.wait_ge(x_s_copied, k - 2)
                at = 2 + 2 * (k % 3)
                for b in range(NB):
                    turn(psum[:, at, b * P:(b + 1) * P], x_nat[:, b, k * P:(k + 1) * P])
                if k == 0:
                    pe.wait_ge(x_s_loaded, 16)
                turn(psum[:, at + 1, 0:SAMPLE], x_nat_s[:, k * P:(k + 1) * P], n=SAMPLE).then_inc(x_turned, 1)

            LAG = 3
            for k in range(KT + LAG):
                if k < KT:
                    start_turn(k)
                if k == LAG:
                    half_ready(0, 0, 0)
                if k == LAG + KH:
                    half_ready(1, 0, 1)
                if k >= LAG:
                    mm = part((k - LAG) // KH, 0, [k - LAG], 0)
                    if (k - LAG) % KH == KH - 1:
                        mm.then_inc(half_done, 1)

            def rms_sum(l):
                pe.wait_ge(x_summed, (l + 1) * KT)
                pe.matmul(M[0], ones, sq_sum[:, 0:SEQ], start=True, stop=True)
                pe.matmul(M[1][:, 0:SAMPLE], ones, sq_sum[:, SEQ:T], start=True, stop=True).then_inc(rms_summed, 1)

            for l in range(2):
                for u in range(HEAD_HALVES):
                    if l or u >= 2:
                        in_half(l, 0, u, 2 * l * KT if u < 2 else None)
                    if u == 2:
                        if l == 0:
                            pe.wait_ge(x_copied, KT)
                            pe.wait_ge(x_s_copied, KT)
                            pe.wait_ge(consts_ready, 1)
                        rms_sum(l)
                first_stage(l, 0)
                with pe.Fori(0, H - 1) as h:
                    for u in range(HEAD_HALVES):
                        in_half(l, h + 1, u)
                        mixer_stage(l, h, u)
                    first_stage(l, h + 1)

                g0, t0, w0 = l * LAYER_HALVES + IN_HALVES, l * LAYER_TILES + 4 * H, (2 * l + 1) * KT
                for u in range(-1, 7):
                    if u >= 0:
                        mixer_stage(l, H - 1, u)
                    for k in LAST_FILL[l][u]:
                        for par in range(2):
                            if k % KH == 0:
                                half_ready(g0 + par + 2 * (k // KH), t0 + par, k // KH)
                            mm = part(par + 2 * (k // KH), par, [k], w0)
                            if k == KH - 1:
                                mm.then_inc(half_done, 1)
                for par in range(2):
                    part(2 + par, par, [KT - 1], w0).then_inc(half_done, 1)

                def out_pair(l, i):
                    for u in range(4):
                        half(i * 4 + (l * LAYER_HALVES + IN_HALVES + u), u, i * 2 + (l * LAYER_TILES + 4 * H + u % 2),
                             u % 2, u // 2)
                        if l == 1 and u < 2:
                            turn_y(i * 2 + (u - 2), u)

                def turn_y(n, par):
                    pe.wait_ge(evacuated, added(1, n))
                    if not (isinstance(n, int) and n == 0):
                        pe.wait_ge(y_copied, n)
                    for b in range(NB):
                        turn(M[0][:, b * P:(b + 1) * P], x_new[par][:, b * P:(b + 1) * P])
                    turn(M[1][:, 0:P], x_new[par][:, LAST:T]).then_inc(y_turned, 1)

                with pe.Fori(1, KT // 2) as i:
                    out_pair(l, i)
                if l == 1:
                    turn_y(KT - 2, 0)
                    turn_y(KT - 1, 1)

        @block.scalar
        def _(act):
            ch = Chain(act, act_chain)
            nc.scalar.preload_act_table_set("natural_log_exp_and_others")

            def func(out, in_, f, **kw):
                return nc.scalar.activation(out, in_, f, **kw)

            def hi(g, slot):
                if not (isinstance(g, int) and g < RING):
                    act.wait_ge(half_done, g - RING + 1)
                act.wait_ge(raw_loaded[slot], raw_count(g, slot))
                func(w_hi[:, slot], w_raw[:, slot], ACT.Copy).then_inc(hi_ready, 1)

            def raw_count(g, slot):
                if isinstance(g, int):
                    return 16 * (g // RING + 1)
                return (g - slot) * 4 + 16

            def split_ahead(l, h, u):
                g = h * HEAD_HALVES + (l * LAYER_HALVES + u + AHEAD)
                hi(g, (u + AHEAD) % RING)

            def act_split(ks):
                for k in ks:
                    func(act_hi[:, k, :], full[:, k, :], ACT.Copy).then_inc(act_hi_ready, 1)

            def att_square(h):
                act.wait_ge(evacuated, h * 4 + 2)
                if not (isinstance(h, int) and h == 0):
                    act.wait_ge(qk_normed, h)
                func(qk_sq, Y[:, 0:2, :], ACT.Square).then_inc(qk_squared, 1)
                func(qk_hi, Y[:, 0:2, :], ACT.Square).then_inc(qk_hi_ready, 1)

            def att_load_past_k(h):
                act.dma_start(past_k, past_k_v[:, :, bass.ds(h, 1), :].rearrange("p b h d -> p b (h d)")).then_inc(past_k_loaded, 16)

            def att_load_past_v(h):
                act.dma_start(past_v, past_v_v[:, :, bass.ds(h, 1), :].rearrange("p b h d -> p b (h d)")).then_inc(past_v_loaded, 16)

            def att_act(h, u):
                if u == 0:
                    act.wait_ge(stage_a, h + 1)
                    ch.done(func(qk_sq[:, :, 0:SEQ], M01, ACT.Ln, scale=1.0 / P, bias=eps[:]))
                    ch.done(func(qk_sq[:, :, SEQ:T], M[2][:, 0:2 * SAMPLE].rearrange("p (b t) -> p b t", b=2), ACT.Ln,
                                 scale=1.0 / P, bias=eps[:]))
                    func(past_kT, M[2][:, 192:448], ACT.Copy).then_inc(past_copied, 1)
                    ch.wait()
                    func(qk_sq, qk_sq, ACT.Exp, scale=-0.5).then_inc(qk_rstd, 1)
                    act.wait_ge(evacuated, h * 4 + 4)
                    ch.done(func(g_tmp, Y[:, 3, :], ACT.Abs))
                    ch.wait()
                    ch.done(func(g_tmp, g_tmp, ACT.Exp, scale=-1.0))
                    act.wait_ge(qk_normed, h + 1)
                    func(qk_hi, qkn, ACT.Copy).then_inc(qkn_hi_ready, 1)
                    ch.wait()
                    func(g_tmp, g_tmp, ACT.Ln, bias=one_c[:]).then_inc(gate_log, 1)
                elif u == 1:
                    act.wait_ge(gate_ls, h + 1)
                    func(g_tmp, g_tmp, ACT.Exp).then_inc(gate_sig, 1)
                    act.wait_ge(v_copied, h + 1)
                    if not (isinstance(h, int) and h == 0):
                        act.wait_ge(stage_d, h)
                    func(v_hi, v_nat[:, 0:3, :], ACT.Copy).then_inc(v_hi_ready, 1)
                elif u == 2:
                    act.wait_ge(stage_b, h + 1)
                    ch.done(func(za[:, 0:512], M[0], ACT.Abs))
                    ch.done(func(za[:, 512:896], M[1][:, 0:384], ACT.Abs))
                    ch.done(func(za[:, 896:Z_ALL], M[2][:, 0:480], ACT.Abs))
                    if not (isinstance(h, int) and h == 0):
                        act.wait_ge(k_stored, h * 32)
                    func(k_nat[:, 0:NB, :], M[3].rearrange("p (b d) -> p b d", b=NB), ACT.Copy).then_inc(k_copied, 1)
                    ch.wait()
                    ch.done(func(za, za, ACT.Exp, scale=-1.0))
                    ch.wait()
                    func(za, za, ACT.Ln, bias=one_c[:]).then_inc(soft_log, 1)
                elif u == 3:
                    act.wait_ge(v_copied, h + 1)
                    act.dma_start(v_prompt_v[:, :, bass.ds(h, 1), :].rearrange("p b h d -> p b (h d)"), v_nat[:, 0:NB, :]).then_inc(v_stored, 16)
                    act.dma_start(v_sample[0, 0][:, bass.ds(h, 1), :].rearrange("p h d -> p (h d)"), v_nat[SROW:P, 4, :]).then_inc(v_stored, 16)
                    act.wait_ge(soft, h + 1)
                    func(sp_hi, za, ACT.Copy).then_inc(sp_hi_ready, 1)
                elif u == 5:
                    act.wait_ge(stage_c, h + 1)
                    ch.done(func(za[:, 0:512], M[0], ACT.Exp))
                    ch.done(func(za[:, 512:896], M[1][:, 0:384], ACT.Exp))
                    func(za[:, 896:Z_ALL], M[2][:, 0:480], ACT.Exp).then_inc(w_att, 1)
                    ch.wait()
                    act.wait_ge(w_att, h + 1)
                    func(sp_hi, za, ACT.Copy).then_inc(att_hi_ready, 1)
                    func(k_nat[:, 4, :], M[3][:, 0:P], ACT.Copy).then_inc(k_last_copied, 1)
                elif u == 6:
                    act.wait_ge(k_copied, h + 1)
                    act.wait_ge(k_last_copied, h + 1)
                    act.dma_start(k_prompt_v[:, :, bass.ds(h, 1), :].rearrange("p b h d -> p b (h d)"), k_nat[:, 0:NB, :]).then_inc(k_stored, 16)
                    act.dma_start(k_sample[0, 0][:, bass.ds(h, 1), :].rearrange("p h d -> p (h d)"), k_nat[SROW:P, 4, :]).then_inc(k_stored, 16)

            def att_next(h, u):
                if u == 2:
                    act.wait_ge(stage_a, h)
                    att_load_past_k(h)
                elif u == 7:
                    act.wait_ge(stage_d, h)
                    att_square(h)
                    att_load_past_v(h)

            def rec_next(h, u):
                if u == 5:
                    act.wait_ge(evacuated, h * 4 + (LAYER_TILES + 2))
                    ch.done(func(r_tmp, Y[:, 0:2, :], ACT.Abs))
                    ch.wait()
                    ch.done(func(r_tmp, r_tmp, ACT.Exp, scale=-1.0))
                    ch.wait()
                    func(r_tmp, r_tmp, ACT.Ln, bias=one_c[:]).then_inc(r_log, 1)
                elif u == 6:
                    act.wait_ge(r_ls, h + 1)
                    ch.done(func(lse, r_tmp[:, 1], ACT.Abs, bias=LOG_BA[:, bass.ds(h, 1)]))
                    ch.wait()
                    ch.done(func(lse, lse, ACT.Exp, scale=-1.0))
                    ch.wait()
                    func(lse, lse, ACT.Ln, bias=one_c[:]).then_inc(r_lse, 1)
                    func(r_tmp[:, 0], r_tmp[:, 0], ACT.Exp).then_inc(r_sig, 1)
                    act.wait_ge(r_kx, h + 1)
                    func(kk, kk, ACT.Exp).then_inc(r_kexp, 1)

            def level_exp(h, i):
                n = T if LEVELS[i] <= SAMPLE // 2 else SEQ
                act.wait_ge(r_diff, h * NL + (i + 1))
                func(dl[i % 2][:, 0:n], dl[i % 2][:, 0:n], ACT.Exp).then_inc(r_dexp, 1)

            def rec_act(h, u):
                if u == 0:
                    act.wait_ge(r_vT, h + 1)
                    ch.done(func(v_nat_r[:, 0:NB, :], M[3].rearrange("p (b d) -> p b d", b=NB), ACT.Copy))
                    func(v_nat_r[:, 4, :], M[2][:, 0:P], ACT.Copy).then_inc(r_v, 1)
                elif u == 1:
                    act.wait_ge(evacuated, h * 4 + (LAYER_TILES + 4))
                    ch.done(func(g_tmp_r, Y[:, 3, :], ACT.Abs))
                    ch.wait()
                    ch.done(func(g_tmp_r, g_tmp_r, ACT.Exp, scale=-1.0))
                    ch.wait()
                    func(g_tmp_r, g_tmp_r, ACT.Ln, bias=one_c[:]).then_inc(r_glog, 1)
                    level_exp(h, 2)
                elif u == 2:
                    act.wait_ge(r_kdT, h + 1)
                    ch.done(func(kd_nat[:, 0:NB, :], M[3].rearrange("p (b d) -> p b d", b=NB), ACT.Copy))
                    func(kd_nat[:, 4, :], M[2][:, 0:P], ACT.Copy).then_inc(r_kdn, 1)
                    level_exp(h, 3)
                    act.wait_ge(r_gls, h + 1)
                    func(g_tmp_r, g_tmp_r, ACT.Exp).then_inc(r_gsig, 1)
                elif u == 3:
                    level_exp(h, 4)
                    level_exp(h, 5)
                elif u == 4:
                    level_exp(h, 6)
                    act.wait_ge(r_state, h + 1)
                    act.dma_start(s_prompt[0, 0][bass.ds(h, 1)].rearrange("h a b -> (h a) b"), S[:, NB, :]).then_inc(s_stored, 16)
                    act.dma_start(s_sample[0, 0][bass.ds(h, 1)].rearrange("h a b -> (h a) b"), S[:, 5, :]).then_inc(s_stored, 16)
                elif u == 6:
                    act.wait_ge(r_out, h + 1)
                    ch.done(func(o_cp[:, 0:SEQ], M[3], ACT.Copy))
                    ch.done(func(o_cp[:, SEQ:T], M[2][:, 0:SAMPLE], ACT.Copy))
                    ch.wait()
                    func(o_sq, o_cp, ACT.Square).then_inc(r_ocp, 1)
                    func(o_hi, o_cp, ACT.Square).then_inc(r_ohi, 1)

            def rec_decays(h):
                level_exp(h, 0)
                act.wait_ge(r_kdx, h + 1)
                func(kd, kd, ACT.Exp).then_inc(r_kde, 1)
                level_exp(h, 1)
                act.wait_ge(r_cum, h + 1)
                func(eb, cum, ACT.Exp).then_inc(r_eb, 1)

            def rec_norm(h):
                act.wait_ge(r_ssq, h + 1)
                act.wait_ge(r_olo, h + 1)
                ch.done(func(o_sq[:, 0:SEQ], M[0], ACT.Ln, scale=1.0 / P, bias=eps[:]))
                ch.done(func(o_sq[:, SEQ:T], M[1][:, 0:SAMPLE], ACT.Ln, scale=1.0 / P, bias=eps[:]))
                ch.wait()
                func(o_sq, o_sq, ACT.Exp, scale=-0.5).then_inc(r_orstd, 1)

            def load_state(h):
                act.dma_start(S[:, 0, :], state_hgrn[0, 0][bass.ds(h, 1)].rearrange("h a b -> (h a) b")).then_inc(s_loaded, 16)

            act.wait_ge(vecs_ready, 1)
            ch.done(func(LB_E, LB_T, ACT.Exp))
            for k in range(KT + 1):
                if k < KT:
                    act.wait_ge(x_turned, k + 1)
                    if k >= XB:
                        act.wait_ge(x_in_stored[k % XB], 16 * (k // XB))
                        act.wait_ge(x_scaled, k - XB + 1)
                        act.wait_ge(x_squared, k - XB + 1)
                    func(x_in[k % XB][:, 0:SEQ], psum[:, 2 + 2 * (k % 3), :], ACT.Copy).then_inc(x_copied, 1)
                if k:
                    act.wait_ge(x_scaled, k)
                    func(act_hi[:, k - 1, :], x_tmp[(k - 1) % 2], ACT.Copy).then_inc(act_hi_ready, 1)
                if k == 1:
                    hi(0, 0)
                if k == 7:
                    hi(1, 1)
                if k < KT:
                    act.wait_ge(x_copied, k + 1)
                    act.wait_ge(x_s_copied, k + 1)
                    act.dma_start(x_residual[k], x_in[k % XB]).then_inc(x_in_stored[k % XB], 16)
                    if k >= 2:
                        act.wait_ge(x_summed, k - 1)
                    func((x_sq, x_sq_b)[k % 2], x_in[k % XB], ACT.Square).then_inc(x_squared, 1)
            hi(2, 2)
            act.wait_ge(vecs_ready, 2)
            ch.done(func(LOG_A, LB_R, ACT.Ln))
            ch.done(func(LOG_BA, ONE_LB, ACT.Ln))
            act.wait_ge(consts_ready, 1)

            def rms(l):
                act.wait_ge(rms_summed, l + 1)
                for b, stored in enumerate((x_in_stored, x_stored)[l]):
                    act.wait_ge(stored, stored_all(l, b))
                if l:
                    act.wait_ge(evacuated, LAYER_TILES)
                ch.done(func(rstd_x[:, 0:SEQ], M[0], ACT.Ln, scale=1.0 / D, bias=eps[:]))
                ch.done(func(rstd_x[:, SEQ:T], M[1][:, 0:SAMPLE], ACT.Ln, scale=1.0 / D, bias=eps[:]))
                ch.wait()
                func(rstd_x[:], rstd_x[:], ACT.Exp, scale=-0.5).then_inc(rstd_ready, 1)

            for l in range(2):
                if l == 1:
                    act.wait_ge(full_ready, KT)
                    act_split(range(2, KT))
                for u in range(HEAD_HALVES):
                    split_ahead(l, 0, u)
                    if u == 2:
                        rms(l)
                        if l == 0:
                            att_load_past_k(0)
                            att_load_past_v(0)
                        else:
                            load_state(0)
                    if l == 0 and u == 7:
                        att_square(0)
                    elif l == 1 and u >= 5:
                        rec_next(0, u)
                if l == 1:
                    rec_decays(0)
                with act.Fori(0, H - 1) as h:
                    ch.enter(h, 0, 10 if l == 0 else 12)
                    for u in range(HEAD_HALVES):
                        split_ahead(l, h + 1, u)
                        if l == 0:
                            att_act(h, u)
                            att_next(h + 1, u)
                        else:
                            rec_act(h, u)
                            if u == 7:
                                rec_norm(h)
                                load_state(h + 1)
                            rec_next(h + 1, u)
                            if u == 7:
                                rec_decays(h + 1)
                    ch.leave(H - 1)
                g0 = l * LAYER_HALVES + IN_HALVES
                for u in range(-1, 7):
                    if u == -1:
                        act.wait_ge(half_done, g0)
                        act.wait_ge(o_ready, l * H + H - 1)
                    else:
                        (att_act if l == 0 else rec_act)(H - 1, u)
                    act_split(LAST_SPLIT[l][u])
                    if u == 1:
                        hi(g0 + 3, 3)
                    if u == 4 - l:
                        hi(g0 + 4, 0)
                    if u == 5:
                        hi(g0 + 5, 1)
                if l == 1:
                    rec_norm(H - 1)
                act.wait_ge(o_ready, (l + 1) * H)
                act_split([KT - 1])

                def out_pair(l, i, first=False, last=False):
                    for u in range(4):
                        if not ((first and u < 3) or (last and l == 1 and u + AHEAD >= 4)):
                            hi(i * 4 + (l * LAYER_HALVES + IN_HALVES + u + AHEAD), (u + AHEAD) % RING)
                        if l == 0 and u >= 2:
                            out_tile(i, u - 2, last)
                        if l == 1 and u < 2 and not first:
                            put_y(i - 1, u)

                def out_tile(i, par, last):
                    n = i * 2 + par
                    if last and par:
                        act.wait_ge(half_done, LAYER_HALVES)
                        act.wait_ge(full_ready, 2)
                        act_split(range(0, 2))
                    act.wait_ge(evacuated, added(l, n))
                    func(full[:, bass.ds(n, 1), :].rearrange("p a t -> p (a t)"), x_new[par], ACT.Copy,
                         scale=NORM[1][:, bass.ds(n, 1)]).then_inc(full_ready, 1)
                    act.wait_ge(x_summed, n + KT)
                    func(x_sq, x_new[par], ACT.Square).then_inc(x_squared, 1)
                    act.dma_start(x_residual[bass.ds(n, 1)].rearrange("a p t -> (a p) t"), x_new[par]
                                  ).then_inc(x_stored[par], 16)

                def put_y(i, par):
                    n = i * 2 + par
                    act.wait_ge(y_turned, n + 1)
                    if not (isinstance(i, int) and i == 0):
                        act.wait_ge(y_stored[par], i * 32)
                    ch.done(func(y_nat[par][:, 0:NB, :], M[0].rearrange("p (b d) -> p b d", b=NB), ACT.Copy))
                    func(y_nat[par][:, 4, :], M[1][:, 0:P], ACT.Copy).then_inc(y_copied, 1)
                    ch.wait()
                    act.wait_ge(y_copied, n + 1)
                    act.dma_start(y_prompt_v[:, :, bass.ds(n * P, P)], y_nat[par][:, 0:NB, :]).then_inc(y_stored[par], 16)
                    act.dma_start(y_sample[0][:, bass.ds(n * P, P)], y_nat[par][SROW:P, 4, :]).then_inc(y_stored[par], 16)

                out_pair(l, 0, first=True)
                first_looped = 1 if l == 0 else 2
                if l == 1:
                    out_pair(l, 1)
                with act.Fori(first_looped, KT // 2 - 1) as i:
                    ch.enter(i - first_looped, 0, 0 if l == 0 else 2)
                    out_pair(l, i)
                    ch.leave(KT // 2 - 1 - first_looped)
                out_pair(l, KT // 2 - 1, last=True)
                if l == 1:
                    put_y(KT // 2 - 1, 0)
                    put_y(KT // 2 - 1, 1)

        @block.vector
        def _(dve):
            ch = Chain(dve, dve_chain)

            def lo(g, slot):
                dve.wait_ge(hi_ready, g + 1)
                dve.tensor_tensor(w_lo[:, slot], w_raw[:, slot], w_hi[:, slot].bitcast(F32), ALU.subtract
                                  ).then_inc(lo_ready, 1)

            def split_ahead(l, h, u):
                lo(h * HEAD_HALVES + (l * LAYER_HALVES + u + AHEAD), (u + AHEAD) % RING)

            def act_split(base, ks=range(KT)):
                for k in ks:
                    dve.wait_ge(act_hi_ready, base + k + 1)
                    dve.tensor_tensor(act_lo[:, k, :], full[:, k, :], act_hi[:, k, :].bitcast(F32), ALU.subtract
                                      ).then_inc(act_lo_ready, 1)

            def evacuate(l, h, j):
                dve.wait_ge(half_done, h * HEAD_HALVES + (l * LAYER_HALVES + 2 * j + 2))
                if l == 0 and j < 2 and not (isinstance(h, int) and h == 0):
                    dve.wait_ge(qk_normed, h)
                dve.tensor_tensor(Y[:, j, :].rearrange("p (a t) -> p a t", a=2), acc[j % 2],
                                  rstd_x[:].rearrange("p (a t) -> p a t", a=2), ALU.mult).then_inc(evacuated, 1)

            def att_dve(h, u):
                if u == 0:
                    dve.wait_ge(stage_a, h + 1)
                    if not (isinstance(h, int) and h == 0):
                        dve.wait_ge(v_stored, h * 32)
                    ch.done(dve.tensor_copy(v_nat[:, 0:NB, :], M[3].rearrange("p (b d) -> p b d", b=NB)))
                    dve.wait_ge(past_copied, h + 1)
                    dve.tensor_copy(v_nat[:, 4, :], M[2][:, 64:192]).then_inc(v_copied, 1)
                    dve.wait_ge(qk_rstd, h + 1)
                    ch.done(dve.scalar_tensor_tensor(out=qn, in0=Y[:, 0, :], scalar=WQS, in1=qk_sq[:, 0, :],
                                                     op0=ALU.mult, op1=ALU.mult))
                    dve.scalar_tensor_tensor(out=kn, in0=Y[:, 1, :], scalar=WK, in1=qk_sq[:, 1, :],
                                             op0=ALU.mult, op1=ALU.mult).then_inc(qk_normed, 1)
                elif u == 1:
                    dve.wait_ge(qkn_hi_ready, h + 1)
                    dve.wait_ge(qk_normed, h + 1)
                    dve.tensor_tensor(qk_lo, qkn, qk_hi.bitcast(F32), ALU.subtract).then_inc(qkn_lo_ready, 1)
                    dve.wait_ge(gate_log, h + 1)
                    dve.scalar_tensor_tensor(out=g_tmp, in0=Y[:, 3, :], scalar=0.0, in1=g_tmp,
                                             op0=ALU.min, op1=ALU.subtract).then_inc(gate_ls, 1)
                elif u == 2:
                    dve.wait_ge(gate_sig, h + 1)
                    dve.tensor_tensor(gate, Y[:, 3, :], g_tmp, ALU.mult).then_inc(gate_ready, 1)
                    dve.wait_ge(v_hi_ready, h + 1)
                    dve.wait_ge(v_copied, h + 1)
                    dve.tensor_tensor(v_lo, v_nat[:, 0:3, :], v_hi.bitcast(F32), ALU.subtract).then_inc(v_lo_ready, 1)
                elif u == 3:
                    dve.wait_ge(soft_log, h + 1)
                    for k, (at, src) in enumerate(((0, M[0]), (512, M[1][:, 0:384]), (896, M[2][:, 0:480]))):
                        n = src.shape[-1]
                        ins = dve.scalar_tensor_tensor(out=za[:, at:at + n], in0=src, scalar=0.0,
                                                       in1=za[:, at:at + n], op0=ALU.max, op1=ALU.add)
                        ins.then_inc(soft, 1) if k == 2 else ch.done(ins)
                elif u == 4:
                    dve.wait_ge(sp_hi_ready, h + 1)
                    dve.tensor_tensor(sp_lo, za, sp_hi.bitcast(F32), ALU.subtract).then_inc(sp_ready, 1)
                elif u == 6:
                    dve.wait_ge(w_att, h + 1)
                    dve.wait_ge(att_hi_ready, h + 1)
                    dve.tensor_tensor(sp_lo, za, sp_hi.bitcast(F32), ALU.subtract).then_inc(weights_ready, 1)
                elif u == 7:
                    dve.wait_ge(stage_d, h + 1)
                    dve.wait_ge(gate_ready, h + 1)
                    ch.done(dve.tensor_tensor(full[:, bass.ds(h, 1), 0:SEQ].rearrange("p a t -> p (a t)"), M[3],
                                              gate[:, 0:SEQ], ALU.mult))
                    dve.tensor_tensor(full[:, bass.ds(h, 1), SEQ:T].rearrange("p a t -> p (a t)"),
                                      M[1][:, 384:384 + SAMPLE], gate[:, SEQ:T], ALU.mult).then_inc(o_ready, 1)

            def att_next(h, u):
                if u == 7:
                    dve.wait_ge(qk_hi_ready, h + 1)
                    dve.tensor_tensor(qk_lo, qk_sq, qk_hi.bitcast(F32), ALU.subtract).then_inc(qk_lo_ready, 1)

            def rec_log_sigmoids(h):
                dve.wait_ge(r_log, h + 1)
                dve.scalar_tensor_tensor(out=r_tmp, in0=Y[:, 0:2, :], scalar=0.0, in1=r_tmp,
                                         op0=ALU.min, op1=ALU.subtract).then_inc(r_ls, 1)

            def rec_next(h, u):
                if u == 6:
                    if not (isinstance(h, int) and h == 0):
                        dve.wait_ge(r_lev, h * NL)
                    dve.wait_ge(r_ls, h + 1)
                    dve.tensor_tensor(kk, r_tmp[:, 1], Y[:, 1, :], ALU.subtract).then_inc(r_kx, 1)
                    dve.wait_ge(r_lse, h + 1)
                    ch.done(dve.tensor_scalar(cum, r_tmp[:, 1], LOG_BA[:, bass.ds(h, 1)], 0.0, ALU.add, ALU.max))
                    ch.wait()
                    ch.done(dve.tensor_tensor(cum, cum, lse, ALU.add))
                    ch.wait()
                    ch.done(dve.tensor_scalar(lse, cum, LOG_A[:, bass.ds(h, 1)], 0.0, ALU.add, ALU.min))
                    dve.wait_ge(r_sig, h + 1)
                    ch.done(dve.tensor_tensor(qs, Y[:, 0, :], r_tmp[:, 0], ALU.mult))
                    ch.wait()
                    dve.tensor_tensor_scan(cum, run_on[:], lse, 0.0, ALU.mult, ALU.add).then_inc(r_cum, 1)
                elif u == 7:
                    dve.wait_ge(r_kexp, h + 1)
                    dve.tensor_scalar(kk, kk, ONE_LB[:, bass.ds(h, 1)], None, ALU.mult).then_inc(r_qk, 1)

            def level(h, i, part):
                m = LEVELS[i]
                n = T if m <= SAMPLE // 2 else SEQ

                def cut(v):
                    v = v[:, 0:n].rearrange("p (b j) -> p b j", j=2 * m)
                    return v[:, :, 0:m], v[:, :, m:2 * m]
                d1, d2 = cut(dl[i % 2])
                c1, c2 = cut(cum)
                x1, x2 = cut(xl[i % 2])
                r = cum[:, 0:n].rearrange("p (b j) -> p b j", j=2 * m)[:, :, m - 1:m].broadcast_to([P, n // (2 * m), m])
                if part == 0:
                    if i >= 2:
                        dve.wait_ge(r_x, h * NL + (i - 1))
                    ch.done(dve.tensor_tensor(d1, r, c1, ALU.subtract))
                    dve.tensor_tensor(d2, c2, r, ALU.subtract).then_inc(r_diff, 1)
                else:
                    dve.wait_ge(r_dexp, h * NL + (i + 1))
                    if i >= 2:
                        dve.wait_ge(r_lev, h * NL + (i - 1))
                    ch.done(dve.tensor_tensor(x1, cut(kk)[0], d1, ALU.mult))
                    dve.tensor_tensor(x2, cut(qs)[1], d2, ALU.mult).then_inc(r_x, 1)

            def put(h, i, bank):
                m = LEVELS[i]
                dve.wait_ge(consts_ready, 1)
                if i:
                    dve.wait_ge(r_put, h * NL + i)
                dve.wait_ge(r_lev, h * NL + (i + 1))
                msk = level_mask[:, MASK_COL[m]:MASK_COL[m] + 64].bitcast(I32).rearrange("p (b j) -> p b j", j=m)
                for b in range(NB):
                    dst = A[:, b * P:(b + 1) * P].rearrange("p (b j) -> p b j", j=2 * m)[:, :, m:2 * m]
                    src = M[bank][:, b * 64:(b + 1) * 64].rearrange("p (b j) -> p b j", j=m)
                    ins = dve.copy_predicated(dst, msk, src)
                    if b < NB - 1 or m <= SAMPLE // 2:
                        ch.done(ins)
                if m <= SAMPLE // 2:
                    dst = A[:, SEQ:T].rearrange("p (b j) -> p b j", j=2 * m)[:, :, m:2 * m]
                    src = M[bank][:, 256:256 + SAMPLE // 2].rearrange("p (b j) -> p b j", j=m)
                    nb = SAMPLE // 2 // m
                    ins = dve.copy_predicated(dst, msk[:, 64 // m - nb:64 // m, :], src)
                ins.then_inc(r_put, 1)

            def rec_distances(h):
                dve.wait_ge(r_cum, h + 1)
                level(h, 0, 0)
                for b in range(5):
                    n = P if b < NB else SAMPLE
                    v = cum[:, b * P:b * P + n]
                    ins = dve.tensor_tensor(kd[:, b * P:b * P + n], v[:, n - 1:n].broadcast_to([P, n]), v, ALU.subtract)
                    ins.then_inc(r_kdx, 1) if b == NB else ch.done(ins)
                level(h, 1, 0)

            def rec_dve(h, u):
                if u == 0:
                    dve.wait_ge(r_qk, h + 1)
                    if not (isinstance(h, int) and h == 0):
                        dve.wait_ge(o_ready, h + H)
                    level(h, 0, 1)
                    dve.wait_ge(r_kde, h + 1)
                    dve.tensor_tensor(kd, kd, kk, ALU.mult).then_inc(r_kd, 1)
                    level(h, 1, 1)
                    dve.wait_ge(r_eb, h + 1)
                    ch.done(dve.tensor_tensor(qe, qs, eb, ALU.mult))
                elif u == 1:
                    dve.wait_ge(r_diag, h + 1)
                    ch.done(dve.tensor_tensor(A[:, 0:SEQ].rearrange("p (b t) -> p b t", b=NB),
                                              M[0].rearrange("p (b t) -> p b t", b=NB),
                                              ident[:].unsqueeze(1).broadcast_to([P, NB, P]), ALU.mult))
                    dve.tensor_tensor(A[:, SEQ:T], M[2][:, P:P + SAMPLE], ident[:, SROW:P], ALU.mult
                                      ).then_inc(r_diag_put, 1)
                    level(h, 2, 0)
                    dve.wait_ge(r_diag_put, h + 1)
                    dve.wait_ge(r_glog, h + 1)
                    dve.scalar_tensor_tensor(out=g_tmp_r, in0=Y[:, 3, :], scalar=0.0, in1=g_tmp_r,
                                             op0=ALU.min, op1=ALU.subtract).then_inc(r_gls, 1)
                    put(h, 0, 1)
                    level(h, 2, 1)
                    level(h, 3, 0)
                elif u == 2:
                    put(h, 1, 0)
                    level(h, 3, 1)
                    level(h, 4, 0)
                elif u == 3:
                    put(h, 2, 1)
                    level(h, 4, 1)
                    level(h, 5, 0)
                    dve.wait_ge(r_upd, h + 1)
                    if not (isinstance(h, int) and h == 0):
                        dve.wait_ge(s_stored, h * 32)
                    dve.wait_ge(s_loaded, h * 16 + 16)
                    ch.done(dve.tensor_copy(S[:, 1, :], M[3][:, 0:P]))
                    ch.done(dve.scalar_tensor_tensor(out=S[:, 5, :], in0=S[:, 0, :], scalar=eb[:, T - 1:T],
                                                     in1=M[2][:, 0:P], op0=ALU.mult, op1=ALU.add))
                    for b in range(1, NB):
                        ch.wait()
                        ins = dve.scalar_tensor_tensor(out=S[:, b + 1, :], in0=S[:, b, :],
                                                       scalar=eb[:, (b + 1) * P - 1:(b + 1) * P],
                                                       in1=M[3][:, b * P:(b + 1) * P], op0=ALU.mult, op1=ALU.add)
                        ins.then_inc(r_state, 1) if b == NB - 1 else ch.done(ins)
                elif u == 4:
                    put(h, 3, 0)
                    level(h, 5, 1)
                    level(h, 6, 0)
                    put(h, 4, 1)
                    level(h, 6, 1)
                    dve.wait_ge(r_gsig, h + 1)
                    dve.tensor_tensor(gate_r, Y[:, 3, :], g_tmp_r, ALU.mult).then_inc(r_gate, 1)
                elif u == 5:
                    put(h, 5, 0)
                    put(h, 6, 1)
                elif u == 6:
                    dve.wait_ge(r_ocp, h + 1)
                    dve.wait_ge(r_ohi, h + 1)
                    dve.tensor_tensor(o_lo, o_sq, o_hi.bitcast(F32), ALU.subtract).then_inc(r_olo, 1)

            def rec_gate(h):
                dve.wait_ge(r_orstd, h + 1)
                dve.wait_ge(r_gate, h + 1)
                ch.done(dve.scalar_tensor_tensor(out=o_cp, in0=o_cp, scalar=WO, in1=o_sq, op0=ALU.mult, op1=ALU.mult))
                ch.wait()
                dve.tensor_tensor(full[:, bass.ds(h, 1), :].rearrange("p a t -> p (a t)"), o_cp, gate_r, ALU.mult
                                  ).then_inc(o_ready, 1)

            dve.wait_ge(vecs_turned, 1)
            ch.done(dve.tensor_copy(vecs[:], M[0][:, 0:51]))
            ch.wait()
            ch.done(dve.tensor_scalar(WQS, WQ, float(P) ** -0.5, None, ALU.mult))
            dve.tensor_tensor(LB_T, LB_RAW, LB_RAW, ALU.subtract).then_inc(vecs_ready, 1)
            for k in range(KT + 1):
                if k < KT:
                    dve.wait_ge(x_turned, k + 1)
                    if k >= XB:
                        dve.wait_ge(x_in_stored[k % XB], 16 * (k // XB))
                        dve.wait_ge(x_scaled, k - XB + 1)
                        dve.wait_ge(x_squared, k - XB + 1)
                    dve.tensor_copy(x_in[k % XB][:, SEQ:T], psum[:, 3 + 2 * (k % 3), 0:SAMPLE]).then_inc(x_s_copied, 1)
                    if k >= 2:
                        dve.wait_ge(act_lo_ready, k - 1)
                    dve.wait_ge(x_s_copied, k + 1)
                    dve.wait_ge(x_copied, k + 1)
                    dve.tensor_scalar(x_tmp[k % 2], x_in[k % XB], NORM[0][:, k:k + 1], None, ALU.mult
                                      ).then_inc(x_scaled, 1)
                if k:
                    dve.wait_ge(act_hi_ready, k)
                    dve.wait_ge(x_scaled, k)
                    dve.tensor_tensor(act_lo[:, k - 1, :], x_tmp[(k - 1) % 2], act_hi[:, k - 1, :].bitcast(F32),
                                      ALU.subtract).then_inc(act_lo_ready, 1)
                if k == 1:
                    lo(0, 0)
                if k == 7:
                    lo(1, 1)
            lo(2, 2)
            dve.wait_ge(act_chain, 1)
            ch.done(dve.reciprocal(LB_R, LB_E))
            ch.wait()
            ch.done(dve.tensor_tensor(LB_T, LB_E, LB_R, ALU.mult))
            ch.wait()
            ch.done(dve.tensor_tensor(LB, LB_T, LB_T, ALU.subtract))
            ch.wait()
            ch.done(dve.tensor_scalar(LB, LB, 0.0, LB_TOP, ALU.max, ALU.min))
            ch.wait()
            ch.done(dve.tensor_scalar(ONE_LB, LB, -1.0, 1.0, ALU.mult, ALU.add))
            ch.wait()
            dve.tensor_scalar(LB_R, LB, LB_FLOOR, TWO60, ALU.max, ALU.mult).then_inc(vecs_ready, 1)
            dve.wait_ge(act_chain, 3)
            ch.done(dve.tensor_scalar(LOG_A, LOG_A, -LN_TWO60, None, ALU.add))
            ch.wait()
            ch.done(dve.tensor_tensor(LOG_BA, LOG_BA, LOG_A, ALU.subtract))

            for l in range(2):
                if l == 1:
                    act_split(2 * KT)
                for u in range(HEAD_HALVES):
                    split_ahead(l, 0, u)
                    if u == 2:
                        dve.wait_ge(rstd_ready, l + 1)
                    if u in (2, 4, 6):
                        evacuate(l, 0, u // 2 - 1)
                    if l == 1 and u == 6:
                        rec_log_sigmoids(0)
                    (att_next if l == 0 else rec_next)(0, u)
                if l == 1:
                    rec_distances(0)
                with dve.Fori(0, H - 1) as h:
                    ch.enter(h, 0, 5 if l == 0 else 55)
                    for u in range(HEAD_HALVES):
                        split_ahead(l, h + 1, u)
                        if u == 0:
                            evacuate(l, h, 3)
                        elif u % 2 == 0:
                            evacuate(l, h + 1, u // 2 - 1)
                        if l == 0:
                            att_dve(h, u)
                            att_next(h + 1, u)
                        else:
                            if u == 6:
                                rec_log_sigmoids(h + 1)
                            rec_dve(h, u)
                            rec_next(h + 1, u)
                            if u == 7:
                                rec_gate(h)
                                rec_distances(h + 1)
                    ch.leave(H - 1)
                evacuate(l, H - 1, 3)
                g0 = l * LAYER_HALVES + IN_HALVES
                for u in range(-1, 8):
                    if u >= 0:
                        (att_dve if l == 0 else rec_dve)(H - 1, u)
                    if u < 7:
                        act_split((2 * l + 1) * KT, LAST_SPLIT[l][u])
                    if u == 1:
                        lo(g0 + 3, 3)
                    if u == 4 - l:
                        lo(g0 + 4, 0)
                    if u == 5:
                        lo(g0 + 5, 1)
                if l == 1:
                    rec_gate(H - 1)
                act_split((2 * l + 1) * KT, [KT - 1])

                def out_pair(l, i, first=False, last=False):
                    for par in range(2):
                        for u in ((0, 1, 2), (3,))[par]:
                            if (first and u < 3) or (last and l == 1 and u + AHEAD >= 4):
                                continue
                            lo(i * 4 + (l * LAYER_HALVES + IN_HALVES + u + AHEAD), (u + AHEAD) % RING)
                        dve.wait_ge(half_done, i * 4 + (l * LAYER_HALVES + IN_HALVES + par + 3))
                        dve.wait_ge(x_old_loaded[par], i * 16 + (16 * (KT // 2) * l + 16))
                        if not (isinstance(i, int) and i == 0):
                            if l == 0:
                                dve.wait_ge(x_stored[par], i * 16)
                                dve.wait_ge(x_squared, i * 2 + (KT + par - 1))
                                dve.wait_ge(full_ready, i * 2 + (par - 1))
                            else:
                                dve.wait_ge(y_turned, i * 2 + (par - 1))
                        dve.tensor_tensor(x_new[par].rearrange("p (a t) -> p a t", a=2), acc[par],
                                          x_old[par].rearrange("p (a t) -> p a t", a=2), ALU.add).then_inc(evacuated, 1)

                out_pair(l, 0, first=True)
                with dve.Fori(1, KT // 2 - 1) as i:
                    out_pair(l, i)
                out_pair(l, KT // 2 - 1, last=True)


_INS = ["x_prompt", "x_sample", "cache_k", "cache_v", "state_hgrn", "norm_w", "w_in", "w_out", "q_norm_w",
        "k_norm_w", "hgrn_norm_w", "hgrn_lb"]
_OUTS = [(1, SEQ, D), (1, SAMPLE, D), (1, 1, SEQ, H, P), (1, 1, SEQ, H, P), (1, 1, H, P, P),
         (1, 1, SAMPLE, H, P), (1, 1, SAMPLE, H, P), (1, 1, H, P, P)]


def kernel(**inputs):
    import numpy as _np
    import concourse.bacc as _bacc
    from concourse.bass_utils import run_bass_kernel_spmd as _run

    nc = _bacc.Bacc("TRN2", target_bir_lowering=False, num_devices=1)
    arrays, args = {}, []
    for name in _INS:
        a = _np.ascontiguousarray(inputs[name])
        arrays[f"in_{name}"] = a
        args.append(nc.dram_tensor(f"in_{name}", a.shape, F32, kind="ExternalInput").ap())
    for i, shape in enumerate(_OUTS):
        args.append(nc.dram_tensor(f"out_{i}", shape, F32, kind="ExternalOutput").ap())
    encoder_step(nc, *args)
    r = _run(nc, [arrays], core_ids=[0])
    return tuple(r.results[0][f"out_{i}"] for i in range(len(_OUTS)))
```

```python
from contextlib import ExitStack

import concourse.bass as bass
from concourse import mybir

F32 = mybir.dt.float32
F32R = mybir.dt.float32r
BF16 = mybir.dt.bfloat16
I32 = mybir.dt.int32
ALU = mybir.AluOpType
ACT = mybir.ActivationFunctionType

P = 128
D = 2048
KT = D // P
H = 16
SEQ, SAMPLE, PAST = 512, 32, 256
T = SEQ + SAMPLE
HT = T // 2
NB = SEQ // P
LAST = T - P
SROW = P - SAMPLE
EPS = 1e-6
MASKED = -1e30
LB_FLOOR = 1e-30
LB_TOP = 1.0 - 1e-6
TWO60 = float(2.0 ** 60)
LN_TWO60 = 41.58883083359672

KH = KT // 2
RING = 4
AHEAD = 3
HEAD_HALVES = 8
IN_HALVES = H * HEAD_HALVES
OUT_HALVES = KT * 2
LAYER_HALVES = IN_HALVES + OUT_HALVES
ALL_HALVES = 2 * LAYER_HALVES
LAYER_TILES = LAYER_HALVES // 2

Z_COL = [0, 512, 896, 1152]
Z_LEN = [512, 384, 256, 128]
Z_PAST0, Z_PAST1, Z_NEW = 1280, 1312, 1344
Z_ALL = 1376
LEVELS = [64, 32, 16, 8, 4, 2, 1]
MASK_COL = {m: 64 * i for i, m in enumerate(LEVELS)}
START_SPLITS = [1, 2, 6, 8, 14, 16]
X_CHUNKS = [0, 2, 4, 8, 12, KT]
DVE_SPLITS = 3
LAST_SPLIT = [{-1: range(0, 4), 0: [], 1: range(4, 12), 2: [], 3: [], 4: range(12, 15), 5: [], 6: []},
              {-1: [], 0: range(0, 6), 1: range(6, 8), 2: range(8, 10), 3: range(10, 12), 4: range(12, 15),
               5: [], 6: []}]
LAST_FILL = [{-1: range(0, 4), 0: [], 1: [4, 5, 6], 2: [7, 8], 3: [9, 10], 4: [11, 12], 5: [13], 6: [14]},
             {-1: [], 0: [], 1: range(0, 4), 2: [4, 5], 3: [6, 7, 8], 4: [9, 10], 5: [11, 12], 6: [13, 14]}]


class Chain:

    def __init__(self, eng, sem):
        self.eng, self.sem, self.base, self.n = eng, sem, 0, 0

    def done(self, ins):
        ins.then_inc(self.sem, 1)
        self.n += 1
        return self.n

    def wait(self, mark=None):
        self.eng.wait_ge(self.sem, self.base + (self.n if mark is None else mark))

    def enter(self, i, per):
        self.outer, self.per = self.base + self.n, per
        self.base, self.n = i * per + self.outer, 0

    def leave(self, times):
        assert self.n == self.per, (self.n, self.per)
        self.base, self.n = self.outer + self.per * times, 0


def encoder_step(nc, x_prompt, x_sample, cache_k, cache_v, state_hgrn, norm_w, w_in, w_out, q_norm_w, k_norm_w,
                 hgrn_norm_w, hgrn_lb, y_prompt, y_sample, k_prompt, v_prompt, s_prompt, k_sample, v_sample,
                 s_sample):
    x_residual = nc.dram_tensor("x_residual", (KT, P, T), F32, kind="Internal").ap()

    with ExitStack() as ctx:
        def sb(name, shape, dt=F32):
            return ctx.enter_context(nc.sbuf_tensor(name, shape, dt))

        def sem(name):
            return ctx.enter_context(nc.semaphore(name))

        act_hi = sb("act_hi", [P, KT, T], F32R)
        act_lo = sb("act_lo", [P, KT, T], F32R)
        full = sb("full", [P, KT, T])
        w_raw = sb("w_raw", [P, RING, KH, P])
        w_hi = sb("w_hi", [P, RING, KH, P], F32R)
        w_lo = sb("w_lo", [P, RING, KH, P], F32R)
        Y = sb("Y", [P, 4, T])
        rstd_x = sb("rstd_x", [P, T])
        ident = sb("ident", [P, P])
        ident_b = sb("ident_b", [P, P], BF16)
        neg_tri = sb("neg_tri", [P, P], F32R)
        neg_ones = sb("neg_ones", [P, P], F32R)
        ones_r = sb("ones_r", [P, P], F32R)
        ones = ones_r[:].bitcast(F32)
        hide = sb("hide", [P, P], BF16)
        hide_last = sb("hide_last", [P, SAMPLE], BF16)
        level_mask = sb("level_mask", [P, 64 * len(LEVELS)])
        run_on = sb("run_on", [P, T])
        vecs = sb("vecs", [P, 51])
        small = sb("small", [P, 8, KT])
        eps = sb("eps", [P, 1])
        one_c = sb("one_c", [P, 1])
        WORK = 10208
        work_at = -(-nc.sbuf_base // 32) * 32
        work = ctx.enter_context(nc.sbuf_tensor("work", [P, WORK], F32))

        def work_r(name, at, n):
            return nc.alloc_sbuf_tensor_at(name, [P, n], F32R, offset=work_at + 4 * at)[:]

        psum = ctx.enter_context(nc.psum_tensor("psum", [P, 8, 512], F32))
        acc = [psum[:, 0:2, 0:HT], psum[:, 2:4, 0:HT]]
        M = [psum[:, 4 + i, :] for i in range(4)]
        M01 = psum[:, 4:6, :]

        NORM = [vecs[:, 0:KT], vecs[:, KT:2 * KT]]
        LB_RAW = vecs[:, 32:48]
        WQ, WK, WO = vecs[:, 48:49], vecs[:, 49:50], vecs[:, 50:51]
        LB, ONE_LB, LOG_A, LOG_BA = small[:, 0], small[:, 1], small[:, 2], small[:, 3]
        LB_E, LB_T, LB_R = small[:, 4], small[:, 5], small[:, 6]
        WQS = small[:, 7, 1:2]

        class Carve:
            def __init__(self):
                self.at = 0

            def __call__(self, n):
                v = work[:, self.at:self.at + n]
                self.at += n
                assert self.at <= WORK, self.at
                return v

        c = Carve()
        qk_sq = c(2 * T).rearrange("p (b t) -> p b t", b=2)
        qkn = c(2 * T).rearrange("p (b t) -> p b t", b=2)
        qn, kn = qkn[:, 0], qkn[:, 1]
        gate = g_tmp = c(T)
        za = c(Z_ALL)
        v_nat = c(5 * P).rearrange("p (b d) -> p b d", b=5)
        k_nat = c(5 * P).rearrange("p (b d) -> p b d", b=5)
        past_kT = c(PAST)
        past_k = c(PAST).rearrange("p (b d) -> p b d", b=2)
        past_v = c(PAST).rearrange("p (b d) -> p b d", b=2)
        sp_hi = work_r("sp_hi", c.at, Z_ALL)
        sp_lo = work_r("sp_lo", c.at + Z_ALL, Z_ALL)
        qk_hi = work_r("qk_hi", c.at, 2 * T).rearrange("p (b t) -> p b t", b=2)
        qk_lo = work_r("qk_lo", c.at + 2 * T, 2 * T).rearrange("p (b t) -> p b t", b=2)
        v_hi, v_lo = [work_r(n, c.at + 2 * Z_ALL + i * 3 * P, 3 * P).rearrange("p (b d) -> p b d", b=3)
                      for i, n in enumerate(("v_hi", "v_lo"))]
        assert c.at + 2 * Z_ALL + 6 * P <= WORK
        c = Carve()
        r_tmp = c(2 * T).rearrange("p (b t) -> p b t", b=2)
        lse = c(T)
        cum = c(T)
        qs, kk, qe, kd = c(T), c(T), c(T), c(T)
        eb = c(T)
        gate_r = g_tmp_r = c(T)
        dl = [c(T) for _ in range(2)]
        xl = [c(T) for _ in range(2)]
        A = c(SEQ + SAMPLE)
        v_nat_r = c(5 * P).rearrange("p (b d) -> p b d", b=5)
        kd_nat = c(5 * P).rearrange("p (b d) -> p b d", b=5)
        S = c(6 * P).rearrange("p (b d) -> p b d", b=6)
        o_cp, o_sq = xl
        o_hi, o_lo = [work_r(n, (4 * 2 + 2 + i) * T, T) for i, n in enumerate(("o_hi", "o_lo"))]
        own = lse
        own_hi = work_r("own_hi", 0, T)
        own_lo = work_r("own_lo", T, T)
        pair = dl[0][:, 0:HT]
        pair_hi = work_r("pair_hi", (4 * 2 + 3) * T, HT)
        pair_lo = work_r("pair_lo", (4 * 2 + 3) * T + HT, HT)
        c = Carve()
        x_old = [c(T) for _ in range(2)]
        x_new = [c(T) for _ in range(2)]
        x_sq = c(T)
        sq_sum = c(T)
        y_nat = [c(5 * P).rearrange("p (b d) -> p b d", b=5) for _ in range(2)]
        x_more = [work[:, c.at - 2 * T + i * T:c.at - T + i * T] for i in range(2)]
        x_tmp = [c(T) for _ in range(2)]
        x_sq_b = c(T)
        x_nat_s = c(D)[0:SAMPLE]
        vec_rows = c(P)[0:51]
        tri_f = c(P)
        neg_f = c(P)
        ones_f = c(P)
        x_in = x_old + x_new + x_more
        XB = len(x_in)
        x_nat = full[:, :, :].rearrange("p a b -> p (a b)")[:, 0:NB * D].rearrange("p (b c) -> p b c", b=NB)

        x_loaded = [sem(f"x_loaded{i}") for i in range(len(X_CHUNKS) - 1)]
        x_s_loaded = sem("x_s_loaded"); vec_loaded = sem("vec_loaded")
        ident_ready = sem("ident_ready"); consts_ready = sem("consts_ready")
        vecs_turned = sem("vecs_turned"); vecs_ready = sem("vecs_ready")
        x_turned = sem("x_turned"); x_copied = sem("x_copied"); x_s_copied = sem("x_s_copied")
        x_scaled = sem("x_scaled"); x_in_stored = [sem(f"x_in_stored{i}") for i in range(XB)]
        first_scaled = sem("first_scaled")
        pool_chain = sem("pool_chain"); act_chain = sem("act_chain"); dve_chain = sem("dve_chain")
        raw_loaded = [sem(f"raw_loaded{i}") for i in range(RING)]
        hi_ready = sem("hi_ready"); lo_ready = sem("lo_ready"); half_done = sem("half_done")
        evacuated = sem("evacuated")
        act_hi_ready = sem("act_hi_ready"); act_lo_ready = sem("act_lo_ready")
        x_old_loaded = [sem("x_old_loaded0"), sem("x_old_loaded1")]
        x_stored = [sem("x_stored0"), sem("x_stored1")]
        x_squared = sem("x_squared"); x_summed = sem("x_summed")
        rms_summed = sem("rms_summed"); rstd_ready = sem("rstd_ready"); full_ready = sem("full_ready")
        y_turned = sem("y_turned"); y_copied = sem("y_copied"); y_stored = [sem("y_stored0"), sem("y_stored1")]
        past_k_loaded = sem("past_k_loaded"); past_v_loaded = sem("past_v_loaded")
        qk_squared = sem("qk_squared"); sq_hi_ready = sem("sq_hi_ready"); sq_lo_ready = sem("sq_lo_ready")
        stage_a = sem("att_sums_and_turns"); past_copied = sem("past_copied"); v_copied = sem("v_copied")
        qk_rstd = sem("qk_rstd"); qk_normed = sem("qk_normed")
        qkn_hi_ready = sem("qkn_hi_ready"); qkn_lo_ready = sem("qkn_lo_ready")
        v_hi_ready = sem("v_hi_ready"); v_lo_ready = sem("v_lo_ready")
        stage_b = sem("att_scores"); k_copied = sem("k_copied"); soft_log = sem("soft_log")
        soft = sem("softplus"); sp_hi_ready = sem("sp_hi_ready"); sp_lo_ready = sem("sp_lo_ready")
        stage_c = sem("att_cumulated"); k_last_copied = sem("k_last_copied")
        att_ready = sem("att_weights"); att_hi_ready = sem("att_hi_ready"); att_lo_ready = sem("att_lo_ready")
        stage_d = sem("att_mixed")
        gate_log = sem("gate_log"); gate_ls = sem("gate_ls"); gate_sig = sem("gate_sig"); gate_ready = sem("gate_ready")
        v_stored = sem("v_stored"); k_stored = sem("k_stored")
        o_ready = sem("o_ready")
        r_log = sem("r_log"); r_ls = sem("r_ls"); r_lse = sem("r_lse"); r_sig = sem("r_sig")
        r_kx = sem("r_kx"); r_kexp = sem("r_kexp"); r_qk = sem("r_qk"); r_cum = sem("r_cum"); r_eb = sem("r_eb")
        r_kdx = sem("r_kdx"); r_kde = sem("r_kde"); r_kd = sem("r_kd")
        r_vT = sem("r_v_turned"); r_v = sem("r_v_copied"); r_kdT = sem("r_kd_turned"); r_kdn = sem("r_kd_copied")
        r_own_prod = sem("r_own_products"); r_own_hi = sem("r_own_hi"); r_own_lo = sem("r_own_lo")
        r_own = sem("r_own_scores"); r_own_v = sem("r_own_scores_times_v")
        r_pair_prod = sem("r_pair_products"); r_pair_hi = sem("r_pair_hi"); r_pair_lo = sem("r_pair_lo")
        r_upd = sem("r_update"); r_state = sem("r_state")
        r_gls = sem("r_gate_ls"); r_glog = sem("r_gate_log"); r_gsig = sem("r_gate_sig"); r_gate = sem("r_gate")
        r_out = sem("r_out"); r_osum = sem("r_out_summed")
        r_osq = sem("r_out_squared"); r_ohi = sem("r_out_sq_hi"); r_olo = sem("r_out_sq_lo")
        r_ssq = sem("r_out_sum"); r_orstd = sem("r_out_rstd")
        s_loaded = sem("s_loaded"); s_stored = sem("s_stored")
        r_diff = sem("r_diff"); r_dexp = sem("r_dexp"); r_x = sem("r_x"); r_lev = sem("r_level_scores")
        r_put = sem("r_scores_put")

        NL = len(LEVELS)

        def added(l, n):
            return n + (l * LAYER_TILES + 4 * H + 1)

        def stored_all(l, b):
            return 16 * len(range(b, KT, (XB, 2)[l]))

        block = ctx.enter_context(nc.Block())

        w_in_v = [w_in[l].rearrange("(kh kt p) c -> kh p kt c", p=P, kt=KH) for l in range(2)]
        w_out_v = [w_out[l].rearrange("(kh kt p) c -> kh p kt c", p=P, kt=KH) for l in range(2)]
        k_prompt_v = k_prompt[0, 0].rearrange("(b p) h d -> p b h d", p=P)
        v_prompt_v = v_prompt[0, 0].rearrange("(b p) h d -> p b h d", p=P)
        past_k_v = cache_k[0, 0].rearrange("(b p) h d -> p b h d", p=P)
        past_v_v = cache_v[0, 0].rearrange("(b p) h d -> p b h d", p=P)
        y_prompt_v = y_prompt[0].rearrange("(b p) c -> p b c", p=P)

        @block.sync
        def _(sp_eng):
            xp = x_prompt[0].rearrange("(b p) c -> p b c", p=P)
            def half(g, slot, src):
                if not (isinstance(g, int) and g < RING):
                    sp_eng.wait_ge(lo_ready, g - RING + 1)
                sp_eng.dma_start(w_raw[:, slot], src).then_inc(raw_loaded[slot], 16)

            def in_half(l, h, u):
                half(h * HEAD_HALVES + (l * LAYER_HALVES + u), u % RING,
                     w_in_v[l][u % 2][:, :, bass.ds(h * P + (u // 2) * D, P)])

            def first_half(u):
                half(u, u, w_in_v[0][u // 2][:, :, (u % 2) * D:(u % 2) * D + P])

            def load_x(q):
                cols = slice(X_CHUNKS[q] * P, X_CHUNKS[q + 1] * P)
                sp_eng.dma_start(x_nat[:, :, cols], xp[:, :, cols]).then_inc(x_loaded[q], 16)

            sp_eng.dma_start(vec_rows[0:32, :], norm_w.rearrange("l (k p) -> (l k) p", p=P)).then_inc(vec_loaded, 16)
            sp_eng.dma_start(vec_rows[32:48, :], hgrn_lb.rearrange("l (k p) -> (l k) p", p=P)).then_inc(vec_loaded, 16)
            sp_eng.dma_start(vec_rows[48:49, :], q_norm_w).then_inc(vec_loaded, 16)
            sp_eng.dma_start(vec_rows[49:50, :], k_norm_w).then_inc(vec_loaded, 16)
            sp_eng.dma_start(vec_rows[50:51, :], hgrn_norm_w).then_inc(vec_loaded, 16)
            load_x(0)
            sp_eng.dma_start(x_nat_s, x_sample[0]).then_inc(x_s_loaded, 16)
            for u in range(2):
                first_half(u)
                load_x(u + 1)
            sp_eng.wait_ge(x_copied, 1)
            load_x(3)
            sp_eng.wait_ge(x_copied, 3)
            first_half(2)
            load_x(4)
            sp_eng.wait_ge(x_copied, 5)
            first_half(3)
            for l in range(2):
                for u in range(4 if l == 0 else 0, HEAD_HALVES):
                    in_half(l, 0, u)
                with sp_eng.Fori(1, H) as h:
                    for u in range(HEAD_HALVES):
                        in_half(l, h, u)
                out0 = l * LAYER_HALVES + IN_HALVES

                def out_pair(i, first):
                    for u in range(4):
                        half(i * 4 + (out0 + u), u, w_out_v[l][u // 2][:, :, bass.ds(i * (2 * P) + (u % 2) * P, P)])
                    for par in range(2):
                        if first:
                            if par == 0:
                                sp_eng.wait_ge(qk_normed if l == 0 else r_own, H)
                            if par == 0:
                                for b, stored in enumerate((x_in_stored, x_stored)[l]):
                                    sp_eng.wait_ge(stored, stored_all(l, b))
                        else:
                            sp_eng.wait_ge(evacuated, added(l, i * 2 + (par - 2)))
                        sp_eng.dma_start(x_old[par], x_residual[bass.ds(i * 2 + par, 1)].rearrange("a p t -> (a p) t")
                                         ).then_inc(x_old_loaded[par], 16)
                out_pair(0, True)
                with sp_eng.Fori(1, KT // 2) as i:
                    out_pair(i, False)
            sp_eng.wait_ge(v_stored, 32 * H)
            sp_eng.wait_ge(k_stored, 32 * H)
            sp_eng.wait_ge(s_stored, 32 * H)
            for par in range(2):
                sp_eng.wait_ge(y_stored[par], 32 * (KT // 2))
                sp_eng.wait_ge(x_stored[par], 16 * (KT // 2))

        @block.gpsimd
        def _(pool):
            ch = Chain(pool, pool_chain)
            ch.done(pool.memset(ident[:], 0.0))
            ch.wait()
            pool.affine_select(out=ident[:], in_=ident[:], pattern=[[-1, P]], base=0, channel_multiplier=1,
                               compare_op=ALU.not_equal, fill=1.0).then_inc(ident_ready, 1)
            ch.done(pool.memset(eps[:], EPS))
            ch.done(pool.memset(one_c[:], 1.0))
            ch.done(pool.memset(ones_f, 1.0))
            ch.done(pool.memset(neg_f, -1.0))
            ch.done(pool.memset(hide[:], 0.0))
            ch.done(pool.memset(hide_last[:], 0.0))
            ch.done(pool.memset(level_mask[:], 1.0))
            ch.done(pool.memset(run_on[:], 1.0))
            ch.done(pool.memset(sq_sum, 0.0))
            ch.wait()
            ch.done(pool.memset(run_on[:, 0:T:P], 0.0))
            ch.done(pool.affine_select(out=tri_f, in_=neg_f, pattern=[[-1, P]], base=0,
                                       channel_multiplier=1, compare_op=ALU.is_ge, fill=0.0))
            ch.done(pool.affine_select(out=hide[:], in_=hide[:], pattern=[[1, P]], base=0, channel_multiplier=-1,
                                       compare_op=ALU.is_gt, fill=MASKED))
            ch.done(pool.affine_select(out=hide_last[:], in_=hide_last[:], pattern=[[0, SAMPLE]], base=-SROW,
                                       channel_multiplier=1, compare_op=ALU.is_ge, fill=MASKED))
            ch.wait()
            ch.done(pool.affine_select(out=hide_last[:], in_=hide_last[:], pattern=[[1, SAMPLE]], base=SROW,
                                       channel_multiplier=-1, compare_op=ALU.is_gt, fill=MASKED))
            for m in LEVELS:
                v = level_mask[:, MASK_COL[m]:MASK_COL[m] + 64].rearrange("p (b j) -> p b j", j=m)
                ch.done(pool.affine_select(out=v, in_=v, pattern=[[-2 * m, 64 // m], [0, m]], base=0,
                                           channel_multiplier=1, compare_op=ALU.is_ge, fill=0.0))
                ch.wait()
                ch.done(pool.affine_select(out=v, in_=v, pattern=[[2 * m, 64 // m], [0, m]], base=m - 1,
                                           channel_multiplier=-1, compare_op=ALU.is_ge, fill=0.0))
                ch.wait()
            pool.wait_ge(ident_ready, 1)
            ch.done(pool.tensor_copy(neg_tri[:], tri_f))
            ch.done(pool.tensor_copy(neg_ones[:], neg_f))
            ch.done(pool.tensor_copy(ones_r[:], ones_f))
            pool.tensor_copy(ident_b[:], ident[:]).then_inc(consts_ready, 1)

            def add_squares(n, squares):
                pool.wait_ge(x_squared, n + 1)
                if not (isinstance(n, int) and n == 0):
                    pool.wait_ge(x_summed, n)
                pool.tensor_tensor(sq_sum, sq_sum, squares, ALU.add).then_inc(x_summed, 1)

            for n in range(KT):
                add_squares(n, (x_sq, x_sq_b)[n % 2])

            def split_last(l):
                base = (2 * l + 1) * KT
                for k in range(DVE_SPLITS, KT - 1):
                    pool.wait_ge(act_hi_ready, base + k + 1)
                    pool.wait_ge(act_lo_ready, base + k)
                    pool.tensor_tensor(act_lo[:, k, :], full[:, k, :], act_hi[:, k, :].bitcast(F32), ALU.subtract
                                       ).then_inc(act_lo_ready, 1)

            split_last(0)
            pool.wait_ge(o_ready, H)
            ch.done(pool.memset(sq_sum, 0.0))
            ch.wait()
            with pool.Fori(0, KT) as i:
                add_squares(i + KT, x_sq)
            split_last(1)

        @block.tensor
        def _(pe):
            def turn(out, in_, n=P, **kw):
                return pe.matmul(out, in_, ident[0:n, 0:n], is_transpose=True, start=True, stop=True, **kw)

            def part(slot, par, ks, wait_act=None):
                for k in ks:
                    if wait_act is not None:
                        pe.wait_ge(act_lo_ready, wait_act + k + 1)
                    for n, (w, a) in enumerate(((w_hi, act_hi), (w_hi, act_lo), (w_lo, act_hi))):
                        for j in range(2):
                            mm = pe.matmul(acc[par][:, j, :], w[:, slot, k % KH, :], a[:, k, j * HT:(j + 1) * HT],
                                           start=(k == 0 and n == 0), stop=(k == KT - 1 and n == 2))
                return mm

            def half_ready(g, t, kh):
                pe.wait_ge(lo_ready, g + 1)
                if kh == 0 and not (isinstance(t, int) and t < 2):
                    pe.wait_ge(evacuated, t - 1)

            def half(g, slot, t, par, kh, wait_act=None):
                half_ready(g, t, kh)
                part(slot, par, range(kh * KH, (kh + 1) * KH), wait_act).then_inc(half_done, 1)

            def in_half(l, h, u, wait_act=None):
                half(h * HEAD_HALVES + (l * LAYER_HALVES + u), u % RING, h * 4 + (l * LAYER_TILES + u // 2),
                     (u // 2) % 2, u % 2, wait_act)

            def att_sums_and_turns(h):
                pe.wait_ge(sq_lo_ready, h + 1)
                pe.wait_ge(evacuated, h * 4 + 3)
                pe.wait_ge(past_k_loaded, (h + 1) * 16)
                if not (isinstance(h, int) and h == 0):
                    pe.wait_ge(o_ready, h)
                for b in range(2):
                    pe.matmul(M[b], ones_r[:], qk_hi[:, b, 0:SEQ], start=True, stop=False)
                    pe.matmul(M[b], ones_r[:], qk_lo[:, b, 0:SEQ], start=False, stop=True)
                out = M[2][:, 0:2 * SAMPLE].rearrange("p (b t) -> p b t", b=2)
                pe.matmul(out, ones_r[:], qk_hi[:, :, SEQ:T], start=True, stop=False)
                pe.matmul(out, ones_r[:], qk_lo[:, :, SEQ:T], start=False, stop=True)
                turn(M[2][:, 64:192], Y[:, 2, LAST:T])
                for b in range(2):
                    turn(M[2][:, 192 + b * P:192 + (b + 1) * P], past_k[:, b, :])
                for b in range(NB):
                    mm = turn(M[3][:, b * P:(b + 1) * P], Y[:, 2, b * P:(b + 1) * P])
                mm.then_inc(stage_a, 1)

            def att_scores(h):
                pe.wait_ge(qkn_lo_ready, h + 1)
                pe.wait_ge(v_copied, h + 1)
                pe.wait_ge(past_copied, h + 1)
                for b in range(3):
                    for n, (k_, q_) in enumerate(((qk_hi, qk_hi), (qk_hi, qk_lo), (qk_lo, qk_hi))):
                        pe.matmul(M[b][:, 0:Z_LEN[b]], k_[:, 1, b * P:(b + 1) * P], q_[:, 0, b * P:SEQ],
                                  start=(n == 0), stop=False, skip_group_check=True)
                pe.matmul(M[2][:, 256:384], kn[:, 3 * P:SEQ], qn[:, 3 * P:SEQ], start=False, stop=False,
                          skip_group_check=True)
                for b in range(2):
                    pe.matmul(M[2][:, 384 + b * SAMPLE:384 + (b + 1) * SAMPLE], past_kT[:, b * P:(b + 1) * P],
                              qn[:, SEQ:T], start=False, stop=True, skip_group_check=True)
                pe.matmul(M[2][:, 448:480], kn[:, LAST:T], qn[:, SEQ:T], start=False, stop=False,
                          skip_group_check=True)
                for out, mask in ((M[0][:, 0:P], hide[:]), (M[1][:, 0:P], hide[:]), (M[2][:, 0:P], hide[:]),
                                  (M[2][:, 256:384], hide[:]), (M[2][:, 448:480], hide_last[:])):
                    pe.matmul(out, ident_b[:], mask, start=False, stop=True, skip_group_check=True)
                for b in range(NB):
                    mm = turn(M[3][:, b * P:(b + 1) * P], kn[:, b * P:(b + 1) * P])
                mm.then_inc(stage_b, 1)

            def att_cumulated(h):
                pe.wait_ge(sp_lo_ready, h + 1)
                pe.wait_ge(k_copied, h + 1)
                turn(M[3][:, 0:P], kn[:, LAST:T])
                for part_ in (sp_hi, sp_lo):
                    for out, at in ((M[0], 0), (M[1][:, 0:384], 512), (M[2][:, 0:480], 896)):
                        pe.matmul(out, neg_tri[:], part_[:, at:at + out.shape[-1]], start=False, stop=True,
                                  skip_group_check=True)
                for part_ in (sp_hi, sp_lo):
                    for b in range(NB):
                        for later in range(b + 1, NB):
                            pe.matmul(M[b][:, (later - b) * P:Z_LEN[b]], neg_ones[:],
                                      part_[:, Z_COL[later]:Z_COL[later] + Z_LEN[later]], start=False, stop=True,
                                      skip_group_check=True)
                    pe.matmul(M[2][:, 384:448], neg_ones[:], part_[:, Z_PAST1:Z_ALL], start=False, stop=True,
                              skip_group_check=True)
                    mm = pe.matmul(M[2][:, 384:416], neg_ones[:], part_[:, Z_NEW:Z_ALL], start=False, stop=True,
                                   skip_group_check=True)
                mm.then_inc(stage_c, 1)

            def att_mixed(h):
                pe.wait_ge(att_lo_ready, h + 1)
                pe.wait_ge(k_last_copied, h + 1)
                pe.wait_ge(past_v_loaded, (h + 1) * 16)
                pe.wait_ge(v_lo_ready, h + 1)
                for b in range(3):
                    for n, (v_, w_) in enumerate(((v_hi, sp_hi), (v_hi, sp_lo), (v_lo, sp_hi))):
                        pe.matmul(M[3][:, b * P:SEQ], v_[:, b, :], w_[:, Z_COL[b]:Z_COL[b] + Z_LEN[b]],
                                  start=(b == 0 and n == 0), stop=False, skip_group_check=True)
                pe.matmul(M[3][:, 3 * P:SEQ], v_nat[:, 3, :], za[:, Z_COL[3]:Z_COL[3] + P], start=False, stop=True,
                          skip_group_check=True)
                out = M[1][:, 384:384 + SAMPLE]
                pe.matmul(out, past_v[:, 0, :], za[:, Z_PAST0:Z_PAST0 + SAMPLE], start=True, stop=False)
                pe.matmul(out, past_v[:, 1, :], za[:, Z_PAST1:Z_PAST1 + SAMPLE], start=False, stop=False)
                pe.matmul(out, v_nat[:, 4, :], za[:, Z_NEW:Z_NEW + SAMPLE], start=False, stop=True).then_inc(stage_d, 1)

            def rec_turn_v(h):
                pe.wait_ge(evacuated, h * 4 + (LAYER_TILES + 3))
                if not (isinstance(h, int) and h == 0):
                    pe.wait_ge(r_osq, h)
                for b in range(NB):
                    turn(M[3][:, b * P:(b + 1) * P], Y[:, 2, b * P:(b + 1) * P])
                turn(M[2][:, 0:P], Y[:, 2, LAST:T]).then_inc(r_vT, 1)

            def rec_level(h, i, bank):
                m = LEVELS[i]
                pe.wait_ge(r_x, h * NL + (i + 1))
                x = xl[i % 2]
                for b in range(NB):
                    rhs = x[:, b * P:(b + 1) * P].rearrange("p (b j) -> p b j", j=2 * m)[:, :, m:2 * m]
                    mm = pe.matmul(M[bank][:, b * 64:(b + 1) * 64], x[:, b * P:(b + 1) * P], rhs,
                                   start=True, stop=True)
                if m <= SAMPLE // 2:
                    rhs = x[:, SEQ:T].rearrange("p (b j) -> p b j", j=2 * m)[:, :, m:2 * m]
                    mm = pe.matmul(M[bank][:, 256:256 + SAMPLE // 2], x[:, LAST:T], rhs, start=True, stop=True)
                mm.then_inc(r_lev, 1)

            def rec_stage(h, u):
                if u == 0:
                    if not (isinstance(h, int) and h == 0):
                        pe.wait_ge(r_orstd, h)
                    rec_level(h, 0, 1)
                elif u == 1:
                    pe.wait_ge(r_kd, h + 1)
                    pe.wait_ge(r_v, h + 1)
                    for b in range(NB):
                        turn(M[3][:, b * P:(b + 1) * P], kd[:, b * P:(b + 1) * P])
                    turn(M[2][:, 0:P], kd[:, LAST:T]).then_inc(r_kdT, 1)
                    rec_level(h, 1, 0)
                elif u == 2:
                    pe.wait_ge(r_kdn, h + 1)
                    for b in range(NB):
                        pe.matmul(M[3][:, b * P:(b + 1) * P], kd_nat[:, b, :], v_nat_r[:, b, :], start=True, stop=True)
                    pe.matmul(M[2][:, 0:P], kd_nat[SROW:P, 4, :], v_nat_r[SROW:P, 4, :], start=True, stop=True
                              ).then_inc(r_upd, 1)
                    pe.wait_ge(r_put, h * NL + 1)
                    rec_level(h, 2, 1)
                    pe.wait_ge(r_own_lo, h + 1)
                    pe.wait_ge(r_put, h * NL + 2)
                    pe.matmul(M[0], ones_r[:], own_hi[:, 0:SEQ], start=True, stop=False)
                    pe.matmul(M[0], ones_r[:], own_lo[:, 0:SEQ], start=False, stop=True)
                    pe.matmul(M[2][:, P:P + SAMPLE], ones_r[:], own_hi[:, SEQ:T], start=True, stop=False)
                    pe.matmul(M[2][:, P:P + SAMPLE], ones_r[:], own_lo[:, SEQ:T], start=False, stop=True
                              ).then_inc(r_own, 1)
                elif u == 3:
                    pe.wait_ge(r_own_v, h + 1)
                    rec_level(h, 3, 0)
                    pe.wait_ge(r_put, h * NL + 3)
                    rec_level(h, 4, 1)
                elif u == 4:
                    pe.wait_ge(r_put, h * NL + 4)
                    rec_level(h, 5, 0)
                elif u == 5:
                    pe.wait_ge(r_put, h * NL + (NL - 1))
                    pe.wait_ge(r_state, h + 1)
                    for b in range(NB):
                        out = M[3][:, b * P:(b + 1) * P]
                        pe.matmul(out, v_nat_r[:, b, :], A[:, b * P:(b + 1) * P], start=True, stop=(b == 0))
                        if b:
                            pe.matmul(out, S[:, b, :], qe[:, b * P:(b + 1) * P], start=False, stop=True)
                    out = M[2][:, 0:SAMPLE]
                    pe.matmul(out, v_nat_r[:, 4, :], A[:, SEQ:T], start=True, stop=False)
                    pe.matmul(out, S[:, 0, :], qe[:, SEQ:T], start=False, stop=True).then_inc(r_out, 1)
                    pe.wait_ge(r_pair_lo, h + 1)
                    pe.matmul(M[1][:, 0:HT], ones_r[:], pair_hi, start=True, stop=False)
                    pe.matmul(M[1][:, 0:HT], ones_r[:], pair_lo, start=False, stop=True).then_inc(r_lev, 1)
                elif u == 6:
                    pe.wait_ge(r_olo, h + 1)
                    pe.matmul(M[0], ones_r[:], o_hi[:, 0:SEQ], start=True, stop=False)
                    pe.matmul(M[0], ones_r[:], o_lo[:, 0:SEQ], start=False, stop=True)
                    pe.matmul(M[1][:, 0:SAMPLE], ones_r[:], o_hi[:, SEQ:T], start=True, stop=False)
                    pe.matmul(M[1][:, 0:SAMPLE], ones_r[:], o_lo[:, SEQ:T], start=False, stop=True).then_inc(r_ssq, 1)

            def mixer_stage(l, h, u):
                if l == 0:
                    if u == 1:
                        att_scores(h)
                    elif u == 4:
                        att_cumulated(h)
                    elif u == 6:
                        att_mixed(h)
                else:
                    rec_stage(h, u)

            def first_stage(l, h):
                if l == 0:
                    att_sums_and_turns(h)
                else:
                    rec_turn_v(h)

            pe.wait_ge(ident_ready, 1)
            pe.wait_ge(vec_loaded, 16 * 5)
            turn(M[0][:, 0:51], vec_rows, n=51).then_inc(vecs_turned, 1)

            def start_turn(k):
                if k in X_CHUNKS:
                    pe.wait_ge(x_loaded[X_CHUNKS.index(k)], 16)
                if k == 1:
                    pe.wait_ge(vecs_ready, 1)
                if k >= 2:
                    pe.wait_ge(x_copied, k - 1)
                    pe.wait_ge(x_s_copied, k - 1)
                at = 6 - 2 * (k % 2)
                for b in range(NB):
                    turn(psum[:, at, b * P:(b + 1) * P], x_nat[:, b, k * P:(k + 1) * P])
                if k == 0:
                    pe.wait_ge(x_s_loaded, 16)
                turn(psum[:, at + 1, 0:SAMPLE], x_nat_s[:, k * P:(k + 1) * P], n=SAMPLE).then_inc(x_turned, 1)

            LAG = 3
            for k in range(KT + LAG):
                if k < KT:
                    start_turn(k)
                if k >= LAG:
                    f = k - LAG
                    for par in range(2):
                        if f % KH == 0:
                            half_ready(par + 2 * (f // KH), par, f // KH)
                        mm = part(par + 2 * (f // KH), par, [f], 0)
                        if f % KH == KH - 1:
                            mm.then_inc(half_done, 1)

            def rms_sum(l):
                pe.wait_ge(x_summed, (l + 1) * KT)
                pe.matmul(M[0], ones, sq_sum[:, 0:SEQ], start=True, stop=True)
                pe.matmul(M[1][:, 0:SAMPLE], ones, sq_sum[:, SEQ:T], start=True, stop=True).then_inc(rms_summed, 1)

            for l in range(2):
                if l == 0:
                    pe.wait_ge(x_copied, KT)
                    pe.wait_ge(x_s_copied, KT)
                    pe.wait_ge(consts_ready, 1)
                    rms_sum(0)
                for u in range(0 if l else 4, HEAD_HALVES):
                    in_half(l, 0, u, 2 * KT if u < 2 else None)
                    if u == 2:
                        rms_sum(1)
                first_stage(l, 0)
                with pe.Fori(0, H - 1) as h:
                    for u in range(HEAD_HALVES):
                        in_half(l, h + 1, u)
                        mixer_stage(l, h, u)
                    first_stage(l, h + 1)

                g0, t0, w0 = l * LAYER_HALVES + IN_HALVES, l * LAYER_TILES + 4 * H, (2 * l + 1) * KT
                for u in range(-1, 7):
                    if u >= 0:
                        mixer_stage(l, H - 1, u)
                    for k in LAST_FILL[l][u]:
                        for par in range(2):
                            if k % KH == 0:
                                half_ready(g0 + par + 2 * (k // KH), t0 + par, k // KH)
                            mm = part(par + 2 * (k // KH), par, [k], w0)
                            if k == KH - 1:
                                mm.then_inc(half_done, 1)
                for par in range(2):
                    part(2 + par, par, [KT - 1], w0).then_inc(half_done, 1)

                def out_pair(l, i):
                    for u in range(4):
                        half(i * 4 + (l * LAYER_HALVES + IN_HALVES + u), u, i * 2 + (l * LAYER_TILES + 4 * H + u % 2),
                             u % 2, u // 2)
                        if l == 1 and u < 2:
                            turn_y(i * 2 + (u - 2), u)

                def turn_y(n, par):
                    pe.wait_ge(evacuated, added(1, n))
                    if not (isinstance(n, int) and n == 0):
                        pe.wait_ge(y_copied, n)
                    for b in range(NB):
                        turn(M[0][:, b * P:(b + 1) * P], x_new[par][:, b * P:(b + 1) * P])
                    turn(M[1][:, 0:P], x_new[par][:, LAST:T]).then_inc(y_turned, 1)

                with pe.Fori(1, KT // 2) as i:
                    out_pair(l, i)
                if l == 1:
                    turn_y(KT - 2, 0)
                    turn_y(KT - 1, 1)

        @block.scalar
        def _(act):
            ch = Chain(act, act_chain)
            nc.scalar.preload_act_table_set("natural_log_exp_and_others")

            def func(out, in_, f, **kw):
                return nc.scalar.activation(out, in_, f, **kw)

            def hi(g, slot):
                if not (isinstance(g, int) and g < RING):
                    act.wait_ge(half_done, g - RING + 1)
                act.wait_ge(raw_loaded[slot], raw_count(g, slot))
                func(w_hi[:, slot], w_raw[:, slot], ACT.Copy).then_inc(hi_ready, 1)

            def raw_count(g, slot):
                if isinstance(g, int):
                    return 16 * (g // RING + 1)
                return (g - slot) * 4 + 16

            def split_ahead(l, h, u):
                g = h * HEAD_HALVES + (l * LAYER_HALVES + u + AHEAD)
                hi(g, (u + AHEAD) % RING)

            def act_split(ks):
                for k in ks:
                    func(act_hi[:, k, :], full[:, k, :], ACT.Copy).then_inc(act_hi_ready, 1)

            def att_square(h):
                act.wait_ge(evacuated, h * 4 + 2)
                if not (isinstance(h, int) and h == 0):
                    act.wait_ge(qk_normed, h)
                func(qk_sq, Y[:, 0:2, :], ACT.Square).then_inc(qk_squared, 1)
                func(qk_hi, Y[:, 0:2, :], ACT.Square).then_inc(sq_hi_ready, 1)

            def att_load_past_k(h):
                act.dma_start(past_k, past_k_v[:, :, bass.ds(h, 1), :].rearrange("p b h d -> p b (h d)")).then_inc(past_k_loaded, 16)

            def att_load_past_v(h):
                act.dma_start(past_v, past_v_v[:, :, bass.ds(h, 1), :].rearrange("p b h d -> p b (h d)")).then_inc(past_v_loaded, 16)

            def att_act(h, u):
                if u == 0:
                    act.wait_ge(stage_a, h + 1)
                    ch.done(func(qk_sq[:, :, 0:SEQ], M01, ACT.Ln, scale=1.0 / P, bias=eps[:]))
                    ch.done(func(qk_sq[:, :, SEQ:T], M[2][:, 0:2 * SAMPLE].rearrange("p (b t) -> p b t", b=2), ACT.Ln,
                                 scale=1.0 / P, bias=eps[:]))
                    func(past_kT, M[2][:, 192:448], ACT.Copy).then_inc(past_copied, 1)
                    ch.wait()
                    func(qk_sq, qk_sq, ACT.Exp, scale=-0.5).then_inc(qk_rstd, 1)
                    act.wait_ge(evacuated, h * 4 + 4)
                    ch.done(func(g_tmp, Y[:, 3, :], ACT.Abs))
                    ch.wait()
                    ch.done(func(g_tmp, g_tmp, ACT.Exp, scale=-1.0))
                    act.wait_ge(qk_normed, h + 1)
                    func(qk_hi, qkn, ACT.Copy).then_inc(qkn_hi_ready, 1)
                    ch.wait()
                    func(g_tmp, g_tmp, ACT.Ln, bias=one_c[:]).then_inc(gate_log, 1)
                elif u == 1:
                    act.wait_ge(gate_ls, h + 1)
                    func(g_tmp, g_tmp, ACT.Exp).then_inc(gate_sig, 1)
                    act.wait_ge(v_copied, h + 1)
                    if not (isinstance(h, int) and h == 0):
                        act.wait_ge(stage_d, h)
                    func(v_hi, v_nat[:, 0:3, :], ACT.Copy).then_inc(v_hi_ready, 1)
                elif u == 2:
                    act.wait_ge(stage_b, h + 1)
                    ch.done(func(za[:, 0:512], M[0], ACT.Abs))
                    ch.done(func(za[:, 512:896], M[1][:, 0:384], ACT.Abs))
                    ch.done(func(za[:, 896:Z_ALL], M[2][:, 0:480], ACT.Abs))
                    if not (isinstance(h, int) and h == 0):
                        act.wait_ge(k_stored, h * 32)
                    func(k_nat[:, 0:NB, :], M[3].rearrange("p (b d) -> p b d", b=NB), ACT.Copy).then_inc(k_copied, 1)
                    ch.wait()
                    ch.done(func(za, za, ACT.Exp, scale=-1.0))
                    ch.wait()
                    func(za, za, ACT.Ln, bias=one_c[:]).then_inc(soft_log, 1)
                elif u == 3:
                    act.wait_ge(v_copied, h + 1)
                    act.dma_start(v_prompt_v[:, :, bass.ds(h, 1), :].rearrange("p b h d -> p b (h d)"), v_nat[:, 0:NB, :]).then_inc(v_stored, 16)
                    act.dma_start(v_sample[0, 0][:, bass.ds(h, 1), :].rearrange("p h d -> p (h d)"), v_nat[SROW:P, 4, :]).then_inc(v_stored, 16)
                    act.wait_ge(soft, h + 1)
                    func(sp_hi, za, ACT.Copy).then_inc(sp_hi_ready, 1)
                elif u == 5:
                    act.wait_ge(stage_c, h + 1)
                    ch.done(func(za[:, 0:512], M[0], ACT.Exp))
                    ch.done(func(za[:, 512:896], M[1][:, 0:384], ACT.Exp))
                    func(za[:, 896:Z_ALL], M[2][:, 0:480], ACT.Exp).then_inc(att_ready, 1)
                    ch.wait()
                    act.wait_ge(att_ready, h + 1)
                    func(sp_hi, za, ACT.Copy).then_inc(att_hi_ready, 1)
                    func(k_nat[:, 4, :], M[3][:, 0:P], ACT.Copy).then_inc(k_last_copied, 1)
                elif u == 6:
                    act.wait_ge(k_copied, h + 1)
                    act.wait_ge(k_last_copied, h + 1)
                    act.dma_start(k_prompt_v[:, :, bass.ds(h, 1), :].rearrange("p b h d -> p b (h d)"), k_nat[:, 0:NB, :]).then_inc(k_stored, 16)
                    act.dma_start(k_sample[0, 0][:, bass.ds(h, 1), :].rearrange("p h d -> p (h d)"), k_nat[SROW:P, 4, :]).then_inc(k_stored, 16)

            def att_next(h, u):
                if u == 2:
                    act.wait_ge(stage_a, h)
                    att_load_past_k(h)
                elif u == 7:
                    act.wait_ge(stage_d, h)
                    att_square(h)
                    att_load_past_v(h)

            def rec_next(h, u):
                if u == 5:
                    act.wait_ge(evacuated, h * 4 + (LAYER_TILES + 2))
                    ch.done(func(r_tmp, Y[:, 0:2, :], ACT.Abs))
                    ch.wait()
                    ch.done(func(r_tmp, r_tmp, ACT.Exp, scale=-1.0))
                    ch.wait()
                    func(r_tmp, r_tmp, ACT.Ln, bias=one_c[:]).then_inc(r_log, 1)
                elif u == 6:
                    act.wait_ge(r_ls, h + 1)
                    ch.done(func(lse, r_tmp[:, 1], ACT.Abs, bias=LOG_BA[:, bass.ds(h, 1)]))
                    ch.wait()
                    ch.done(func(lse, lse, ACT.Exp, scale=-1.0))
                    ch.wait()
                    func(lse, lse, ACT.Ln, bias=one_c[:]).then_inc(r_lse, 1)
                    func(r_tmp[:, 0], r_tmp[:, 0], ACT.Exp).then_inc(r_sig, 1)
                    act.wait_ge(r_kx, h + 1)
                    func(kk, kk, ACT.Exp).then_inc(r_kexp, 1)

            def level_exp(h, i):
                n = T if LEVELS[i] <= SAMPLE // 2 else SEQ
                act.wait_ge(r_diff, h * NL + (i + 1))
                func(dl[i % 2][:, 0:n], dl[i % 2][:, 0:n], ACT.Exp).then_inc(r_dexp, 1)

            def rec_act(h, u):
                if u == 0:
                    act.wait_ge(r_vT, h + 1)
                    ch.done(func(v_nat_r[:, 0:NB, :], M[3].rearrange("p (b d) -> p b d", b=NB), ACT.Copy))
                    func(v_nat_r[:, 4, :], M[2][:, 0:P], ACT.Copy).then_inc(r_v, 1)
                elif u == 1:
                    act.wait_ge(r_own_prod, h + 1)
                    func(own_hi, own, ACT.Copy).then_inc(r_own_hi, 1)
                    act.wait_ge(evacuated, h * 4 + (LAYER_TILES + 4))
                    ch.done(func(g_tmp_r, Y[:, 3, :], ACT.Abs))
                    ch.wait()
                    ch.done(func(g_tmp_r, g_tmp_r, ACT.Exp, scale=-1.0))
                    ch.wait()
                    func(g_tmp_r, g_tmp_r, ACT.Ln, bias=one_c[:]).then_inc(r_glog, 1)
                    level_exp(h, 2)
                elif u == 2:
                    act.wait_ge(r_kdT, h + 1)
                    ch.done(func(kd_nat[:, 0:NB, :], M[3].rearrange("p (b d) -> p b d", b=NB), ACT.Copy))
                    func(kd_nat[:, 4, :], M[2][:, 0:P], ACT.Copy).then_inc(r_kdn, 1)
                    level_exp(h, 3)
                    act.wait_ge(r_gls, h + 1)
                    func(g_tmp_r, g_tmp_r, ACT.Exp).then_inc(r_gsig, 1)
                elif u == 3:
                    level_exp(h, 4)
                    level_exp(h, 5)
                elif u == 4:
                    level_exp(h, 6)
                    act.wait_ge(r_pair_prod, h + 1)
                    func(pair_hi, pair, ACT.Copy).then_inc(r_pair_hi, 1)
                    act.wait_ge(r_state, h + 1)
                    act.dma_start(s_prompt[0, 0][bass.ds(h, 1)].rearrange("h a b -> (h a) b"), S[:, NB, :]).then_inc(s_stored, 16)
                    act.dma_start(s_sample[0, 0][bass.ds(h, 1)].rearrange("h a b -> (h a) b"), S[:, 5, :]).then_inc(s_stored, 16)
                elif u == 6:
                    act.wait_ge(r_osum, h + 1)
                    func(o_sq, o_cp, ACT.Square).then_inc(r_osq, 1)
                    func(o_hi, o_cp, ACT.Square).then_inc(r_ohi, 1)

            def rec_decays(h):
                level_exp(h, 0)
                act.wait_ge(r_kdx, h + 1)
                func(kd, kd, ACT.Exp).then_inc(r_kde, 1)
                level_exp(h, 1)
                act.wait_ge(r_cum, h + 1)
                func(eb, cum, ACT.Exp).then_inc(r_eb, 1)

            def rec_norm(h):
                act.wait_ge(r_ssq, h + 1)
                act.wait_ge(r_olo, h + 1)
                ch.done(func(o_sq[:, 0:SEQ], M[0], ACT.Ln, scale=1.0 / P, bias=eps[:]))
                ch.done(func(o_sq[:, SEQ:T], M[1][:, 0:SAMPLE], ACT.Ln, scale=1.0 / P, bias=eps[:]))
                ch.wait()
                func(o_sq, o_sq, ACT.Exp, scale=-0.5).then_inc(r_orstd, 1)

            def load_state(h):
                act.dma_start(S[:, 0, :], state_hgrn[0, 0][bass.ds(h, 1)].rearrange("h a b -> (h a) b")).then_inc(s_loaded, 16)

            act.wait_ge(vecs_ready, 1)
            ch.done(func(LB_E, LB_T, ACT.Exp))
            for k in range(KT + 1):
                if k < KT:
                    act.wait_ge(x_turned, k + 1)
                    if k >= XB:
                        act.wait_ge(x_in_stored[k % XB], 16 * (k // XB))
                        act.wait_ge(x_scaled, k - XB + 1)
                        act.wait_ge(x_squared, k - XB + 1)
                    func(x_in[k % XB][:, 0:SEQ], psum[:, 6 - 2 * (k % 2), :], ACT.Copy).then_inc(x_copied, 1)
                if k:
                    act.wait_ge(x_scaled, k)
                    func(act_hi[:, k - 1, :], x_tmp[(k - 1) % 2], ACT.Copy).then_inc(act_hi_ready, 1)
                if k in START_SPLITS:
                    g = START_SPLITS.index(k)
                    hi(g, g % RING)
                if k < KT:
                    act.wait_ge(x_copied, k + 1)
                    act.wait_ge(x_s_copied, k + 1)
                    act.dma_start(x_residual[k], x_in[k % XB]).then_inc(x_in_stored[k % XB], 16)
                    if k >= 2:
                        act.wait_ge(x_summed, k - 1)
                    func((x_sq, x_sq_b)[k % 2], x_in[k % XB], ACT.Square).then_inc(x_squared, 1)
            hi(6, 2)
            act.wait_ge(vecs_ready, 2)
            ch.done(func(LOG_A, LB_R, ACT.Ln))
            ch.done(func(LOG_BA, ONE_LB, ACT.Ln))
            act.wait_ge(consts_ready, 1)

            def rms(l):
                act.wait_ge(rms_summed, l + 1)
                for b, stored in enumerate((x_in_stored, x_stored)[l]):
                    act.wait_ge(stored, stored_all(l, b))
                if l:
                    act.wait_ge(evacuated, LAYER_TILES)
                ch.done(func(rstd_x[:, 0:SEQ], M[0], ACT.Ln, scale=1.0 / D, bias=eps[:]))
                ch.done(func(rstd_x[:, SEQ:T], M[1][:, 0:SAMPLE], ACT.Ln, scale=1.0 / D, bias=eps[:]))
                ch.wait()
                func(rstd_x[:], rstd_x[:], ACT.Exp, scale=-0.5).then_inc(rstd_ready, 1)

            for l in range(2):
                if l == 1:
                    act.wait_ge(full_ready, KT)
                    act_split(range(2, KT))
                if l == 0:
                    rms(0)
                    att_load_past_k(0)
                    att_load_past_v(0)
                for u in range(0 if l else 4, HEAD_HALVES):
                    split_ahead(l, 0, u)
                    if u == 2:
                        rms(1)
                        load_state(0)
                    if l == 0 and u == 7:
                        act.wait_ge(first_scaled, 1)
                        att_square(0)
                    elif l == 1 and u >= 5:
                        rec_next(0, u)
                if l == 1:
                    rec_decays(0)
                with act.Fori(0, H - 1) as h:
                    ch.enter(h, 10)
                    for u in range(HEAD_HALVES):
                        split_ahead(l, h + 1, u)
                        if l == 0:
                            att_act(h, u)
                            att_next(h + 1, u)
                        else:
                            rec_act(h, u)
                            if u == 7:
                                rec_norm(h)
                                load_state(h + 1)
                            rec_next(h + 1, u)
                            if u == 7:
                                rec_decays(h + 1)
                    ch.leave(H - 1)
                g0 = l * LAYER_HALVES + IN_HALVES
                for u in range(-1, 7):
                    if u == -1:
                        act.wait_ge(half_done, g0)
                        act.wait_ge(o_ready, l * H + H - 1)
                    else:
                        (att_act if l == 0 else rec_act)(H - 1, u)
                    act_split(LAST_SPLIT[l][u])
                    if u == 1:
                        hi(g0 + 3, 3)
                    if u == 4 - l:
                        hi(g0 + 4, 0)
                    if u == 6 - l:
                        hi(g0 + 5, 1)
                if l == 1:
                    rec_norm(H - 1)
                act.wait_ge(o_ready, (l + 1) * H)
                act_split([KT - 1])

                def out_pair(l, i, first=False, last=False):
                    for u in range(4):
                        if not ((first and u < 3) or (last and l == 1 and u + AHEAD >= 4)):
                            hi(i * 4 + (l * LAYER_HALVES + IN_HALVES + u + AHEAD), (u + AHEAD) % RING)
                        if l == 0 and u >= 2:
                            out_tile(i, u - 2, last)
                        if l == 1 and u < 2 and not first:
                            put_y(i - 1, u)

                def out_tile(i, par, last):
                    n = i * 2 + par
                    if last and par:
                        act.wait_ge(half_done, LAYER_HALVES)
                        act.wait_ge(full_ready, 2)
                        act_split(range(0, 2))
                    act.wait_ge(evacuated, added(l, n))
                    func(full[:, bass.ds(n, 1), :].rearrange("p a t -> p (a t)"), x_new[par], ACT.Copy,
                         scale=NORM[1][:, bass.ds(n, 1)]).then_inc(full_ready, 1)
                    act.wait_ge(x_summed, n + KT)
                    func(x_sq, x_new[par], ACT.Square).then_inc(x_squared, 1)
                    act.dma_start(x_residual[bass.ds(n, 1)].rearrange("a p t -> (a p) t"), x_new[par]
                                  ).then_inc(x_stored[par], 16)

                def put_y(i, par):
                    n = i * 2 + par
                    act.wait_ge(y_turned, n + 1)
                    if not (isinstance(i, int) and i == 0):
                        act.wait_ge(y_stored[par], i * 32)
                    ch.done(func(y_nat[par][:, 0:NB, :], M[0].rearrange("p (b d) -> p b d", b=NB), ACT.Copy))
                    func(y_nat[par][:, 4, :], M[1][:, 0:P], ACT.Copy).then_inc(y_copied, 1)
                    ch.wait()
                    act.wait_ge(y_copied, n + 1)
                    act.dma_start(y_prompt_v[:, :, bass.ds(n * P, P)], y_nat[par][:, 0:NB, :]).then_inc(y_stored[par], 16)
                    act.dma_start(y_sample[0][:, bass.ds(n * P, P)], y_nat[par][SROW:P, 4, :]).then_inc(y_stored[par], 16)

                out_pair(l, 0, first=True)
                first_looped = 1 if l == 0 else 2
                if l == 1:
                    out_pair(l, 1)
                with act.Fori(first_looped, KT // 2 - 1) as i:
                    ch.enter(i - first_looped, 0 if l == 0 else 2)
                    out_pair(l, i)
                    ch.leave(KT // 2 - 1 - first_looped)
                out_pair(l, KT // 2 - 1, last=True)
                if l == 1:
                    put_y(KT // 2 - 1, 0)
                    put_y(KT // 2 - 1, 1)

        @block.vector
        def _(dve):
            ch = Chain(dve, dve_chain)

            def lo(g, slot):
                dve.wait_ge(hi_ready, g + 1)
                dve.tensor_tensor(w_lo[:, slot], w_raw[:, slot], w_hi[:, slot].bitcast(F32), ALU.subtract
                                  ).then_inc(lo_ready, 1)

            def split_ahead(l, h, u):
                lo(h * HEAD_HALVES + (l * LAYER_HALVES + u + AHEAD), (u + AHEAD) % RING)

            def act_split(base, ks):
                for k in ks:
                    dve.wait_ge(act_hi_ready, base + k + 1)
                    dve.tensor_tensor(act_lo[:, k, :], full[:, k, :], act_hi[:, k, :].bitcast(F32), ALU.subtract
                                      ).then_inc(act_lo_ready, 1)

            def evacuate(l, h, j):
                dve.wait_ge(half_done, h * HEAD_HALVES + (l * LAYER_HALVES + 2 * j + 2))
                if l == 0 and j < 2 and not (isinstance(h, int) and h == 0):
                    dve.wait_ge(qk_normed, h)
                dve.tensor_tensor(Y[:, j, :].rearrange("p (a t) -> p a t", a=2), acc[j % 2],
                                  rstd_x[:].rearrange("p (a t) -> p a t", a=2), ALU.mult).then_inc(evacuated, 1)

            def att_dve(h, u):
                if u == 0:
                    dve.wait_ge(stage_a, h + 1)
                    if not (isinstance(h, int) and h == 0):
                        dve.wait_ge(v_stored, h * 32)
                    ch.done(dve.tensor_copy(v_nat[:, 0:NB, :], M[3].rearrange("p (b d) -> p b d", b=NB)))
                    dve.wait_ge(past_copied, h + 1)
                    dve.tensor_copy(v_nat[:, 4, :], M[2][:, 64:192]).then_inc(v_copied, 1)
                    dve.wait_ge(qk_rstd, h + 1)
                    dve.wait_ge(first_scaled, 1)
                    ch.done(dve.scalar_tensor_tensor(out=qn, in0=Y[:, 0, :], scalar=WQS, in1=qk_sq[:, 0, :],
                                                     op0=ALU.mult, op1=ALU.mult))
                    dve.scalar_tensor_tensor(out=kn, in0=Y[:, 1, :], scalar=WK, in1=qk_sq[:, 1, :],
                                             op0=ALU.mult, op1=ALU.mult).then_inc(qk_normed, 1)
                elif u == 1:
                    dve.wait_ge(qkn_hi_ready, h + 1)
                    dve.wait_ge(qk_normed, h + 1)
                    dve.tensor_tensor(qk_lo, qkn, qk_hi.bitcast(F32), ALU.subtract).then_inc(qkn_lo_ready, 1)
                    dve.wait_ge(gate_log, h + 1)
                    dve.scalar_tensor_tensor(out=g_tmp, in0=Y[:, 3, :], scalar=0.0, in1=g_tmp,
                                             op0=ALU.min, op1=ALU.subtract).then_inc(gate_ls, 1)
                elif u == 2:
                    dve.wait_ge(gate_sig, h + 1)
                    dve.tensor_tensor(gate, Y[:, 3, :], g_tmp, ALU.mult).then_inc(gate_ready, 1)
                    dve.wait_ge(v_hi_ready, h + 1)
                    dve.wait_ge(v_copied, h + 1)
                    dve.tensor_tensor(v_lo, v_nat[:, 0:3, :], v_hi.bitcast(F32), ALU.subtract).then_inc(v_lo_ready, 1)
                elif u == 3:
                    dve.wait_ge(soft_log, h + 1)
                    for k, (at, src) in enumerate(((0, M[0]), (512, M[1][:, 0:384]), (896, M[2][:, 0:480]))):
                        n = src.shape[-1]
                        ins = dve.scalar_tensor_tensor(out=za[:, at:at + n], in0=src, scalar=0.0,
                                                       in1=za[:, at:at + n], op0=ALU.max, op1=ALU.add)
                        ins.then_inc(soft, 1) if k == 2 else ch.done(ins)
                elif u == 4:
                    dve.wait_ge(sp_hi_ready, h + 1)
                    dve.tensor_tensor(sp_lo, za, sp_hi.bitcast(F32), ALU.subtract).then_inc(sp_lo_ready, 1)
                elif u == 6:
                    dve.wait_ge(att_ready, h + 1)
                    dve.wait_ge(att_hi_ready, h + 1)
                    dve.tensor_tensor(sp_lo, za, sp_hi.bitcast(F32), ALU.subtract).then_inc(att_lo_ready, 1)
                elif u == 7:
                    dve.wait_ge(stage_d, h + 1)
                    dve.wait_ge(gate_ready, h + 1)
                    ch.done(dve.tensor_tensor(full[:, bass.ds(h, 1), 0:SEQ].rearrange("p a t -> p (a t)"), M[3],
                                              gate[:, 0:SEQ], ALU.mult))
                    dve.tensor_tensor(full[:, bass.ds(h, 1), SEQ:T].rearrange("p a t -> p (a t)"),
                                      M[1][:, 384:384 + SAMPLE], gate[:, SEQ:T], ALU.mult).then_inc(o_ready, 1)

            def att_next(h, u):
                if u == 7:
                    dve.wait_ge(qk_squared, h + 1)
                    dve.wait_ge(sq_hi_ready, h + 1)
                    dve.tensor_tensor(qk_lo, qk_sq, qk_hi.bitcast(F32), ALU.subtract).then_inc(sq_lo_ready, 1)

            def rec_log_sigmoids(h):
                dve.wait_ge(r_log, h + 1)
                dve.scalar_tensor_tensor(out=r_tmp, in0=Y[:, 0:2, :], scalar=0.0, in1=r_tmp,
                                         op0=ALU.min, op1=ALU.subtract).then_inc(r_ls, 1)
                dve.wait_ge(r_ls, h + 1)
                dve.tensor_tensor(kk, r_tmp[:, 1], Y[:, 1, :], ALU.subtract).then_inc(r_kx, 1)

            def rec_next(h, u):
                if u == 6:
                    dve.wait_ge(r_lse, h + 1)
                    ch.done(dve.tensor_scalar(cum, r_tmp[:, 1], LOG_BA[:, bass.ds(h, 1)], 0.0, ALU.add, ALU.max))
                    ch.wait()
                    ch.done(dve.tensor_tensor(cum, cum, lse, ALU.add))
                    ch.wait()
                    ch.done(dve.tensor_scalar(lse, cum, LOG_A[:, bass.ds(h, 1)], 0.0, ALU.add, ALU.min))
                    dve.wait_ge(r_sig, h + 1)
                    ch.done(dve.tensor_tensor(qs, Y[:, 0, :], r_tmp[:, 0], ALU.mult))
                    ch.wait()
                    dve.tensor_tensor_scan(cum, run_on[:], lse, 0.0, ALU.mult, ALU.add).then_inc(r_cum, 1)
                elif u == 7:
                    dve.wait_ge(r_kexp, h + 1)
                    dve.tensor_scalar(kk, kk, ONE_LB[:, bass.ds(h, 1)], None, ALU.mult).then_inc(r_qk, 1)

            def level(h, i, part):
                m = LEVELS[i]
                n = T if m <= SAMPLE // 2 else SEQ

                def cut(v):
                    v = v[:, 0:n].rearrange("p (b j) -> p b j", j=2 * m)
                    return v[:, :, 0:m], v[:, :, m:2 * m]
                d1, d2 = cut(dl[i % 2])
                c1, c2 = cut(cum)
                x1, x2 = cut(xl[i % 2])
                r = cum[:, 0:n].rearrange("p (b j) -> p b j", j=2 * m)[:, :, m - 1:m].broadcast_to([P, n // (2 * m), m])
                if part == 0:
                    if i >= 2:
                        dve.wait_ge(r_x, h * NL + (i - 1))
                    ch.done(dve.tensor_tensor(d1, r, c1, ALU.subtract))
                    dve.tensor_tensor(d2, c2, r, ALU.subtract).then_inc(r_diff, 1)
                else:
                    dve.wait_ge(r_dexp, h * NL + (i + 1))
                    if i >= 2:
                        dve.wait_ge(r_lev, h * NL + (i - 1))
                    ch.done(dve.tensor_tensor(x1, cut(kk)[0], d1, ALU.mult))
                    dve.tensor_tensor(x2, cut(qs)[1], d2, ALU.mult).then_inc(r_x, 1)

            def put(h, i, bank):
                m = LEVELS[i]
                dve.wait_ge(consts_ready, 1)
                if i:
                    dve.wait_ge(r_put, h * NL + i)
                dve.wait_ge(r_lev, h * NL + (i + 1))
                msk = level_mask[:, MASK_COL[m]:MASK_COL[m] + 64].bitcast(I32).rearrange("p (b j) -> p b j", j=m)
                for b in range(NB):
                    dst = A[:, b * P:(b + 1) * P].rearrange("p (b j) -> p b j", j=2 * m)[:, :, m:2 * m]
                    src = M[bank][:, b * 64:(b + 1) * 64].rearrange("p (b j) -> p b j", j=m)
                    ins = dve.copy_predicated(dst, msk, src)
                    if b < NB - 1 or m <= SAMPLE // 2:
                        ch.done(ins)
                if m <= SAMPLE // 2:
                    dst = A[:, SEQ:T].rearrange("p (b j) -> p b j", j=2 * m)[:, :, m:2 * m]
                    src = M[bank][:, 256:256 + SAMPLE // 2].rearrange("p (b j) -> p b j", j=m)
                    nb = SAMPLE // 2 // m
                    ins = dve.copy_predicated(dst, msk[:, 64 // m - nb:64 // m, :], src)
                ins.then_inc(r_put, 1)

            def rec_distances(h):
                dve.wait_ge(r_cum, h + 1)
                level(h, 0, 0)
                for b in range(5):
                    n = P if b < NB else SAMPLE
                    v = cum[:, b * P:b * P + n]
                    ins = dve.tensor_tensor(kd[:, b * P:b * P + n], v[:, n - 1:n].broadcast_to([P, n]), v, ALU.subtract)
                    ins.then_inc(r_kdx, 1) if b == NB else ch.done(ins)
                level(h, 1, 0)
                dve.wait_ge(r_qk, h + 1)
                if not (isinstance(h, int) and h == 0):
                    dve.wait_ge(o_ready, h + H)
                level(h, 0, 1)
                dve.wait_ge(r_kde, h + 1)
                dve.tensor_tensor(kd, kd, kk, ALU.mult).then_inc(r_kd, 1)
                level(h, 1, 1)

            def rec_dve(h, u):
                if u == 0:
                    dve.tensor_tensor(own, qs, kk, ALU.mult).then_inc(r_own_prod, 1)
                    dve.wait_ge(r_eb, h + 1)
                    ch.done(dve.tensor_tensor(qe, qs, eb, ALU.mult))
                elif u == 1:
                    level(h, 2, 0)
                    dve.wait_ge(r_glog, h + 1)
                    dve.scalar_tensor_tensor(out=g_tmp_r, in0=Y[:, 3, :], scalar=0.0, in1=g_tmp_r,
                                             op0=ALU.min, op1=ALU.subtract).then_inc(r_gls, 1)
                    put(h, 0, 1)
                    level(h, 2, 1)
                    level(h, 3, 0)
                elif u == 2:
                    put(h, 1, 0)
                    level(h, 3, 1)
                    dve.wait_ge(r_own_hi, h + 1)
                    dve.wait_ge(r_own_prod, h + 1)
                    dve.tensor_tensor(own_lo, own, own_hi.bitcast(F32), ALU.subtract).then_inc(r_own_lo, 1)
                    level(h, 4, 0)
                elif u == 3:
                    dve.wait_ge(r_own, h + 1)
                    dve.wait_ge(r_own_hi, h + 1)
                    dve.wait_ge(r_own_lo, h + 1)
                    ch.done(dve.tensor_tensor(own[:, 0:SEQ], M[0], Y[:, 2, 0:SEQ], ALU.mult))
                    dve.tensor_tensor(own[:, SEQ:T], M[2][:, P:P + SAMPLE], Y[:, 2, SEQ:T], ALU.mult
                                      ).then_inc(r_own_v, 1)
                    put(h, 2, 1)
                    level(h, 4, 1)
                    level(h, 5, 0)
                    dve.wait_ge(r_upd, h + 1)
                    if not (isinstance(h, int) and h == 0):
                        dve.wait_ge(s_stored, h * 32)
                    dve.wait_ge(s_loaded, h * 16 + 16)
                    ch.done(dve.tensor_copy(S[:, 1, :], M[3][:, 0:P]))
                    ch.done(dve.scalar_tensor_tensor(out=S[:, 5, :], in0=S[:, 0, :], scalar=eb[:, T - 1:T],
                                                     in1=M[2][:, 0:P], op0=ALU.mult, op1=ALU.add))
                    for b in range(1, NB):
                        ch.wait()
                        ins = dve.scalar_tensor_tensor(out=S[:, b + 1, :], in0=S[:, b, :],
                                                       scalar=eb[:, (b + 1) * P - 1:(b + 1) * P],
                                                       in1=M[3][:, b * P:(b + 1) * P], op0=ALU.mult, op1=ALU.add)
                        ins.then_inc(r_state, 1) if b == NB - 1 else ch.done(ins)
                elif u == 4:
                    put(h, 3, 0)
                    level(h, 5, 1)
                    level(h, 6, 0)
                    put(h, 4, 1)
                    level(h, 6, 1)
                    dve.wait_ge(r_x, h * NL + NL)
                    dve.tensor_tensor(pair, xl[0][:, 0:T:2], xl[0][:, 1:T:2], ALU.mult).then_inc(r_pair_prod, 1)
                    dve.wait_ge(r_gsig, h + 1)
                    dve.tensor_tensor(gate_r, Y[:, 3, :], g_tmp_r, ALU.mult).then_inc(r_gate, 1)
                elif u == 5:
                    put(h, 5, 0)
                    dve.wait_ge(r_pair_hi, h + 1)
                    dve.tensor_tensor(pair_lo, pair, pair_hi.bitcast(F32), ALU.subtract).then_inc(r_pair_lo, 1)
                elif u == 6:
                    dve.wait_ge(r_osq, h + 1)
                    dve.wait_ge(r_ohi, h + 1)
                    dve.tensor_tensor(o_lo, o_sq, o_hi.bitcast(F32), ALU.subtract).then_inc(r_olo, 1)

            def rec_output(h):
                dve.wait_ge(r_lev, h * NL + NL)
                dve.wait_ge(r_own_v, h + 1)
                dve.wait_ge(r_pair_lo, h + 1)
                dve.wait_ge(r_put, h * NL + (NL - 1))
                dve.tensor_tensor(pair, M[1][:, 0:HT], Y[:, 2, 0:T:2], ALU.mult).then_inc(r_put, 1)
                dve.wait_ge(r_put, h * NL + NL)
                ch.done(dve.tensor_tensor(own[:, 1:T:2], own[:, 1:T:2], pair, ALU.add))
                ch.wait()
                ch.done(dve.tensor_tensor(o_cp[:, 0:SEQ], M[3], own[:, 0:SEQ], ALU.add))
                dve.tensor_tensor(o_cp[:, SEQ:T], M[2][:, 0:SAMPLE], own[:, SEQ:T], ALU.add).then_inc(r_osum, 1)

            def rec_gate(h):
                dve.wait_ge(r_orstd, h + 1)
                dve.wait_ge(r_gate, h + 1)
                ch.done(dve.scalar_tensor_tensor(out=o_cp, in0=o_cp, scalar=WO, in1=o_sq, op0=ALU.mult, op1=ALU.mult))
                ch.wait()
                dve.tensor_tensor(full[:, bass.ds(h, 1), :].rearrange("p a t -> p (a t)"), o_cp, gate_r, ALU.mult
                                  ).then_inc(o_ready, 1)

            dve.wait_ge(vecs_turned, 1)
            ch.done(dve.tensor_copy(vecs[:], M[0][:, 0:51]))
            ch.wait()
            ch.done(dve.tensor_scalar(WQS, WQ, float(P) ** -0.5, None, ALU.mult))
            dve.tensor_tensor(LB_T, LB_RAW, LB_RAW, ALU.subtract).then_inc(vecs_ready, 1)
            for k in range(KT + 1):
                if k < KT:
                    dve.wait_ge(x_turned, k + 1)
                    if k >= XB:
                        dve.wait_ge(x_in_stored[k % XB], 16 * (k // XB))
                        dve.wait_ge(x_scaled, k - XB + 1)
                        dve.wait_ge(x_squared, k - XB + 1)
                    dve.tensor_copy(x_in[k % XB][:, SEQ:T], psum[:, 7 - 2 * (k % 2), 0:SAMPLE]).then_inc(x_s_copied, 1)
                    if k >= 2:
                        dve.wait_ge(act_lo_ready, k - 1)
                    dve.wait_ge(x_s_copied, k + 1)
                    dve.wait_ge(x_copied, k + 1)
                    dve.tensor_scalar(x_tmp[k % 2], x_in[k % XB], NORM[0][:, k:k + 1], None, ALU.mult
                                      ).then_inc(x_scaled, 1)
                if k:
                    dve.wait_ge(act_hi_ready, k)
                    dve.wait_ge(x_scaled, k)
                    dve.tensor_tensor(act_lo[:, k - 1, :], x_tmp[(k - 1) % 2], act_hi[:, k - 1, :].bitcast(F32),
                                      ALU.subtract).then_inc(act_lo_ready, 1)
                if k in START_SPLITS:
                    g = START_SPLITS.index(k)
                    lo(g, g % RING)
            for j in range(2):
                dve.wait_ge(half_done, 3 + j)
                dve.tensor_copy(Y[:, j, :].rearrange("p (a t) -> p a t", a=2), acc[j]).then_inc(evacuated, 1)
            lo(6, 2)
            dve.wait_ge(act_chain, 1)
            ch.done(dve.reciprocal(LB_R, LB_E))
            ch.wait()
            ch.done(dve.tensor_tensor(LB_T, LB_E, LB_R, ALU.mult))
            ch.wait()
            ch.done(dve.tensor_tensor(LB, LB_T, LB_T, ALU.subtract))
            ch.wait()
            ch.done(dve.tensor_scalar(LB, LB, 0.0, LB_TOP, ALU.max, ALU.min))
            ch.wait()
            ch.done(dve.tensor_scalar(ONE_LB, LB, -1.0, 1.0, ALU.mult, ALU.add))
            ch.wait()
            dve.tensor_scalar(LB_R, LB, LB_FLOOR, TWO60, ALU.max, ALU.mult).then_inc(vecs_ready, 1)
            dve.wait_ge(act_chain, 3)
            ch.done(dve.tensor_scalar(LOG_A, LOG_A, -LN_TWO60, None, ALU.add))
            ch.wait()
            ch.done(dve.tensor_tensor(LOG_BA, LOG_BA, LOG_A, ALU.subtract))

            for l in range(2):
                if l == 1:
                    act_split(2 * KT, range(KT))
                    ch.done(dve.memset(A, 0.0))
                    ch.wait()
                if l == 0:
                    dve.wait_ge(rstd_ready, 1)
                    dve.wait_ge(evacuated, 2)
                    dve.tensor_tensor(Y[:, 0:2, :], Y[:, 0:2, :], rstd_x[:].unsqueeze(1).broadcast_to([P, 2, T]),
                                      ALU.mult).then_inc(first_scaled, 1)
                for u in range(0 if l else 4, HEAD_HALVES):
                    split_ahead(l, 0, u)
                    if u == 2:
                        dve.wait_ge(rstd_ready, 2)
                    if u == 6 or (l == 1 and u in (2, 4)):
                        evacuate(l, 0, u // 2 - 1)
                    if l == 1 and u == 5:
                        rec_log_sigmoids(0)
                    (att_next if l == 0 else rec_next)(0, u)
                if l == 1:
                    rec_distances(0)
                with dve.Fori(0, H - 1) as h:
                    ch.enter(h, 5 if l == 0 else 53)
                    for u in range(HEAD_HALVES):
                        split_ahead(l, h + 1, u)
                        if l == 1 and u == 6:
                            rec_output(h)
                        if u == 0:
                            evacuate(l, h, 3)
                        elif u % 2 == 0:
                            evacuate(l, h + 1, u // 2 - 1)
                        if l == 0:
                            att_dve(h, u)
                            att_next(h + 1, u)
                        else:
                            rec_dve(h, u)
                            if u == 5:
                                rec_log_sigmoids(h + 1)
                            rec_next(h + 1, u)
                            if u == 7:
                                rec_gate(h)
                                rec_distances(h + 1)
                    ch.leave(H - 1)
                evacuate(l, H - 1, 3)
                g0 = l * LAYER_HALVES + IN_HALVES
                for u in range(-1, 8):
                    if l == 1 and u == 6:
                        rec_output(H - 1)
                    if u >= 0:
                        (att_dve if l == 0 else rec_dve)(H - 1, u)
                    if u == l - 1:
                        act_split((2 * l + 1) * KT, range(DVE_SPLITS))
                    if u == 1:
                        lo(g0 + 3, 3)
                    if u == 4 - l:
                        lo(g0 + 4, 0)
                    if u == 6 - l:
                        lo(g0 + 5, 1)
                if l == 1:
                    rec_gate(H - 1)
                dve.wait_ge(act_lo_ready, (2 * l + 2) * KT - 1)
                act_split((2 * l + 1) * KT, [KT - 1])

                def out_pair(l, i, first=False, last=False):
                    for par in range(2):
                        for u in ((0, 1, 2), (3,))[par]:
                            if (first and u < 3) or (last and l == 1 and u + AHEAD >= 4):
                                continue
                            lo(i * 4 + (l * LAYER_HALVES + IN_HALVES + u + AHEAD), (u + AHEAD) % RING)
                        dve.wait_ge(half_done, i * 4 + (l * LAYER_HALVES + IN_HALVES + par + 3))
                        dve.wait_ge(x_old_loaded[par], i * 16 + (16 * (KT // 2) * l + 16))
                        if not (isinstance(i, int) and i == 0):
                            if l == 0:
                                dve.wait_ge(x_stored[par], i * 16)
                                dve.wait_ge(x_squared, i * 2 + (KT + par - 1))
                                dve.wait_ge(full_ready, i * 2 + (par - 1))
                            else:
                                dve.wait_ge(y_turned, i * 2 + (par - 1))
                        dve.tensor_tensor(x_new[par].rearrange("p (a t) -> p a t", a=2), acc[par],
                                          x_old[par].rearrange("p (a t) -> p a t", a=2), ALU.add).then_inc(evacuated, 1)

                out_pair(l, 0, first=True)
                with dve.Fori(1, KT // 2 - 1) as i:
                    out_pair(l, i)
                out_pair(l, KT // 2 - 1, last=True)


_INS = ["x_prompt", "x_sample", "cache_k", "cache_v", "state_hgrn", "norm_w", "w_in", "w_out", "q_norm_w",
        "k_norm_w", "hgrn_norm_w", "hgrn_lb"]
_OUTS = [(1, SEQ, D), (1, SAMPLE, D), (1, 1, SEQ, H, P), (1, 1, SEQ, H, P), (1, 1, H, P, P),
         (1, 1, SAMPLE, H, P), (1, 1, SAMPLE, H, P), (1, 1, H, P, P)]


def kernel(**inputs):
    import numpy as _np
    import concourse.bacc as _bacc
    from concourse.bass_utils import run_bass_kernel_spmd as _run

    nc = _bacc.Bacc("TRN2", target_bir_lowering=False, num_devices=1)
    arrays, args = {}, []
    for name in _INS:
        a = _np.ascontiguousarray(inputs[name])
        arrays[f"in_{name}"] = a
        args.append(nc.dram_tensor(f"in_{name}", a.shape, F32, kind="ExternalInput").ap())
    for i, shape in enumerate(_OUTS):
        args.append(nc.dram_tensor(f"out_{i}", shape, F32, kind="ExternalOutput").ap())
    encoder_step(nc, *args)
    r = _run(nc, [arrays], core_ids=[0])
    return tuple(r.results[0][f"out_{i}"] for i in range(len(_OUTS)))
```
